# Optimizing a Trainium2 kernel written in Bass

```python
import math
import jax, jax.numpy as jnp
from jax import lax
import numpy as np

D_MODEL = 1024
BATCH = 1
SEQ = 512
DEPTH = 2

CHUNK = 64
N_A = DEPTH - DEPTH // 2
N_B = DEPTH // 2
EPS = 1e-6
DN_HEADS = 8
DN_HEAD_DIM = 128
DN_W = DN_HEADS * DN_HEAD_DIM
DN_CONV = 4
SW_Q_HEADS = 16
SW_KV_HEADS = 2
SW_HEAD_DIM = 64
SW_W = SW_Q_HEADS * SW_HEAD_DIM
SW_KV_W = SW_KV_HEADS * SW_HEAD_DIM
WINDOW = 128
WINDOW_CHUNKS = WINDOW // CHUNK
MEM_LEN = 256
MEM_HEADS = 4
MEM_HEAD_DIM = 128
MEM_W = MEM_HEADS * MEM_HEAD_DIM
D_FF = -(-8 * D_MODEL // (3 * 256)) * 256
A_IN = 4 * DN_W + 2 * DN_HEADS + MEM_W
A_OUT = DN_W + MEM_W
B_IN = SW_W + MEM_W
B_OUT = SW_W + MEM_W

kernel_name = 'yoco_gated_deltanet_swa_sink_alibi_memory'

def rms_norm(x, g):
    xf = x.astype(jnp.float32)
    y = xf * lax.rsqrt(jnp.mean(xf * xf, axis=-1, keepdims=True) + EPS)
    return (y * g.astype(jnp.float32)).astype(x.dtype)

def l2_norm(x):
    xf = x.astype(jnp.float32)
    return xf * lax.rsqrt(jnp.sum(xf * xf, axis=-1, keepdims=True) + EPS)

def alibi_slopes(n):
    return jnp.exp2(-8.0 * jnp.arange(1, n + 1, dtype=jnp.float32) / n)

def causal_depthwise_conv(x, w):
    k = w.shape[0]
    return lax.conv_general_dilated(
        x, w[:, None, :].astype(x.dtype), window_strides=(1,), padding=[(k - 1, 0)],
        dimension_numbers=('NWC', 'WIO', 'NWC'), feature_group_count=x.shape[-1])

def gated_delta_rule(q, k, v, g, beta):
    f32 = jnp.float32
    B, S, H, Dk = q.shape
    Dv = v.shape[-1]
    N = S // CHUNK

    def to_chunks(t):
        return t.astype(f32).reshape(B, N, CHUNK, H, -1).transpose(0, 3, 1, 2, 4)

    q, k, v = to_chunks(q), to_chunks(k), to_chunks(v)
    g = g.astype(f32).reshape(B, N, CHUNK, H).transpose(0, 3, 1, 2)
    beta = beta.astype(f32).reshape(B, N, CHUNK, H).transpose(0, 3, 1, 2)
    g = jnp.cumsum(g, axis=-1)
    idx = jnp.arange(CHUNK)
    tril = idx[:, None] >= idx[None, :]
    strict = idx[:, None] > idx[None, :]
    decay = jnp.exp(jnp.where(tril, g[..., :, None] - g[..., None, :], -jnp.inf))
    k_beta = k * beta[..., None]
    v_beta = v * beta[..., None]
    m = jnp.where(strict, jnp.einsum('bhncd,bhnsd->bhncs', k_beta, k) * decay, 0.0)
    eye = jnp.eye(CHUNK, dtype=f32)
    t_inv = lax.linalg.triangular_solve(eye + m, jnp.broadcast_to(eye, m.shape), left_side=True,
                                        lower=True, unit_diagonal=True)
    u = t_inv @ v_beta
    w = t_inv @ (k_beta * jnp.exp(g)[..., None])
    attn_intra = jnp.where(tril, jnp.einsum('bhncd,bhnsd->bhncs', q, k) * decay, 0.0)
    q_dec = q * jnp.exp(g)[..., None]
    k_dec = k * jnp.exp(g[..., -1:] - g)[..., None]
    g_last = jnp.exp(g[..., -1])

    def step(state, inp):
        qd, kd, u_c, w_c, a_c, gl = inp
        v_new = u_c - jnp.einsum('bhcd,bhde->bhce', w_c, state)
        o = jnp.einsum('bhcd,bhde->bhce', qd, state) + jnp.einsum('bhcs,bhse->bhce', a_c, v_new)
        state = state * gl[..., None, None] + jnp.einsum('bhcd,bhce->bhde', kd, v_new)
        return state, o

    xs = tuple(jnp.moveaxis(t, 2, 0) for t in (q_dec, k_dec, u, w, attn_intra, g_last))
    _, o = lax.scan(step, jnp.zeros((B, H, Dk, Dv), f32), xs)
    return o.transpose(1, 0, 3, 2, 4).reshape(B, S, H, Dv)

def memory_attention(mq, mem_n, w_mem_kv, q_norm, k_norm):
    B, S, _ = mq.shape
    M = mem_n.shape[1]
    kv = mem_n @ w_mem_kv
    mk, mv = jnp.split(kv, 2, axis=-1)
    q = rms_norm(mq.reshape(B, S, MEM_HEADS, MEM_HEAD_DIM), q_norm)
    k = rms_norm(mk.reshape(B, M, MEM_HEADS, MEM_HEAD_DIM), k_norm)
    v = mv.reshape(B, M, MEM_HEADS, MEM_HEAD_DIM)
    s = jnp.einsum('bshd,bmhd->bhsm', q, k).astype(jnp.float32) * (MEM_HEAD_DIM ** -0.5)
    p = jax.nn.softmax(s, axis=-1).astype(v.dtype)
    o = jnp.einsum('bhsm,bmhd->bshd', p, v)
    return o.reshape(B, S, MEM_W)

def sliding_window_attention(q, k, v, sinks):
    f32 = jnp.float32
    B, S, Hq, Dh = q.shape
    Hkv = k.shape[2]
    G = Hq // Hkv
    N = S // CHUNK
    W = WINDOW_CHUNKS
    L = W * CHUNK
    qb = q.reshape(B, N, CHUNK, Hkv, G, Dh)
    pad = [(0, 0), ((W - 1) * CHUNK, 0), (0, 0), (0, 0)]
    kc = jnp.pad(k, pad).reshape(B, N + W - 1, CHUNK, Hkv, Dh)
    vc = jnp.pad(v, pad).reshape(B, N + W - 1, CHUNK, Hkv, Dh)
    kb = jnp.concatenate([kc[:, j:j + N] for j in range(W)], axis=2)
    vb = jnp.concatenate([vc[:, j:j + N] for j in range(W)], axis=2)
    qi = jnp.arange(CHUNK)
    kl = jnp.arange(L)
    dist = jnp.abs(qi[:, None] + (W - 1) * CHUNK - kl[None, :]).astype(f32)
    valid = (jnp.arange(N)[:, None] - (W - 1) + kl[None, :] // CHUNK) >= 0
    slopes = alibi_slopes(Hq).reshape(Hkv, G)
    s = jnp.einsum('bnqkgd,bnlkd->bnkgql', qb, kb).astype(f32) * (Dh ** -0.5)
    s = s - slopes[:, :, None, None] * dist
    s = jnp.where(valid[None, :, None, None, None, :], s, -jnp.inf)
    sink = sinks.astype(f32).reshape(Hkv, G)[None, None, :, :, None, None]
    mx = jnp.maximum(jnp.max(s, axis=-1, keepdims=True), sink)
    p = jnp.exp(s - mx)
    p = p / (jnp.sum(p, axis=-1, keepdims=True) + jnp.exp(sink - mx))
    o = jnp.einsum('bnkgql,bnlkd->bnqkgd', p.astype(vb.dtype), vb)
    return o.reshape(B, S, Hq * Dh)

def swiglu(h, w_gate_up, w_down):
    gate, up = jnp.split(h @ w_gate_up, 2, axis=-1)
    return (jax.nn.silu(gate) * up) @ w_down

def mixer_a(x, mem_n, norm, w_in, conv_w, a_log, dt_bias, out_norm, w_out,
            w_mem_kv, mq_norm, mk_norm):
    B, S, _ = x.shape
    h = rms_norm(x, norm)
    proj = h @ w_in
    qkv, z, b, a, mq = jnp.split(
        proj, [3 * DN_W, 4 * DN_W, 4 * DN_W + DN_HEADS, 4 * DN_W + 2 * DN_HEADS], axis=-1)
    qkv = jax.nn.silu(causal_depthwise_conv(qkv, conv_w))
    q, k, v = jnp.split(qkv, 3, axis=-1)
    q = l2_norm(q.reshape(B, S, DN_HEADS, DN_HEAD_DIM)) * (DN_HEAD_DIM ** -0.5)
    k = l2_norm(k.reshape(B, S, DN_HEADS, DN_HEAD_DIM))
    v = v.reshape(B, S, DN_HEADS, DN_HEAD_DIM)
    beta = jax.nn.sigmoid(b.astype(jnp.float32))
    g = -jnp.exp(a_log.astype(jnp.float32)) * jax.nn.softplus(
        a.astype(jnp.float32) + dt_bias.astype(jnp.float32))
    o = gated_delta_rule(q, k, v, g, beta)
    o = rms_norm(o, out_norm) * jax.nn.silu(z.reshape(B, S, DN_HEADS, DN_HEAD_DIM).astype(jnp.float32))
    o = o.reshape(B, S, DN_W).astype(x.dtype)
    m = memory_attention(mq, mem_n, w_mem_kv, mq_norm, mk_norm)
    return jnp.concatenate([o, m], axis=-1) @ w_out

def mixer_b(x, shared_k, shared_v, mem_n, norm, w_in, q_norm, sinks, w_out,
            w_mem_kv, mq_norm, mk_norm):
    B, S, _ = x.shape
    h = rms_norm(x, norm)
    q, mq = jnp.split(h @ w_in, [SW_W], axis=-1)
    q = rms_norm(q.reshape(B, S, SW_Q_HEADS, SW_HEAD_DIM), q_norm)
    o = sliding_window_attention(q, shared_k, shared_v, sinks)
    m = memory_attention(mq, mem_n, w_mem_kv, mq_norm, mk_norm)
    return jnp.concatenate([o, m], axis=-1) @ w_out

def shared_kv(x, kv_norm, w_kv, k_norm):
    B, S, _ = x.shape
    k, v = jnp.split(rms_norm(x, kv_norm) @ w_kv, 2, axis=-1)
    k = rms_norm(k.reshape(B, S, SW_KV_HEADS, SW_HEAD_DIM), k_norm)
    v = v.reshape(B, S, SW_KV_HEADS, SW_HEAD_DIM)
    return k, v

def setup_inputs(seed: int = 0) -> dict:
    key = jax.random.key(seed)
    ks = iter(jax.random.split(key, 32))
    f32 = jnp.float32

    def nrm(shape, scale):
        return jax.random.normal(next(ks), shape, f32) * scale

    def gain(shape):
        return 1.0 + 0.02 * jax.random.normal(next(ks), shape, f32)

    x = nrm((BATCH, SEQ, D_MODEL), 1.0)
    mem = nrm((BATCH, MEM_LEN, D_MODEL), 1.0)
    a_norm = gain((N_A, D_MODEL))
    a_w_in = nrm((N_A, D_MODEL, A_IN), D_MODEL ** -0.5)
    a_conv = nrm((N_A, DN_CONV, 3 * DN_W), DN_CONV ** -0.5)
    a_A_log = jnp.log(jax.random.uniform(next(ks), (N_A, DN_HEADS), f32, 1.0, 16.0))
    dt = jnp.exp(jax.random.uniform(next(ks), (N_A, DN_HEADS), f32,
                                    math.log(1e-3), math.log(1e-1)))
    a_dt_bias = dt + jnp.log(-jnp.expm1(-dt))
    a_out_norm = gain((N_A, DN_HEAD_DIM))
    a_w_out = nrm((N_A, A_OUT, D_MODEL), A_OUT ** -0.5)
    kv_norm = gain((D_MODEL,))
    w_kv = nrm((D_MODEL, 2 * SW_KV_W), D_MODEL ** -0.5)
    k_norm = gain((SW_HEAD_DIM,))
    b_norm = gain((N_B, D_MODEL))
    b_w_in = nrm((N_B, D_MODEL, B_IN), D_MODEL ** -0.5)
    b_q_norm = gain((N_B, SW_HEAD_DIM))
    b_sinks = nrm((N_B, SW_Q_HEADS), 0.5)
    b_w_out = nrm((N_B, B_OUT, D_MODEL), B_OUT ** -0.5)
    mem_norm = gain((DEPTH, D_MODEL))
    w_mem_kv = nrm((DEPTH, D_MODEL, 2 * MEM_W), D_MODEL ** -0.5)
    mem_q_norm = gain((DEPTH, MEM_HEAD_DIM))
    mem_k_norm = gain((DEPTH, MEM_HEAD_DIM))
    ffn_norm = gain((DEPTH, D_MODEL))
    w_gate_up = nrm((DEPTH, D_MODEL, 2 * D_FF), D_MODEL ** -0.5)
    w_down = nrm((DEPTH, D_FF, D_MODEL), D_FF ** -0.5)
    return dict(x=x, mem=mem, a_norm=a_norm, a_w_in=a_w_in, a_conv=a_conv, a_A_log=a_A_log,
                a_dt_bias=a_dt_bias, a_out_norm=a_out_norm, a_w_out=a_w_out, kv_norm=kv_norm,
                w_kv=w_kv, k_norm=k_norm, b_norm=b_norm, b_w_in=b_w_in, b_q_norm=b_q_norm,
                b_sinks=b_sinks, b_w_out=b_w_out, mem_norm=mem_norm, w_mem_kv=w_mem_kv,
                mem_q_norm=mem_q_norm, mem_k_norm=mem_k_norm, ffn_norm=ffn_norm,
                w_gate_up=w_gate_up, w_down=w_down)

def reference(x, mem, a_norm, a_w_in, a_conv, a_A_log, a_dt_bias, a_out_norm, a_w_out,
              kv_norm, w_kv, k_norm, b_norm, b_w_in, b_q_norm, b_sinks, b_w_out,
              mem_norm, w_mem_kv, mem_q_norm, mem_k_norm, ffn_norm, w_gate_up, w_down):
    shared_k = shared_v = None
    for i in range(DEPTH):
        mem_n = rms_norm(mem, mem_norm[i])
        if i < N_A:
            x = x + mixer_a(x, mem_n, a_norm[i], a_w_in[i], a_conv[i], a_A_log[i], a_dt_bias[i],
                            a_out_norm[i], a_w_out[i], w_mem_kv[i], mem_q_norm[i], mem_k_norm[i])
        else:
            j = i - N_A
            x = x + mixer_b(x, shared_k, shared_v, mem_n, b_norm[j], b_w_in[j], b_q_norm[j],
                            b_sinks[j], b_w_out[j], w_mem_kv[i], mem_q_norm[i], mem_k_norm[i])
        x = x + swiglu(rms_norm(x, ffn_norm[i]), w_gate_up[i], w_down[i])
        if i == N_A - 1:
            shared_k, shared_v = shared_kv(x, kv_norm, w_kv, k_norm)
    return x


_drawn_inputs = setup_inputs


def setup_inputs(seed=0):
    import zlib

    import numpy as np

    out = dict(_drawn_inputs(seed))
    spreads = {}
    factors = {'a_norm': 3.127,
     'a_out_norm': 5.144,
     'kv_norm': 8.0,
     'k_norm': 8.0,
     'b_norm': 8.0,
     'b_q_norm': 8.0,
     'b_sinks': 8.0,
     'mem_norm': 8.0,
     'mem_q_norm': 8.0,
     'mem_k_norm': 8.0,
     'ffn_norm': 2.828}
    for name, (base, spread) in spreads.items():
        noise = np.random.default_rng([zlib.crc32(name.encode()), seed]).standard_normal(out[name].shape)
        drawn = base * np.exp(spread * noise) if base else spread * noise
        out[name] = __import__('jax').numpy.asarray(drawn.astype(out[name].dtype))
    for name, factor in factors.items():
        out[name] = (out[name] * factor).astype(out[name].dtype)
    return out
```

```python
import math
from contextlib import ExitStack

import numpy as np

import concourse.bass as bass
from concourse import mybir

F32 = mybir.dt.float32
F32R = mybir.dt.float32r
ALU = mybir.AluOpType
ACT = mybir.ActivationFunctionType
AX = mybir.AxisListType

P = 128
D_MODEL = 1024
SEQ = 512
MEM_LEN = 256
DN_HEADS = 8
DN_W = DN_HEADS * P
MEM_HEADS = 4
MEM_W = MEM_HEADS * P
SW_HEADS = 16
SW_DIM = 64
SW_KV = 2
D_FF = -(-8 * D_MODEL // (3 * 256)) * 256
EPS = 1e-6

KT = D_MODEL // P
NT = SEQ // P
MT_ = MEM_LEN // P
CAT = (DN_W + MEM_W) // P
HALF = D_FF // P // 2
WIN = 3 * SW_DIM
LEVELS = 7
QPB = P // SW_DIM

_order = [("mem0", 2 * MEM_HEADS), ("mem1", 2 * MEM_HEADS), ("dn", 4 * DN_HEADS), ("mq0", MEM_HEADS),
          ("out0", 2 * KT), ("up00", 2 * HALF), ("down00", 2 * KT), ("up01", 2 * HALF), ("down01", 2 * KT),
          ("kv", 2), ("swq", SW_HEADS // QPB), ("mq1", MEM_HEADS), ("out1", 2 * KT),
          ("up10", 2 * HALF), ("down10", 2 * KT), ("up11", 2 * HALF), ("down11", 2 * KT)]
BLOCK0, TILE0 = {}, {}
_b = _n = 0
for _name, _count in _order:
    BLOCK0[_name], TILE0[_name] = _b, _n
    _b += _count
    _n += _count // 2 if _name.startswith(("out", "down")) else _count
N_BLOCKS, N_TILES = _b, _n
OUT_SUB = (CAT // 2, CAT // 2)
DOWN_SUB = ((HALF + 1) // 2, HALF // 2)
RING = 4


def subtiles(block):
    for name, count in _order:
        if BLOCK0[name] <= block < BLOCK0[name] + count:
            half = (block - BLOCK0[name]) % 2
            return OUT_SUB[half] if name.startswith("out") else DOWN_SUB[half] if name.startswith("down") else KT
    raise ValueError(block)


COLS = {}
_c = 0
for _name, _count in [("a_norm", KT), ("ffn0", KT), ("kv_norm", KT), ("b_norm", KT), ("ffn1", KT), ("mem0", KT),
                      ("mem1", KT), ("out_norm", 1), ("mq0", 1), ("mq1", 1), ("mk0", 1), ("mk1", 1), ("k_norm", 1),
                      ("q_norm", 1), ("conv", DN_HEADS * 3 * 4), ("a_log", DN_HEADS), ("dt", DN_HEADS),
                      ("sinks", SW_HEADS), ("nslope", SW_HEADS), ("eps", 1), ("ln_q", 1), ("ln_s", 1)]:
    COLS[_name] = _c
    _c += _count
N_COLS = _c

(IDENT, ONES, ONES64, TRIU, NEG_LOWER, LEVEL0) = range(6)
N_SQ = 6 + LEVELS - 1


def squares():
    r, c = np.arange(P)[:, None], np.arange(P)[None, :]
    out = np.zeros((P, N_SQ, P), np.float32)
    out[:, IDENT] = r == c
    out[:, ONES] = 1.0
    out[:, ONES64] = r // SW_DIM == c // SW_DIM
    out[:, TRIU] = r <= c
    out[:, NEG_LOWER] = np.where(r <= c, 0.0, -1e30)
    out[:, LEVEL0] = (c == r + 1) & (r % 2 == 0)
    for k in range(1, LEVELS):
        b = 2 ** k
        out[:, LEVEL0 + k] = (r // b % 2 == 1) & (c // b == r // b - 1)
    return out


def distances():
    i, j = np.arange(P)[:, None], np.arange(WIN)[None, :]
    d = np.abs(i + SW_DIM - j).astype(np.float32)
    d = np.where((j // SW_DIM >= i // SW_DIM) & (j // SW_DIM <= i // SW_DIM + 1), d, 1e30)
    out = np.repeat(d[:, None, :], NT, axis=1)
    out[:, 0, :SW_DIM] = 1e30
    return out.astype(np.float32)


KR, KS, KRS = 14, 18, 15
(CQ, CK, CV, SZ, QN, KN, TT, ZZ, AT, MM, PM, DD, EG, VB, KBG, KDEC, E0, E1, EC) = range(19)
WS = 19


def yoco_kernel(nc, x, mem, w_stream, w_out, w_down, w_ba, cols_in, squares_in, dist_in, out):
    with ExitStack() as ctx:
        def sb(name, shape, dt=F32):
            return ctx.enter_context(nc.sbuf_tensor(name, shape, dt))

        def sem(name):
            return ctx.enter_context(nc.semaphore(name))

        xT = sb("xT", [P, KT, SEQ])
        act_hi = sb("act_hi", [P, KT + CAT, SEQ], F32R)
        act_lo = sb("act_lo", [P, KT + CAT, SEQ], F32R)
        w_raw = sb("w_raw", [P, RING, KT * P])
        w_hi = sb("w_hi", [P, RING, KT * P], F32R)
        w_lo = sb("w_lo", [P, RING, KT * P], F32R)
        ws = sb("ws", [P, WS, SEQ])
        kmem = sb("kmem", [P, 2 * MEM_HEADS, MEM_LEN])
        vmem = sb("vmem", [P, 2 * MEM_HEADS, MT_ * P])
        sq_c = sb("sq_c", [P, N_SQ, P])
        cols = sb("cols", [P, N_COLS])
        dn_s = sb("dn_s", [P, 8, DN_HEADS * NT])
        state = sb("state", [P, P])
        st = sb("st", [P, 64])

        bank = ctx.enter_context(nc.psum_tensor("bank", [P, 8, 512], F32))

        class S:
            consts_loaded = sem("consts_loaded")
            cols_loaded = sem("cols_loaded")
            dist_loaded = sem("dist_loaded")
            x_loaded = sem("x_loaded")
            mem_loaded = sem("mem_loaded")
            ba_loaded = sem("ba_loaded")
            hi_done = sem("hi_done")
            lo_done = sem("lo_done")
            block_used = sem("block_used")
            acc_free = sem("acc_free")
            m_sq = sem("m_sq")
            m_ln = sem("m_ln")
            m_rstd = sem("m_rstd")
            m_scaled = sem("m_scaled")
            m_tr = sem("m_tr")
            m_evac_hi = sem("m_evac_hi")
            m_evac_lo = sem("m_evac_lo")
            x_sq = sem("x_sq")
            x_ln = sem("x_ln")
            x_rstd = sem("x_rstd")
            x_scaled = sem("x_scaled")
            x_raw_tr = sem("x_raw_tr")
            x_raw_copied = sem("x_raw_copied")
            x_tr = sem("x_tr")
            x_evac_hi = sem("x_evac_hi")
            x_evac_lo = sem("x_evac_lo")
            mk_sq = sem("mk_sq")
            mk_ss = sem("mk_ss")
            mk_ln = sem("mk_ln")
            mk_rstd = sem("mk_rstd")
            mk_done = sem("mk_done")
            ba_hi = sem("ba_hi")
            ba_split = sem("ba_split")
            ba_mm = sem("ba_mm")
            ba_dve = sem("ba_dve")
            ba_act = sem("ba_act")
            ba_g = sem("ba_g")
            ba_cum = sem("ba_cum")
            cv_tap = sem("cv_tap")
            cv_conv = sem("cv_conv")
            cv_exp = sem("cv_exp")
            cv_one = sem("cv_one")
            c_ready = sem("c_ready")
            sq_done = sem("sq_done")
            ss_done = sem("ss_done")
            rr_ln = sem("rr_ln")
            rr_done = sem("rr_done")
            qn_done = sem("qn_done")
            kn_done = sem("kn_done")
            ug_done = sem("ug_done")
            gb_done = sem("gb_done")
            eg_done = sem("eg_done")
            dm_pre = sem("dm_pre")
            dm_done = sem("dm_done")
            kb_done = sem("kb_done")
            vtr_done = sem("vtr_done")
            ktr_done = sem("ktr_done")
            vb_done = sem("vb_done")
            kbg_done = sem("kbg_done")
            kdec_done = sem("kdec_done")
            qd_done = sem("qd_done")
            gg_done = sem("gg_done")
            at_done = sem("at_done")
            mt_done = sem("mt_done")
            z_pre = sem("z_pre")
            z_done = sem("z_done")
            t_tr = sem("t_tr")
            t_done = sem("t_done")
            p_mm = sem("p_mm")
            p_done = sem("p_done")
            tz_mm = sem("tz_mm")
            tz_done = sem("tz_done")
            nw_mm = sem("nw_mm")
            nw_done = sem("nw_done")
            v_mm = sem("v_mm")
            v_done = sem("v_done")
            s_mm = sem("s_mm")
            s_done = sem("s_done")
            o_done = sem("o_done")
            osq = sem("osq")
            oss = sem("oss")
            o_ln = sem("o_ln")
            o_rstd = sem("o_rstd")
            o_t1 = sem("o_t1")
            o_t2 = sem("o_t2")
            o_hi = sem("o_hi")
            o_lo = sem("o_lo")
            mq_sq = sem("mq_sq")
            mq_ss = sem("mq_ss")
            mq_ln = sem("mq_ln")
            mq_rstd = sem("mq_rstd")
            mq_n = sem("mq_n")
            mq_sc = sem("mq_sc")
            mq_max = sem("mq_max")
            mq_exp = sem("mq_exp")
            mq_rcp = sem("mq_rcp")
            mq_p = sem("mq_p")
            mq_tr = sem("mq_tr")
            mq_pt = sem("mq_pt")
            mq_o = sem("mq_o")
            mq_hi = sem("mq_hi")
            mq_lo = sem("mq_lo")
            r_hi = sem("r_hi")
            r_lo = sem("r_lo")
            r_sq = sem("r_sq")
            r_acc = sem("r_acc")
            r_ss = sem("r_ss")
            r_ln = sem("r_ln")
            r_done = sem("r_done")
            f_silu = sem("f_silu")
            f_hid = sem("f_hid")
            f_hi = sem("f_hi")
            f_lo = sem("f_lo")
            kv_sq = sem("kv_sq")
            kv_ss = sem("kv_ss")
            kv_ln = sem("kv_ln")
            kv_rstd = sem("kv_rstd")
            kv_n = sem("kv_n")
            kv_dup = sem("kv_dup")
            kv_done = sem("kv_done")
            kv_r = sem("kv_r")
            b_h = sem("b_h")
            b_hi = sem("b_hi")
            b_lo = sem("b_lo")
            sw_sq = sem("sw_sq")
            sw_ss = sem("sw_ss")
            sw_ln = sem("sw_ln")
            sw_rstd = sem("sw_rstd")
            sw_sc = sem("sw_sc")
            sw_s = sem("sw_s")
            sw_mx = sem("sw_mx")
            sw_nm = sem("sw_nm")
            sw_exp = sem("sw_exp")
            sw_den = sem("sw_den")
            sw_p = sem("sw_p")
            sw_tr = sem("sw_tr")
            sw_pt = sem("sw_pt")
            sw_ptp = sem("sw_ptp")
            sw_o = sem("sw_o")
            sw_o_hi = sem("sw_o_hi")
            sw_o_lo = sem("sw_o_lo")
            fin_tr = sem("fin_tr")
            fin_done = sem("fin_done")

        raw_loaded = [sem(f"raw_loaded{i}") for i in range(RING)]
        stored = sem("stored")

        block = ctx.enter_context(nc.Block())

        def due(n):
            return not isinstance(n, int) or n > 0

        def at_once(eng):
            eng.wait_ge(S.consts_loaded, 16)

        def turns(eng, n, body):
            body(0)
            if n > 3:
                with eng.Fori(1, n - 1) as i:
                    body(i)
            elif n == 3:
                body(1)
            if n > 1:
                body(n - 1)

        def w(i):
            return ws[:, i, :]

        def w4(i):
            return ws[:, i, :].rearrange("p (t c) -> p t c", t=NT)

        def sq(i):
            return sq_c[:, i, :]

        def over_tiles(i):
            return sq_c[:, i:i + 1, :].to_broadcast([P, NT, P])

        def col(name, i=0):
            return cols[:, COLS[name] + i:COLS[name] + i + 1]

        def psum(b, n=512):
            return bank[:, b, 0:n]

        def psum4(b):
            return bank[:, b, :].rearrange("p (t c) -> p t c", t=NT)

        def tt(i, t):
            return ws[:, i, t * P:(t + 1) * P]

        D = [2, 3, 4, 5, 6, 7]

        BETA, GG, GCUM, GL, EDEC, NBEG, TMP1, TMP2 = range(8)

        def dn(i):
            return dn_s[:, i, :].rearrange("p (h t) -> p h t", h=DN_HEADS)

        def dn_bcast(i, h):
            return dn(i)[:, h, :].unsqueeze(2).to_broadcast([P, NT, P])

        kwin = ws[:, 8:11, :].rearrange("p t c -> p (t c)")[:, 0:SW_KV * (SW_DIM + SEQ)].rearrange(
            "p (g c) -> p g c", g=SW_KV)
        V_T, PT_OWN, PT_PREV, R_T, SQ_T, KN_T = 11, (12, 13), (14, 15), 16, 15, 5

        def swp(e):
            return ws[:, 4 + 2 * e:6 + 2 * e, :].rearrange("p a (t c) -> p (a t) c", c=2 * P)

        distance = ws[:, 17:19, :].rearrange("p t c -> p (t c)")[:, 0:NT * WIN].rearrange("p (t c) -> p t c", t=NT)
        ba_w = sb("ba_w", [P, 2, KT * 16], F32R)

        H_AT = (0, KT)

        H_NEXT = {"out0": 0, "down01": 0, "out1": KT}

        def col_k(name, k):
            return cols[:, bass.ds(k + COLS[name], 1)]

        def conv_w(h, j, tap):
            return cols[:, bass.ds(12 * h + (COLS["conv"] + 4 * j + tap), 1)]

        def hid_tile(layer, it, j):
            if layer == 0:
                return 2 * it + j + KT
            return 2 * it + j if j < 8 else KT + j

        def mq_p_of(t):
            return ws[:, 4 + t // 2, (t % 2) * MEM_LEN:(t % 2 + 1) * MEM_LEN]

        def cat_tile(layer, k):
            return KT + k if layer == 0 else (k if k < KT else KT + k)

        @block.sync
        def _(sp):
            sp.dma_start(ws[:, 8:12, :].rearrange("p t c -> p (t c)"),
                         mem.rearrange("(t p) d -> p t d", p=P)).then_inc(S.mem_loaded, 16)
            sp.dma_start(sq_c[:], squares_in).then_inc(S.consts_loaded, 16)
            sp.dma_start(cols[:], cols_in).then_inc(S.cols_loaded, 16)

            sp.dma_start(ws[:, E0, 0:KT * 16], w_ba).then_inc(S.ba_loaded, 16)

            def load(it, c, source, width):
                b = 4 * it + c
                if due(b - RING + 1):
                    sp.wait_ge(S.hi_done, b - RING + 1)
                if due(b - RING + 1):
                    sp.wait_ge(S.lo_done, b - RING + 1)
                sp.dma_start(w_raw[:, c % RING, 0:width * P], source).then_inc(raw_loaded[c % RING], 16)

            def load_plain(name, base_row, count):
                b0 = BLOCK0[name]

                def body(i):
                    for j in range(4):
                        load(i, b0 + j, w_stream[base_row + 4 * i + j], KT)
                if count >= 4:
                    turns(sp, count // 4, body)
                for j in range(count // 4 * 4, count):
                    load(0, b0 + j, w_stream[base_row + j], KT)

            def load_pairs(name, array, sub):
                b0 = BLOCK0[name]

                def body(i):
                    for j in range(4):
                        lo = (j % 2) * sub[0] * P
                        load(i, b0 + j, array[2 * i + j // 2, :, lo:lo + sub[j % 2] * P], sub[j % 2])
                turns(sp, KT // 2, body)

            row = 0
            for name, count in _order:
                if name.startswith("out"):
                    load_pairs(name, w_out[int(name[3])], OUT_SUB)
                elif name.startswith("down"):
                    load_pairs(name, w_down[2 * int(name[4]) + int(name[5])], DOWN_SUB)
                else:
                    load_plain(name, row, count)
                    row += count
                if name == "mem0":
                    sp.dma_start(ws[:, 0:8, :].rearrange("p t c -> p (t c)"),
                                 x.rearrange("(t p) d -> p t d", p=P)).then_inc(S.x_loaded, 16)
                if name == "kv":
                    sp.dma_start(ws[:, 17:19, :].rearrange("p t c -> p (t c)")[:, 0:NT * WIN],
                                 dist_in.rearrange("p t c -> p (t c)")).then_inc(S.dist_loaded, 16)
            sp.wait_ge(S.fin_done, NT)
            sp.dma_start(out.rearrange("(t p) d -> p t d", p=P),
                         ws[:, 0:8, :].rearrange("p (t a) c -> p t (a c)", t=NT)).then_inc(stored, 16)
            sp.wait_ge(stored, 16)

        @block.gpsimd
        def _(pool):
            def lower(it, c, width):
                pool.wait_ge(S.hi_done, 4 * it + c + 1)
                s = c % RING
                nc.gpsimd.tensor_tensor(w_lo[:, s, 0:width * P], w_raw[:, s, 0:width * P],
                                        w_hi[:, s, 0:width * P].bitcast(F32), ALU.subtract).then_inc(S.lo_done, 1)

            for name, count in _order:
                b0 = BLOCK0[name]
                if count >= 4:
                    turns(pool, count // 4, lambda i: [lower(i, b0 + j, subtiles(b0 + j)) for j in range(4)])
                for j in range(count // 4 * 4, count):
                    lower(0, b0 + j, subtiles(b0 + j))

        @block.tensor
        def _(pe):
            def product(it, c, nsub, k0, act0, acc, start, stop, n=SEQ, off=0, part=(0, 2)):
                if part[0] == 0:
                    pe.wait_ge(S.lo_done, 4 * it + c + 1)
                ks = range(nsub * part[0] // 2, nsub * part[1] // 2)
                for k in ks:
                    wsl = slice(k * P, (k + 1) * P)
                    for m, (wt, at) in enumerate(((w_hi, act_hi), (w_hi, act_lo), (w_lo, act_hi))):
                        mm = nc.tensor.matmul(acc, wt[:, c % RING, wsl], at[:, act0(k0 + k), off:off + n],
                                              start=(start and k == 0 and m == 0),
                                              stop=(stop and k == nsub - 1 and m == 2))
                if ks[-1] == nsub - 1:
                    mm.then_inc(S.block_used, 1)

            def acc_ready(n):
                if due(n - 1):
                    pe.wait_ge(S.acc_free, n - 1)

            def transposes4(dst, source):
                for t in range(NT):
                    mm = nc.tensor.transpose(bank[:, dst, t * P:(t + 1) * P], tt(source, t), sq(IDENT))
                return mm

            pe.wait_ge(S.consts_loaded, 16)
            pe.wait_ge(S.m_scaled, MT_)
            for k in range(KT):
                if k >= 4:
                    if due(2 * (k - 3)):
                        pe.wait_ge(S.m_evac_hi, 2 * (k - 3))
                    if due(2 * (k - 3)):
                        pe.wait_ge(S.m_evac_lo, 2 * (k - 3))
                for t in range(MT_):
                    mm = nc.tensor.transpose(bank[:, D[k % 4], t * P:(t + 1) * P],
                                             ws[:, 8 + 2 * t:10 + 2 * t, :].rearrange("p a c -> p (a c)")[
                                                 :, k * P:(k + 1) * P], sq(IDENT))
                mm.then_inc(S.m_tr, 1)

            def mem_proj(layer):
                b0, n0 = BLOCK0[f"mem{layer}"], TILE0[f"mem{layer}"]
                pe.wait_ge(S.m_evac_lo, 2 * KT)

                def body(i):
                    for j in range(2):
                        n = n0 + 4 * i + 2 * j
                        head = 2 * i + j + MEM_HEADS * layer
                        acc_ready(n)
                        product(i, b0 + 2 * j, KT, 0, lambda k: KT + k, psum(0, MEM_LEN), True, True,
                                n=MEM_LEN, off=MEM_LEN * layer)
                        acc_ready(n + 1)
                        pe.wait_ge(S.lo_done, 4 * i + b0 + 2 * j + 2)
                        s = (b0 + 2 * j + 1) % RING
                        for t in range(MT_):
                            off = MEM_LEN * layer + t * P
                            for k in range(KT):
                                for m, (at, wt) in enumerate(((act_hi, w_hi), (act_lo, w_hi), (act_hi, w_lo))):
                                    mm = nc.tensor.matmul(bank[:, 1, t * P:(t + 1) * P],
                                                          at[:, KT + k, off:off + P],
                                                          wt[:, s, k * P:(k + 1) * P],
                                                          start=(k == 0 and m == 0), stop=(k == KT - 1 and m == 2))
                        mm.then_inc(S.block_used, 1)
                        pe.wait_ge(S.mk_sq, head + 1)
                        if due(head):
                            pe.wait_ge(S.mk_ln, head)
                        nc.tensor.matmul(psum(D[4], MEM_LEN), sq(ONES), w(KS)[:, 0:MEM_LEN],
                                         start=True, stop=True).then_inc(S.mk_ss, 1)
                turns(pe, MEM_HEADS // 2, body)

            mem_proj(0)

            def x_transposes(k):
                for t in range(NT):
                    mm = nc.tensor.transpose(bank[:, D[k % 4], t * P:(t + 1) * P],
                                             ws[:, 2 * t:2 * t + 2, :].rearrange("p a c -> p (a c)")[
                                                 :, k * P:(k + 1) * P], sq(IDENT))
                return mm
            pe.wait_ge(S.x_loaded, 16)
            for k in range(KT):
                if due(k - 3):
                    pe.wait_ge(S.x_raw_copied, k - 3)
                x_transposes(k).then_inc(S.x_raw_tr, 1)
            mem_proj(1)
            pe.wait_ge(S.x_scaled, NT)
            pe.wait_ge(S.x_raw_copied, KT)
            for k in range(KT):
                if due(k - 3):
                    pe.wait_ge(S.x_evac_lo, k - 3)
                x_transposes(k).then_inc(S.x_tr, 1)

            pe.wait_ge(S.x_evac_lo, KT)
            pe.wait_ge(S.ba_split, 1)
            for t in range(NT):
                for k in range(KT):
                    for m, (at, wi) in enumerate(((act_hi, 0), (act_lo, 0), (act_hi, 1))):
                        mm = nc.tensor.matmul(bank[:, D[0], t * 16:(t + 1) * 16], at[:, k, t * P:(t + 1) * P],
                                              ba_w[:, wi, k * 16:(k + 1) * 16],
                                              start=(k == 0 and m == 0), stop=(k == KT - 1 and m == 2))
            mm.then_inc(S.ba_mm, 1)
            pe.wait_ge(S.ba_g, 1)
            nc.tensor.matmul(bank[:, D[1], 0:32], sq(TRIU), dn_s[:, GG, :], start=True, stop=True)
            nc.tensor.matmul(bank[:, D[2], 0:32], sq(ONES), dn_s[:, GG, :], start=True, stop=True
                             ).then_inc(S.ba_cum, 1)

            def proj_dn(h, j):
                c = BLOCK0["dn"] + j
                acc_ready(TILE0["dn"] + 4 * h + j)
                product(h, c, KT, 0, lambda k: k, psum(j % 2), True, True)

            def delta(h, fill):
                pe.wait_ge(S.sq_done, 2 * h + 1)
                if due(h):
                    pe.wait_ge(S.at_done, h)
                nc.tensor.matmul(psum(D[0]), sq(ONES), w(E0), start=True, stop=True).then_inc(S.ss_done, 1)
                pe.wait_ge(S.sq_done, 2 * h + 2)
                if due(h):
                    pe.wait_ge(S.mt_done, h)
                nc.tensor.matmul(psum(D[1]), sq(ONES), w(E1), start=True, stop=True).then_inc(S.ss_done, 1)
                pe.wait_ge(S.ug_done, 2 * h + 1)
                if due(h):
                    pe.wait_ge(S.o_ln, h)
                nc.tensor.matmul(psum(D[2]), sq(ONES), w(KBG), start=True, stop=True).then_inc(S.gb_done, 1)
                pe.wait_ge(S.ug_done, 2 * h + 2)
                if due(NT * h):
                    pe.wait_ge(S.v_done, NT * h)
                nc.tensor.matmul(psum(D[3]), sq(ONES), w(KDEC), start=True, stop=True).then_inc(S.gb_done, 1)
                pe.wait_ge(S.c_ready, 3 * h + 3)
                if due(3 * h):
                    pe.wait_ge(S.s_done, 3 * h)
                transposes4(D[4], CV).then_inc(S.vtr_done, 1)
                pe.wait_ge(S.kn_done, h + 1)
                if due(h):
                    pe.wait_ge(S.o_t1, h)
                transposes4(D[5], KN).then_inc(S.ktr_done, 1)
                fill(0)
                pe.wait_ge(S.kb_done, h + 1)
                for t in range(NT):
                    mm = nc.tensor.matmul(bank[:, D[1], t * P:(t + 1) * P], tt(KN, t), tt(PM, t), start=True, stop=True)
                mm.then_inc(S.gg_done, 1)
                pe.wait_ge(S.qn_done, h + 1)
                for t in range(NT):
                    mm = nc.tensor.matmul(bank[:, D[0], t * P:(t + 1) * P], tt(KN, t), tt(QN, t), start=True, stop=True)
                mm.then_inc(S.gg_done, 1)
                fill(1)
                pe.wait_ge(S.z_done, h + 1)
                pe.wait_ge(S.dm_pre, 2 * h + 1)
                transposes4(D[2], ZZ).then_inc(S.t_tr, 1)
                for k in range(1, LEVELS):
                    last = k == LEVELS - 1
                    n = 6 * h + k
                    pe.wait_ge(S.t_done, h + 1)
                    if due(n - 1):
                        pe.wait_ge(S.tz_done, n - 1)
                    for t in range(NT):
                        mm = nc.tensor.matmul(bank[:, D[3], t * P:(t + 1) * P], tt(MM, t), tt(TT, t),
                                              start=True, stop=True)
                    mm.then_inc(S.p_mm, 1)
                    if k == 3:
                        fill(2)
                    if due(n):
                        pe.wait_ge(S.p_done, n)
                    pe.wait_ge(S.vb_done, h + 1)
                    pe.wait_ge(S.kdec_done, h + 1)
                    for t in range(NT):
                        if not last:
                            nc.tensor.matmul(bank[:, D[4], t * P:(t + 1) * P], tt(ZZ, t), tt(PM, t),
                                             start=True, stop=True)
                        mm = nc.tensor.matmul(bank[:, D[5], t * P:(t + 1) * P], tt(PM, t), tt(ZZ, t),
                                              start=True, stop=True)
                    mm.then_inc(S.tz_mm, 1)
                pe.wait_ge(S.tz_done, 6 * h + 6)
                pe.wait_ge(S.kbg_done, h + 1)
                for t in range(NT):
                    mm = nc.tensor.matmul(bank[:, D[2], t * P:(t + 1) * P], tt(KBG, t), tt(ZZ, t), start=True, stop=True)
                mm.then_inc(S.nw_mm, 1)
                pe.wait_ge(S.at_done, h + 1)
                for t in range(NT):
                    n = NT * h + t
                    if due(n):
                        pe.wait_ge(S.v_done, n)
                    v_acc = bank[:, D[3], 0:P]
                    mm = nc.tensor.matmul(v_acc, tt(ZZ, t), tt(VB, t), start=True, stop=(t == 0))
                    if t:
                        pe.wait_ge(S.nw_done, h + 1)
                        if due(3 * h + t):
                            pe.wait_ge(S.s_done, 3 * h + t)
                        mm = nc.tensor.matmul(v_acc, tt(MM, t), state[:], start=False, stop=True)
                    mm.then_inc(S.v_mm, 1)
                    o_acc = bank[:, D[5], t * P:(t + 1) * P]
                    pe.wait_ge(S.qd_done, h + 1)
                    if t:
                        nc.tensor.matmul(o_acc, state[:], tt(EG, t), start=True, stop=False)
                    pe.wait_ge(S.v_done, n + 1)
                    if t < NT - 1:
                        nc.tensor.matmul(bank[:, D[4], 0:P], tt(KDEC, t), ws[:, E0, t * P:(t + 1) * P],
                                         start=True, stop=True).then_inc(S.s_mm, 1)
                    mm = nc.tensor.matmul(o_acc, ws[:, E0, t * P:(t + 1) * P], tt(AT, t), start=(t == 0), stop=True)
                mm.then_inc(S.o_done, 1)
                fill(3)
                pe.wait_ge(S.osq, h + 1)
                nc.tensor.matmul(psum(D[2]), sq(ONES), w(E1), start=True, stop=True).then_inc(S.oss, 1)

            pe.wait_ge(S.x_evac_lo, KT)
            for j in range(4):
                proj_dn(0, j)
            turns(pe, DN_HEADS - 1, lambda h: delta(h, lambda j: proj_dn(h + 1, j)))
            delta(DN_HEADS - 1, lambda j: None)

            def mem_attention(layer):
                name = f"mq{layer}"

                def project(j, part):
                    if part[0] == 0:
                        acc_ready(TILE0[name] + j)
                    product(0, BLOCK0[name] + j, KT, 0, lambda k: H_AT[layer] + k, psum(j % 2),
                            True, True, part=part)
                project(0, (0, 2))
                for j in range(MEM_HEADS):
                    u = layer * MEM_HEADS + j
                    pe.wait_ge(S.mq_sq, u + 1)
                    if due(u):
                        pe.wait_ge(S.mq_ln, u)
                    nc.tensor.matmul(psum(D[0]), sq(ONES), w(1), start=True, stop=True).then_inc(S.mq_ss, 1)
                    if j + 1 < MEM_HEADS:
                        project(j + 1, (0, 1))
                    pe.wait_ge(S.mq_n, u + 1)
                    for t in range(NT):
                        mm = nc.tensor.matmul(bank[:, D[2] + t // 2, (t % 2) * MEM_LEN:(t % 2 + 1) * MEM_LEN],
                                              tt(3, t), kmem[:, u, :], start=True, stop=True)
                    mm.then_inc(S.mq_sc, 1)
                    if j + 1 < MEM_HEADS:
                        project(j + 1, (1, 2))
                    pe.wait_ge(S.mq_p, u + 1)
                    for m in range(MT_):
                        for t in range(NT):
                            p_t = ws[:, 4:6, :].rearrange("p a c -> p (a c)")[
                                :, t * MEM_LEN + m * P:t * MEM_LEN + (m + 1) * P]
                            mm = nc.tensor.transpose(bank[:, D[4] + m, t * P:(t + 1) * P], p_t, sq(IDENT))
                    mm.then_inc(S.mq_tr, 1)
                    pe.wait_ge(S.mq_pt, u + 1)
                    for m in range(MT_):
                        mm = nc.tensor.matmul(psum(D[1]), vmem[:, u, m * P:(m + 1) * P], w(6 + m),
                                              start=(m == 0), stop=(m == MT_ - 1))
                    mm.then_inc(S.mq_o, 1)

            mem_attention(0)

            def out_tiles(name, layer, sub, act_of):
                def body(i):
                    for j in range(2):
                        acc_ready(TILE0[name] + 2 * i + j)
                        c = BLOCK0[name] + 2 * j
                        product(i, c, sub[0], 0, act_of, psum(j), True, False)
                        product(i, c + 1, sub[1], sub[0], act_of, psum(j), False, True)
                turns(pe, KT // 2, body)

            def row_sums(r):
                if due(KT * (r + 1)):
                    pe.wait_ge(S.r_acc, KT * (r + 1))
                nc.tensor.matmul(psum(D[0]), sq(ONES), w(SQ_T), start=True, stop=True).then_inc(S.r_ss, 1)

            def ffn(layer):
                h_of = (lambda k: H_AT[layer] + k)
                for half in range(2):
                    b0, n0 = BLOCK0[f"up{layer}{half}"], TILE0[f"up{layer}{half}"]

                    def pair(it, j):
                        for g in range(2):
                            acc_ready(4 * it + n0 + 2 * j + g)
                            product(it, b0 + 2 * j + g, KT, 0, h_of, psum(g), True, True)
                            if half == 0 and isinstance(it, int) and (it, j, g) == (0, 0, 0):
                                row_sums(2 * layer)

                    def body(it):
                        pair(it, 0)
                        pair(it, 1)
                    if half == 0:
                        if due(KT * (2 * layer + 1)):
                            pe.wait_ge(S.r_lo, KT * (2 * layer + 1))
                    turns(pe, 4, body)
                    for j in range(8, HALF):
                        pair(0, j)
                    pe.wait_ge(S.f_lo, HALF * (2 * layer + half + 1))
                    out_tiles(f"down{layer}{half}", layer, DOWN_SUB, lambda k: cat_tile(layer, k))

            pe.wait_ge(S.mq_lo, MEM_HEADS)
            pe.wait_ge(S.o_lo, DN_HEADS)
            out_tiles("out0", 0, OUT_SUB, lambda k: cat_tile(0, k))
            ffn(0)

            pe.wait_ge(S.r_lo, 2 * KT)
            acc_ready(TILE0["kv"])
            product(0, BLOCK0["kv"], KT, 0, lambda k: k, psum(0), True, True)
            row_sums(1)
            acc_ready(TILE0["kv"] + 1)
            pe.wait_ge(S.lo_done, BLOCK0["kv"] + 2)
            s = (BLOCK0["kv"] + 1) % RING
            for t in range(NT):
                for k in range(KT):
                    for m, (at, wt) in enumerate(((act_hi, w_hi), (act_lo, w_hi), (act_hi, w_lo))):
                        mm = nc.tensor.matmul(bank[:, 1, t * P:(t + 1) * P], at[:, k, t * P:(t + 1) * P],
                                              wt[:, s, k * P:(k + 1) * P],
                                              start=(k == 0 and m == 0), stop=(k == KT - 1 and m == 2))
            mm.then_inc(S.block_used, 1)
            pe.wait_ge(S.r_done, 2)
            for t in range(NT):
                mm = nc.tensor.matmul(bank[:, D[1], t:t + 1], ws[:, R_T, t * P:(t + 1) * P], sq_c[:, IDENT, 0:1],
                                      start=True, stop=True)
            mm.then_inc(S.kv_ss, 1)
            pe.wait_ge(S.kv_sq, 1)
            pe.wait_ge(S.r_ln, 2)
            nc.tensor.matmul(psum(D[0]), sq(ONES64), w(3), start=True, stop=True).then_inc(S.kv_ss, 1)

            def sw_project(it, j, part):
                c = BLOCK0["swq"] + j
                if part[0] == 0:
                    acc_ready(TILE0["swq"] + 4 * it + j)
                product(it, c, KT, 0, lambda k: KT + k, psum(j % 2), True, True, part=part)

            def sw_attention(it, j, fill):
                u = 4 * it + j
                pe.wait_ge(S.sw_sq, u + 1)
                if due(u):
                    pe.wait_ge(S.sw_o_hi, u)
                nc.tensor.matmul(psum(D[4]), sq(ONES64), w(1), start=True, stop=True).then_inc(S.sw_ss, 1)
                fill((0, 1))
                pe.wait_ge(S.acc_free, TILE0["swq"] + u + 1)
                if due(2 * u):
                    pe.wait_ge(S.sw_pt, 2 * u)
                for e in range(QPB):
                    rows = slice(SW_DIM * e, SW_DIM * (e + 1))
                    for t in range(NT):
                        mm = nc.tensor.matmul(bank[:, D[0] + 2 * e + t // 2, (t % 2) * 256:(t % 2) * 256 + WIN],
                                              ws[rows, 3, t * P:(t + 1) * P],
                                              kwin[rows, it, t * P:t * P + WIN],
                                              start=True, stop=True)
                    mm.then_inc(S.sw_sc, 1)
                fill((1, 2))
                for e in range(QPB):
                    pe.wait_ge(S.sw_p, 2 * u + e + 1)
                    own, prev = (D[4], D[5]) if e == 0 else (D[0], D[1])
                    for t in range(NT):
                        mm = nc.tensor.transpose(bank[:, own, t * P:(t + 1) * P], swp(e)[:, t, P:2 * P], sq(IDENT))
                        if t:
                            mm = nc.tensor.transpose(bank[:, prev, t * P:(t + 1) * P], swp(e)[:, t, 0:P], sq(IDENT))
                    mm.then_inc(S.sw_tr, 1)
                for e in range(QPB):
                    pe.wait_ge(S.sw_pt, 2 * u + e + 1)
                    pe.wait_ge(S.sw_ptp, 2 * u + e + 1)
                    rows = slice(SW_DIM * e, SW_DIM * (e + 1))
                    for t in range(NT):
                        o_acc = bank[rows, D[2], t * P:(t + 1) * P]
                        v_of = slice(it * SW_DIM, (it + 1) * SW_DIM)
                        mm = nc.tensor.matmul(o_acc, tt(V_T, t)[:, v_of], tt(PT_OWN[e], t),
                                              start=True, stop=(t == 0))
                        if t:
                            mm = nc.tensor.matmul(o_acc, tt(V_T, t - 1)[:, v_of], tt(PT_PREV[e], t),
                                                  start=False, stop=True)
                mm.then_inc(S.sw_o, 1)

            pe.wait_ge(S.b_lo, KT)
            sw_project(0, 0, (0, 2))
            for it in range(SW_KV):
                for j in range(4):
                    last = it == SW_KV - 1 and j == 3
                    nxt = (it, j + 1) if j < 3 else (it + 1, 0)
                    sw_attention(it, j, (lambda part: None) if last else (lambda part: sw_project(*nxt, part)))
            mem_attention(1)

            pe.wait_ge(S.mq_lo, 2 * MEM_HEADS)
            pe.wait_ge(S.sw_o_lo, SW_HEADS // QPB)
            out_tiles("out1", 1, OUT_SUB, lambda k: cat_tile(1, k))
            ffn(1)

            pe.wait_ge(S.acc_free, N_TILES)
            for t in range(NT):
                if t:
                    if due(t):
                        pe.wait_ge(S.fin_done, t)
                for k in range(KT):
                    mm = nc.tensor.transpose(bank[:, D[0] + k // 4, (k % 4) * P:(k % 4 + 1) * P],
                                             xT[:, k, t * P:(t + 1) * P], sq(IDENT))
                mm.then_inc(S.fin_tr, 1)

        @block.scalar
        def _(act):
            def a(out_, in_, func, **kw):
                return nc.scalar.activation(out_, in_, func, **kw)

            def upper(it, c):
                b = 4 * it + c
                if isinstance(b, int) and b >= N_BLOCKS:
                    return
                width = subtiles(b if isinstance(b, int) else c + 4) * P
                s = c % RING
                act.wait_ge(raw_loaded[s], 16 * it + 16 * (c // RING) + 16)
                if due(b - RING + 1):
                    act.wait_ge(S.block_used, b - RING + 1)
                a(w_hi[:, s, 0:width], w_raw[:, s, 0:width], ACT.Copy).then_inc(S.hi_done, 1)

            act.preload_act_table_set("natural_log_exp_and_others")
            act.wait_ge(S.mem_loaded, 16)
            act.wait_ge(S.cols_loaded, 16)

            def rows(first, t):
                return ws[:, first + 2 * t:first + 2 * t + 2, :].rearrange("p a c -> p (a c)")
            for t in range(MT_):
                a(rows(12, t), rows(8, t), ACT.Square, accum_out=st[:, t:t + 1]).then_inc(S.m_sq, 1)
            act.wait_ge(S.m_sq, MT_)
            a(st[:, 6:8], st[:, 0:2], ACT.Ln, scale=1.0 / D_MODEL, bias=col("eps")).then_inc(S.m_ln, 1)
            act.wait_ge(S.m_ln, 1)
            a(st[:, 6:8], st[:, 6:8], ACT.Exp, scale=-0.5).then_inc(S.m_rstd, 1)
            act.wait_ge(S.m_rstd, 1)
            for t in range(MT_):
                a(rows(8, t), rows(8, t), ACT.Copy, scale=st[:, 6 + t:7 + t]).then_inc(S.m_scaled, 1)
            upper(0, 0)
            upper(0, 1)
            for k in range(KT):
                act.wait_ge(S.m_tr, k + 1)
                for layer in range(2):
                    a(act_hi[:, KT + k, MEM_LEN * layer:MEM_LEN * (layer + 1)], psum(D[k % 4], MEM_LEN), ACT.Copy, scale=col(f"mem{layer}", k)).then_inc(S.m_evac_hi, 1)

            def mem_keys(layer):
                def body(i):
                    for j in range(2):
                        c = BLOCK0[f"mem{layer}"] + 2 * j
                        head = 2 * i + j + MEM_HEADS * layer
                        upper(i, c + 2)
                        act.wait_ge(S.acc_free, 4 * i + TILE0[f"mem{layer}"] + 2 * j + 1)
                        if due(head):
                            act.wait_ge(S.mk_ss, head)
                        a(w(KS)[:, 0:MEM_LEN], w(KR)[:, 0:MEM_LEN], ACT.Square).then_inc(S.mk_sq, 1)
                        upper(i, c + 3)
                        act.wait_ge(S.mk_ss, head + 1)
                        if due(head):
                            act.wait_ge(S.mk_done, head)
                        a(w(KRS)[:, 0:MEM_LEN], psum(D[4], MEM_LEN), ACT.Ln, scale=1.0 / P, bias=col("eps")).then_inc(S.mk_ln, 1)
                        act.wait_ge(S.mk_ln, head + 1)
                        a(w(KRS)[:, 0:MEM_LEN], w(KRS)[:, 0:MEM_LEN], ACT.Exp, scale=-0.5).then_inc(S.mk_rstd, 1)
                turns(act, MEM_HEADS // 2, body)

            mem_keys(0)
            act.wait_ge(S.x_loaded, 16)
            act.wait_ge(S.m_tr, KT)
            for t in range(NT):
                if due(t - 1):
                    act.wait_ge(S.x_sq, t - 1)
                a(rows(8, t % 2), rows(0, t), ACT.Square, accum_out=st[:, 2 + t:3 + t]).then_inc(S.x_sq, 1)
            act.wait_ge(S.x_sq, NT)
            a(st[:, 8:12], st[:, 2:6], ACT.Ln, scale=1.0 / D_MODEL, bias=col("eps")).then_inc(S.x_ln, 1)
            act.wait_ge(S.x_ln, 1)
            a(st[:, 8:12], st[:, 8:12], ACT.Exp, scale=-0.5).then_inc(S.x_rstd, 1)
            act.wait_ge(S.x_rstd, 1)
            act.wait_ge(S.x_raw_tr, KT)
            for t in range(NT):
                a(rows(0, t), rows(0, t), ACT.Copy, scale=st[:, 8 + t:9 + t]).then_inc(S.x_scaled, 1)
            act.wait_ge(S.ba_loaded, 16)
            a(ba_w[:, 0, :], w(E0)[:, 0:KT * 16], ACT.Copy).then_inc(S.ba_hi, 1)
            mem_keys(1)
            for k in range(KT):
                act.wait_ge(S.x_tr, k + 1)
                a(act_hi[:, k, :], psum(D[k % 4]), ACT.Copy, scale=col("a_norm", k)).then_inc(S.x_evac_hi, 1)

            act.wait_ge(S.ba_mm, 1)
            ba_ps = bank[:, D[0], 0:NT * 16].rearrange("p (t c) -> p c t", t=NT)
            a(dn(TMP1), ba_ps[:, 0:DN_HEADS, :], ACT.Exp, scale=-1.0).then_inc(S.ba_act, 1)
            a(st[:, 16:24], cols[:, COLS["a_log"]:COLS["a_log"] + DN_HEADS], ACT.Exp).then_inc(S.ba_act, 1)
            act.wait_ge(S.ba_dve, 2)
            a(dn(GL), dn(GL), ACT.Exp, scale=-1.0).then_inc(S.ba_act, 1)
            act.wait_ge(S.ba_act, 3)
            a(dn(GL), dn(GL), ACT.Ln, bias=sq_c[:, ONES, 0:1]).then_inc(S.ba_act, 1)
            act.wait_ge(S.ba_dve, 7)
            a(dn_s[:, GL, :], bank[:, D[2], 0:32], ACT.Exp).then_inc(S.ba_act, 1)
            a(dn(EDEC), dn(TMP1), ACT.Exp).then_inc(S.ba_act, 1)
            a(dn(TMP2), dn(GCUM), ACT.Exp).then_inc(S.ba_act, 1)

            def conv_tile(h, j):
                c = BLOCK0["dn"] + j
                upper(h, c + 2)
                m = 4 * h + j
                act.wait_ge(S.block_used, 4 * h + c + 1)
                if j < 3:
                    at_once(act)
                    nc.scalar.activation(w(CQ + j), psum(j % 2), ACT.Copy,
                                         scale=conv_w(h, j, 3)).then_inc(S.cv_tap, 1)
                    act.wait_ge(S.acc_free, TILE0["dn"] + m + 1)
                if j == 0:
                    if due(TILE0["dn"] + m):
                        act.wait_ge(S.acc_free, TILE0["dn"] + m)
                else:
                    if due(3 * h + j):
                        act.wait_ge(S.c_ready, 3 * h + j)
                a(w(EC), w(CQ + j) if j < 3 else psum(1), ACT.Exp, scale=-1.0).then_inc(S.cv_exp, 1)

            def delta(h, fill):
                act.wait_ge(S.c_ready, 3 * h + 1)
                if due(h):
                    act.wait_ge(S.o_done, h)
                a(w(E0), w(CQ), ACT.Square).then_inc(S.sq_done, 1)
                act.wait_ge(S.c_ready, 3 * h + 2)
                if due(h):
                    act.wait_ge(S.o_t1, h)
                a(w(E1), w(CK), ACT.Square).then_inc(S.sq_done, 1)
                for m, (e, ln_scale) in enumerate(((E0, "ln_q"), (E1, None))):
                    act.wait_ge(S.ss_done, 2 * h + m + 1)
                    a(w(e), psum(D[m]), ACT.Ln, bias=col("eps")).then_inc(S.rr_ln, 1)
                    act.wait_ge(S.rr_ln, 2 * h + m + 1)
                    kw = dict(bias=col(ln_scale)) if ln_scale else {}
                    a(w(e), w(e), ACT.Exp, scale=-0.5, **kw).then_inc(S.rr_done, 1)
                act.wait_ge(S.gb_done, 2 * h + 1)
                a(w(EG), psum(D[2]), ACT.Exp).then_inc(S.eg_done, 1)
                act.wait_ge(S.dm_pre, 2 * h + 2)
                a(w(DD), w(DD), ACT.Exp).then_inc(S.dm_done, 1)
                fill(0)
                fill(1)
                fill(2)
                act.wait_ge(S.nw_mm, h + 1)
                a(w(MM), psum(D[2]), ACT.Copy).then_inc(S.nw_done, 1)
                for t in range(NT):
                    act.wait_ge(S.v_mm, NT * h + t + 1)
                    act.wait_ge(S.qn_done, h + 1)
                    a(tt(E0, t), bank[:, D[3], 0:P], ACT.Copy).then_inc(S.v_done, 1)
                act.wait_ge(S.o_done, h + 1)
                a(w(E1), psum(D[5]), ACT.Square).then_inc(S.osq, 1)
                fill(3)
                act.wait_ge(S.oss, h + 1)
                a(w(E1), psum(D[2]), ACT.Ln, scale=1.0 / P, bias=col("eps")).then_inc(S.o_ln, 1)
                act.wait_ge(S.o_ln, h + 1)
                a(w(E1), w(E1), ACT.Exp, scale=-0.5).then_inc(S.o_rstd, 1)
                at_once(act)
                act.wait_ge(S.o_t2, h + 1)
                a(act_hi[:, KT + h, :], w(DD), ACT.Copy).then_inc(S.o_hi, 1)

            for j in range(4):
                conv_tile(0, j)
            turns(act, DN_HEADS - 1, lambda h: delta(h, lambda j: conv_tile(h + 1, j)))
            delta(DN_HEADS - 1, lambda j: None)

            def mem_attention(layer):
                c = BLOCK0[f"mq{layer}"]
                upper(0, c + 2)
                for j in range(MEM_HEADS):
                    u = layer * MEM_HEADS + j
                    act.wait_ge(S.acc_free, TILE0[f"mq{layer}"] + j + 1)
                    a(w(1), w(0), ACT.Square).then_inc(S.mq_sq, 1)
                    act.wait_ge(S.mq_ss, u + 1)
                    if due(u):
                        act.wait_ge(S.mq_n, u)
                    a(w(2), psum(D[0]), ACT.Ln, scale=1.0 / P, bias=col("eps")).then_inc(S.mq_ln, 1)
                    act.wait_ge(S.mq_ln, u + 1)
                    a(w(2), w(2), ACT.Exp, scale=-0.5, bias=col("ln_q")).then_inc(S.mq_rstd, 1)
                    if j + 1 < MEM_HEADS:
                        upper(0, c + j + 3)
                    act.wait_ge(S.mq_max, 2 * u + 2)
                    if due(u):
                        act.wait_ge(S.mq_tr, u)
                    if due(u):
                        act.wait_ge(S.mq_p, u)
                    for t in range(NT):
                        a(mq_p_of(t), bank[:, D[2] + t // 2, (t % 2) * MEM_LEN:(t % 2 + 1) * MEM_LEN], ACT.Exp, bias=st[:, 28 + t:29 + t], accum_out=st[:, 32 + t:33 + t]).then_inc(S.mq_exp, 1)
                    act.wait_ge(S.mq_tr, u + 1)
                    a(ws[:, 6:8, :], bank[:, D[4]:D[4] + 2, :], ACT.Copy).then_inc(S.mq_pt, 1)
                    act.wait_ge(S.mq_o, u + 1)
                    a(act_hi[:, cat_tile(layer, KT + j), :], psum(D[1]), ACT.Copy).then_inc(S.mq_hi, 1)

            mem_attention(0)

            def residual(name, gain, r, last):
                def body(i):
                    for j in range(2):
                        k = 2 * i + j
                        upper(i, BLOCK0[name] + 2 * j + 2)
                        upper(i, BLOCK0[name] + 2 * j + 3)
                        if last:
                            continue
                        act.wait_ge(S.acc_free, TILE0[name] + k + 1)
                        q = KT * r + k
                        if due(q - 1):
                            act.wait_ge(S.r_acc, q - 1)
                        a(w(13 + j), xT[:, k, :], ACT.Square).then_inc(S.r_sq, 1)
                        at_once(act)
                        nc.scalar.activation(act_hi[:, H_NEXT[name] + k, :], xT[:, k, :], ACT.Copy,
                                             scale=gain(k)).then_inc(S.r_hi, 1)
                turns(act, KT // 2, body)

            def rstd(r):
                act.wait_ge(S.r_ss, r + 1)
                a(w(R_T), psum(D[0]), ACT.Ln, scale=1.0 / D_MODEL, bias=col("eps")).then_inc(S.r_ln, 1)
                act.wait_ge(S.r_ln, r + 1)
                a(w(R_T), w(R_T), ACT.Exp, scale=-0.5).then_inc(S.r_done, 1)

            def ffn(layer):
                for half in range(2):
                    c = BLOCK0[f"up{layer}{half}"]

                    def pair(it, j):
                        upper(it, c + 2 * j + 2)
                        upper(it, c + 2 * j + 3)
                        f = HALF * (2 * layer + half) + 2 * it + j
                        act.wait_ge(S.acc_free, 4 * it + TILE0[f"up{layer}{half}"] + 2 * j + 1)
                        if due(f - 1):
                            act.wait_ge(S.f_hid, f - 1)
                        a(w(2 + j % 2), w(j % 2), ACT.Silu).then_inc(S.f_silu, 1)
                        act.wait_ge(S.f_hid, f + 1)
                        if due(f - 1):
                            act.wait_ge(S.f_lo, f - 1)
                        at_once(act)
                        a(act_hi[:, hid_tile(layer, it, j), :], w(6 + j % 2), ACT.Copy).then_inc(S.f_hi, 1)

                    def body(it):
                        pair(it, 0)
                        pair(it, 1)
                    if half == 0:
                        rstd(2 * layer)
                    turns(act, 4, body)
                    for j in range(8, HALF):
                        pair(0, j)
                    nxt = None if half == 0 or layer == 1 else (lambda k: col_k("kv_norm", k))
                    residual(f"down{layer}{half}", nxt, 1, nxt is None)

            residual("out0", lambda k: col_k("ffn0", k), 0, False)
            ffn(0)

            upper(0, BLOCK0["kv"] + 2)
            upper(0, BLOCK0["kv"] + 3)
            rstd(1)
            act.wait_ge(S.acc_free, TILE0["kv"] + 1)
            a(w(3), w(2), ACT.Square).then_inc(S.kv_sq, 1)
            act.wait_ge(S.kv_ss, 2)
            a(w(4), psum(D[0]), ACT.Ln, scale=1.0 / SW_DIM, bias=col("eps")).then_inc(S.kv_ln, 1)
            act.wait_ge(S.kv_ln, 1)
            a(w(4), w(4), ACT.Exp, scale=-0.5).then_inc(S.kv_rstd, 1)
            for k in range(KT):
                if k == 2:
                    act.wait_ge(S.kv_n, 1)
                    for g in range(SW_KV):
                        other = slice(SW_DIM * (1 - g), SW_DIM * (2 - g))
                        act.dma_start(kwin[other, g, SW_DIM:], ws[SW_DIM * g:SW_DIM * (g + 1), KN_T, :]
                                      ).then_inc(S.kv_dup, 16)
                act.wait_ge(S.b_h, 2 * k + 2)
                a(act_hi[:, KT + k, :], w(6 + k % 2), ACT.Copy).then_inc(S.b_hi, 1)

            for u in range(SW_HEADS // QPB):
                c = BLOCK0["swq"] + u
                upper(0, c + 2)
                act.wait_ge(S.block_used, c + 1)
                if due(u):
                    act.wait_ge(S.sw_ss, u)
                a(w(1), psum(u % 2), ACT.Square).then_inc(S.sw_sq, 1)
                act.wait_ge(S.sw_ss, u + 1)
                if due(TILE0["swq"] + u):
                    act.wait_ge(S.acc_free, TILE0["swq"] + u)
                a(w(2), psum(D[4]), ACT.Ln, scale=1.0 / SW_DIM, bias=col("eps")).then_inc(S.sw_ln, 1)
                act.wait_ge(S.sw_ln, u + 1)
                a(w(2), w(2), ACT.Exp, scale=-0.5, bias=col("ln_s")).then_inc(S.sw_rstd, 1)
                for e in range(QPB):
                    n = 2 * u + e
                    act.wait_ge(S.sw_nm, n + 1)
                    for t in range(NT):
                        a(swp(e)[:, t, SW_DIM:], swp(e)[:, t, SW_DIM:], ACT.Exp,
                          bias=st[:, 36 + 4 * e + t:37 + 4 * e + t], accum_out=st[:, 44 + 4 * e + t:45 + 4 * e + t]).then_inc(S.sw_exp, 1)
                    a(st[:, 52 + 4 * e:56 + 4 * e], st[:, 36 + 4 * e:40 + 4 * e], ACT.Exp,
                      bias=col("sinks", n)).then_inc(S.sw_exp, 1)
                for e in range(QPB):
                    n = 2 * u + e
                    act.wait_ge(S.sw_tr, n + 1)
                    if due(u):
                        act.wait_ge(S.sw_o, u)
                    a(w(PT_OWN[e]), psum(D[4] if e == 0 else D[0]), ACT.Copy).then_inc(S.sw_pt, 1)
                act.wait_ge(S.sw_o, u + 1)
                a(act_hi[:, u, :], psum(D[2]), ACT.Copy).then_inc(S.sw_o_hi, 1)

            mem_attention(1)
            residual("out1", lambda k: col_k("ffn1", k), 2, False)
            ffn(1)

        @block.vector
        def _(dve):
            V = nc.vector

            def mul(out_, x_, y_):
                return V.tensor_tensor(out_, x_, y_, ALU.mult)

            def sub(out_, x_, y_):
                return V.tensor_tensor(out_, x_, y_, ALU.subtract)

            def stt(out_, x_, scalar, y_, op0, op1):
                return V.scalar_tensor_tensor(out=out_, in0=x_, scalar=scalar, in1=y_, op0=op0, op1=op1)

            def cp(out_, x_):
                return V.tensor_copy(out_, x_)

            def hi(tile_):
                return act_hi[:, tile_, :].bitcast(F32)

            dve.wait_ge(S.consts_loaded, 16)
            dve.wait_ge(S.cols_loaded, 16)
            for k in range(KT):
                dve.wait_ge(S.m_evac_hi, 2 * k + 2)
                for layer in range(2):
                    own = slice(MEM_LEN * layer, MEM_LEN * (layer + 1))
                    stt(act_lo[:, KT + k, own], psum(D[k % 4], MEM_LEN), col(f"mem{layer}", k), hi(KT + k)[:, own],
                        ALU.mult, ALU.subtract).then_inc(S.m_evac_lo, 1)

            def mem_kv(layer):
                def body(i):
                    for j in range(2):
                        c, n = BLOCK0[f"mem{layer}"] + 2 * j, 4 * i + TILE0[f"mem{layer}"] + 2 * j
                        head = 2 * i + j + MEM_HEADS * layer
                        dve.wait_ge(S.block_used, 4 * i + c + 1)
                        if due(head):
                            dve.wait_ge(S.mk_sq, head)
                        if due(head):
                            dve.wait_ge(S.mk_done, head)
                        cp(w(KR)[:, 0:MEM_LEN], psum(0, MEM_LEN)).then_inc(S.acc_free, 1)
                        dve.wait_ge(S.block_used, 4 * i + c + 2)
                        cp(vmem[:, head, :], psum(1, MT_ * P)).then_inc(S.acc_free, 1)
                        dve.wait_ge(S.mk_rstd, head + 1)
                        dve.wait_ge(S.acc_free, n + 1)
                        stt(kmem[:, head, :], w(KR)[:, 0:MEM_LEN], col(f"mk{layer}"), w(KRS)[:, 0:MEM_LEN],
                            ALU.mult, ALU.mult).then_inc(S.mk_done, 1)
                turns(dve, MEM_HEADS // 2, body)

            mem_kv(0)
            for k in range(KT):
                dve.wait_ge(S.x_raw_tr, k + 1)
                cp(xT[:, k, :], psum(D[k % 4])).then_inc(S.x_raw_copied, 1)
            dve.wait_ge(S.ba_hi, 1)
            sub(ba_w[:, 1, :], w(E0)[:, 0:KT * 16], ba_w[:, 0, :].bitcast(F32)).then_inc(S.ba_split, 1)
            mem_kv(1)
            for k in range(KT):
                dve.wait_ge(S.x_evac_hi, k + 1)
                stt(act_lo[:, k, :], psum(D[k % 4]), col("a_norm", k), hi(k), ALU.mult, ALU.subtract).then_inc(S.x_evac_lo, 1)

            def over_t(name):
                return cols[:, COLS[name]:COLS[name] + DN_HEADS].unsqueeze(2).to_broadcast([P, DN_HEADS, NT])
            ba_ps = bank[:, D[0], 0:NT * 16].rearrange("p (t c) -> p c t", t=NT)
            dve.wait_ge(S.ba_act, 1)
            V.tensor_tensor(dn(TMP2), ba_ps[:, DN_HEADS:, :], over_t("dt"), ALU.add).then_inc(S.ba_dve, 1)
            dve.wait_ge(S.ba_dve, 1)
            stt(dn(GL), dn(TMP2), -1.0, dn(TMP2), ALU.mult, ALU.max).then_inc(S.ba_dve, 1)
            V.tensor_scalar(dn(TMP1), dn(TMP1), 1.0, None, ALU.add).then_inc(S.ba_dve, 1)
            dve.wait_ge(S.ba_dve, 3)
            V.reciprocal(dn(BETA), dn(TMP1)).then_inc(S.ba_dve, 1)
            dve.wait_ge(S.ba_act, 4)
            stt(dn(TMP2), dn(TMP2), 0.0, dn(GL), ALU.max, ALU.add).then_inc(S.ba_dve, 1)
            dve.wait_ge(S.ba_dve, 5)
            stt(dn(GG), dn(TMP2), -1.0, st[:, 16:24].unsqueeze(2).to_broadcast([P, DN_HEADS, NT]),
                ALU.mult, ALU.mult).then_inc(S.ba_g, 1)
            dve.wait_ge(S.ba_cum, 1)
            cp(dn_s[:, GCUM, :], bank[:, D[1], 0:32]).then_inc(S.ba_dve, 1)
            dve.wait_ge(S.ba_dve, 6)
            sub(dn_s[:, TMP1, :], bank[:, D[2], 0:32], dn_s[:, GCUM, :]).then_inc(S.ba_dve, 1)
            dve.wait_ge(S.ba_act, 7)
            stt(dn(NBEG), dn(BETA), -1.0, dn(TMP2), ALU.mult, ALU.mult).then_inc(S.ba_dve, 1)
            dve.wait_ge(S.ba_dve, 8)

            def conv_tile(h, j):
                m = 4 * h + j
                if j < 3:
                    dve.wait_ge(S.cv_tap, 3 * h + j + 1)
                    for d in range(1, 4):
                        taps = 6 * h + 2 * j + d - 1
                        if d > 1:
                            if due(taps):
                                dve.wait_ge(S.cv_conv, taps)
                        stt(w(CQ + j)[:, d:], psum(j % 2)[:, 0:SEQ - d], conv_w(h, j, 3 - d), w(CQ + j)[:, d:],
                            ALU.mult, ALU.add).then_inc(S.cv_conv if d < 3 else S.acc_free, 1)
                dve.wait_ge(S.cv_exp, m + 1)
                V.tensor_scalar(w(EC), w(EC), 1.0, None, ALU.add).then_inc(S.cv_one, 1)
                dve.wait_ge(S.cv_one, 2 * m + 1)
                V.reciprocal(w(EC), w(EC)).then_inc(S.cv_one, 1)
                dve.wait_ge(S.cv_one, 2 * m + 2)
                if j < 3:
                    mul(w(CQ + j), w(CQ + j), w(EC)).then_inc(S.c_ready, 1)
                else:
                    mul(w(SZ), psum(1), w(EC)).then_inc(S.acc_free, 1)

            def delta(h, fill):
                if due(h):
                    dve.wait_ge(S.nw_mm, h)
                mul(w4(KBG), over_tiles(TRIU), dn_bcast(GG, h)).then_inc(S.ug_done, 1)
                if due(h):
                    dve.wait_ge(S.o_done, h)
                mul(w4(KDEC), over_tiles(IDENT), dn_bcast(BETA, h)).then_inc(S.ug_done, 1)
                dve.wait_ge(S.rr_done, 2 * h + 1)
                mul(w(QN), w(CQ), w(E0)).then_inc(S.qn_done, 1)
                dve.wait_ge(S.rr_done, 2 * h + 2)
                mul(w(KN), w(CK), w(E1)).then_inc(S.kn_done, 1)
                dve.wait_ge(S.gb_done, 2 * h + 2)
                dve.wait_ge(S.kn_done, h + 1)
                mul(w(PM), w(KN), psum(D[3])).then_inc(S.kb_done, 1)
                dve.wait_ge(S.eg_done, h + 1)
                if due(h):
                    dve.wait_ge(S.o_lo, h)
                V.tensor_tensor(w4(DD), psum4(D[2]), over_tiles(NEG_LOWER), ALU.add).then_inc(S.dm_pre, 1)
                dve.wait_ge(S.dm_pre, 2 * h + 1)
                sub(w4(DD), w4(DD), dn_bcast(GCUM, h)).then_inc(S.dm_pre, 1)
                dve.wait_ge(S.qn_done, h + 1)
                mul(w(EG), w(EG), w(QN)).then_inc(S.qd_done, 1)
                dve.wait_ge(S.vtr_done, h + 1)
                mul(w4(VB), psum4(D[4]), dn_bcast(BETA, h)).then_inc(S.vb_done, 1)
                dve.wait_ge(S.ktr_done, h + 1)
                mul(w4(KBG), psum4(D[5]), dn_bcast(NBEG, h)).then_inc(S.kbg_done, 1)
                mul(w4(KDEC), psum4(D[5]), dn_bcast(EDEC, h)).then_inc(S.kdec_done, 1)
                fill(0)
                dve.wait_ge(S.dm_done, h + 1)
                dve.wait_ge(S.gg_done, 2 * h + 1)
                mul(w(MM), psum(D[1]), w(DD)).then_inc(S.mt_done, 1)
                dve.wait_ge(S.gg_done, 2 * h + 2)
                mul(w(AT), psum(D[0]), w(DD)).then_inc(S.at_done, 1)
                dve.wait_ge(S.mt_done, h + 1)
                mul(w4(ZZ), w4(MM), over_tiles(LEVEL0)).then_inc(S.z_pre, 1)
                dve.wait_ge(S.z_pre, h + 1)
                sub(w4(ZZ), over_tiles(IDENT), w4(ZZ)).then_inc(S.z_done, 1)
                fill(1)
                dve.wait_ge(S.t_tr, h + 1)
                cp(w(TT), psum(D[2])).then_inc(S.t_done, 1)
                for k in range(1, LEVELS):
                    n = 6 * h + k
                    if due(n):
                        dve.wait_ge(S.p_mm, n)
                    mul(w4(PM), psum4(D[3]), over_tiles(LEVEL0 + k)).then_inc(S.p_done, 1)
                    if k == 3:
                        fill(2)
                    if due(n):
                        dve.wait_ge(S.tz_mm, n)
                    if k < LEVELS - 1:
                        sub(ws[:, TT:ZZ + 1, :], ws[:, TT:ZZ + 1, :], bank[:, D[4]:D[4] + 2, :]).then_inc(S.tz_done, 1)
                    else:
                        sub(w(ZZ), w(ZZ), psum(D[5])).then_inc(S.tz_done, 1)
                for t in range(NT - 1):
                    dve.wait_ge(S.s_mm, 3 * h + t + 1)
                    if t == 0:
                        cp(state[:], bank[:, D[4], 0:P]).then_inc(S.s_done, 1)
                    else:
                        if due(3 * h + t):
                            dve.wait_ge(S.s_done, 3 * h + t)
                        stt(state[:], state[:], dn(GL)[:, h, t:t + 1], bank[:, D[4], 0:P], ALU.mult, ALU.add).then_inc(S.s_done, 1)
                dve.wait_ge(S.o_rstd, h + 1)
                mul(w(PM), psum(D[5]), w(E1)).then_inc(S.o_t1, 1)
                dve.wait_ge(S.o_t1, h + 1)
                stt(w(DD), w(PM), col("out_norm"), w(SZ), ALU.mult, ALU.mult).then_inc(S.o_t2, 1)
                dve.wait_ge(S.o_hi, h + 1)
                sub(act_lo[:, KT + h, :], w(DD), hi(KT + h)).then_inc(S.o_lo, 1)
                fill(3)

            for j in range(4):
                conv_tile(0, j)
            turns(dve, DN_HEADS - 1, lambda h: delta(h, lambda j: conv_tile(h + 1, j)))
            delta(DN_HEADS - 1, lambda j: None)

            def mem_attention(layer):
                for j in range(MEM_HEADS):
                    u = layer * MEM_HEADS + j
                    dve.wait_ge(S.block_used, BLOCK0[f"mq{layer}"] + j + 1)
                    if due(u):
                        dve.wait_ge(S.mq_sq, u)
                    cp(w(0), psum(j % 2)).then_inc(S.acc_free, 1)
                    dve.wait_ge(S.mq_rstd, u + 1)
                    if due(u):
                        dve.wait_ge(S.mq_sc, u)
                    dve.wait_ge(S.acc_free, TILE0[f"mq{layer}"] + j + 1)
                    stt(w(3), w(0), col(f"mq{layer}"), w(2), ALU.mult, ALU.mult).then_inc(S.mq_n, 1)
                    dve.wait_ge(S.mq_sc, u + 1)
                    if due(2 * u):
                        dve.wait_ge(S.mq_max, 2 * u)
                    V.tensor_reduce(st[:, 24:28], bank[:, D[2]:D[2] + 2, :].rearrange("p a (b c) -> p (a b) c", b=2),
                                    AX.X, ALU.max).then_inc(S.mq_max, 1)
                    dve.wait_ge(S.mq_max, 2 * u + 1)
                    V.tensor_scalar(st[:, 28:32], st[:, 24:28], -1.0, None, ALU.mult).then_inc(S.mq_max, 1)
                    if due(NT * (u + 1)):
                        dve.wait_ge(S.mq_exp, NT * (u + 1))
                    V.reciprocal(st[:, 32:36], st[:, 32:36]).then_inc(S.mq_rcp, 1)
                    dve.wait_ge(S.mq_rcp, u + 1)
                    p4 = ws[:, 4:6, :].rearrange("p a (b c) -> p (a b) c", b=2)
                    mul(p4, p4, st[:, 32:36].unsqueeze(2).to_broadcast([P, NT, MEM_LEN])).then_inc(S.mq_p, 1)
                    dve.wait_ge(S.mq_hi, u + 1)
                    tile_ = cat_tile(layer, KT + j)
                    sub(act_lo[:, tile_, :], psum(D[1]), hi(tile_)).then_inc(S.mq_lo, 1)

            mem_attention(0)

            def residual(name, gain, r, last):
                def body(i):
                    for j in range(2):
                        k = 2 * i + j
                        dve.wait_ge(S.block_used, 4 * i + BLOCK0[name] + 2 * j + 2)
                        V.tensor_tensor(xT[:, k, :], xT[:, k, :], psum(j), ALU.add
                                        ).then_inc(S.acc_free, 1)
                        if last:
                            continue
                        q = KT * r + k
                        dve.wait_ge(S.r_sq, q + 1)
                        if due(q):
                            dve.wait_ge(S.r_acc, q)
                        if isinstance(k, int) and k == 0:
                            if due(r):
                                dve.wait_ge(S.r_ss, r)
                            cp(w(SQ_T), w(13 + j)).then_inc(S.r_acc, 1)
                        else:
                            V.tensor_tensor(w(SQ_T), w(SQ_T), w(13 + j), ALU.add).then_inc(S.r_acc, 1)
                        dve.wait_ge(S.r_hi, q + 1)
                        stt(act_lo[:, H_NEXT[name] + k, :], xT[:, k, :], gain(k), hi(H_NEXT[name] + k),
                            ALU.mult, ALU.subtract).then_inc(S.r_lo, 1)
                turns(dve, KT // 2, body)

            def ffn(layer):
                for half in range(2):
                    c = BLOCK0[f"up{layer}{half}"]

                    def pair(it, j):
                        f = HALF * (2 * layer + half) + 2 * it + j
                        dve.wait_ge(S.block_used, 4 * it + c + 2 * j + 1)
                        dve.wait_ge(S.r_done, 2 * layer + 1)
                        if due(f - 1):
                            dve.wait_ge(S.f_silu, f - 1)
                        mul(w(j % 2), psum(0), w(R_T)).then_inc(S.acc_free, 1)
                        dve.wait_ge(S.block_used, 4 * it + c + 2 * j + 2)
                        mul(w(4 + j % 2), psum(1), w(R_T)).then_inc(S.acc_free, 1)
                        dve.wait_ge(S.f_silu, f + 1)
                        dve.wait_ge(S.acc_free, 4 * it + TILE0[f"up{layer}{half}"] + 2 * j + 2)
                        if due(f - 1):
                            dve.wait_ge(S.f_lo, f - 1)
                        mul(w(6 + j % 2), w(4 + j % 2), w(2 + j % 2)).then_inc(S.f_hid, 1)
                        dve.wait_ge(S.f_hi, f + 1)
                        tile_ = hid_tile(layer, it, j)
                        sub(act_lo[:, tile_, :], w(6 + j % 2), hi(tile_)).then_inc(S.f_lo, 1)

                    def body(it):
                        pair(it, 0)
                        pair(it, 1)
                    turns(dve, 4, body)
                    for j in range(8, HALF):
                        pair(0, j)
                    nxt = None if half == 0 or layer == 1 else (lambda k: col_k("kv_norm", k))
                    residual(f"down{layer}{half}", nxt, 1, nxt is None)

            residual("out0", lambda k: col_k("ffn0", k), 0, False)
            ffn(0)

            V.memset(kwin[:, :, 0:SW_DIM], 0.0).then_inc(S.kv_done, 1)
            dve.wait_ge(S.r_done, 2)
            dve.wait_ge(S.block_used, BLOCK0["kv"] + 1)
            mul(w(2), psum(0), w(R_T)).then_inc(S.acc_free, 1)
            dve.wait_ge(S.kv_ss, 1)
            cp(st[:, 12:16], bank[:, D[1], 0:NT]).then_inc(S.kv_r, 1)
            dve.wait_ge(S.block_used, BLOCK0["kv"] + 2)
            dve.wait_ge(S.kv_r, 1)
            mul(w4(V_T), psum4(1), st[:, 12:16].unsqueeze(2).to_broadcast([P, NT, P])).then_inc(S.acc_free, 1)
            dve.wait_ge(S.kv_rstd, 1)
            dve.wait_ge(S.acc_free, TILE0["kv"] + 1)
            stt(w(KN_T), w(2), col("k_norm"), w(4), ALU.mult, ALU.mult).then_inc(S.kv_n, 1)
            dve.wait_ge(S.kv_n, 1)
            for g in range(SW_KV):
                rows_ = slice(SW_DIM * g, SW_DIM * (g + 1))
                cp(kwin[rows_, g, SW_DIM:], ws[rows_, KN_T, :]).then_inc(S.kv_done, 1)
            for k in range(KT):
                if due(k - 1):
                    dve.wait_ge(S.b_lo, k - 1)
                mul(w(6 + k % 2), xT[:, k, :], w(R_T)).then_inc(S.b_h, 1)
                dve.wait_ge(S.b_h, 2 * k + 1)
                V.tensor_scalar(w(6 + k % 2), w(6 + k % 2), col("b_norm", k), None, ALU.mult).then_inc(S.b_h, 1)
                dve.wait_ge(S.b_hi, k + 1)
                sub(act_lo[:, KT + k, :], w(6 + k % 2), hi(KT + k)).then_inc(S.b_lo, 1)

            dve.wait_ge(S.dist_loaded, 16)
            dve.wait_ge(S.kv_dup, 32)
            dve.wait_ge(S.b_lo, KT)
            for e in range(QPB):
                V.memset(swp(e)[:, :, 0:SW_DIM], 0.0).then_inc(S.kv_done, 1)
                V.memset(ws[:, PT_PREV[e], 0:P], 0.0).then_inc(S.kv_done, 1)
            for u in range(SW_HEADS // QPB):
                dve.wait_ge(S.sw_rstd, u + 1)
                if due(2 * u):
                    dve.wait_ge(S.sw_sc, 2 * u)
                stt(w(3), psum(u % 2), col("q_norm"), w(2), ALU.mult, ALU.mult).then_inc(S.acc_free, 1)
                for e in range(QPB):
                    n = 2 * u + e
                    dve.wait_ge(S.sw_sc, n + 1)
                    if due(n - 1):
                        dve.wait_ge(S.sw_tr, n - 1)
                    scores = bank[:, D[0] + 2 * e:D[0] + 2 * e + 2, :].rearrange("p a (b c) -> p (a b) c", b=2)
                    stt(swp(e)[:, :, SW_DIM:], distance, col("nslope", n), scores[:, :, 0:WIN],
                        ALU.mult, ALU.add).then_inc(S.sw_s, 1)
                    dve.wait_ge(S.sw_s, n + 1)
                    V.tensor_reduce(st[:, 24 + 4 * e:28 + 4 * e], swp(e)[:, :, SW_DIM:], AX.X, ALU.max
                                    ).then_inc(S.sw_mx, 1)
                    dve.wait_ge(S.sw_mx, n + 1)
                    if due(2 * n - 2):
                        dve.wait_ge(S.sw_den, 2 * n - 2)
                    V.tensor_scalar(st[:, 36 + 4 * e:40 + 4 * e], st[:, 24 + 4 * e:28 + 4 * e], col("sinks", n), -1.0,
                                    ALU.max, ALU.mult).then_inc(S.sw_nm, 1)
                for e in range(QPB):
                    n = 2 * u + e
                    den = st[:, 44 + 4 * e:48 + 4 * e]
                    if due((NT + 1) * (n + 1)):
                        dve.wait_ge(S.sw_exp, (NT + 1) * (n + 1))
                    V.tensor_tensor(den, den, st[:, 52 + 4 * e:56 + 4 * e], ALU.add).then_inc(S.sw_den, 1)
                    dve.wait_ge(S.sw_den, 2 * n + 1)
                    V.reciprocal(den, den).then_inc(S.sw_den, 1)
                    dve.wait_ge(S.sw_den, 2 * n + 2)
                    mul(swp(e)[:, :, SW_DIM:], swp(e)[:, :, SW_DIM:], den.unsqueeze(2).to_broadcast([P, NT, WIN])).then_inc(S.sw_p, 1)
                for e in range(QPB):
                    n = 2 * u + e
                    dve.wait_ge(S.sw_tr, n + 1)
                    if due(u):
                        dve.wait_ge(S.sw_o, u)
                    cp(ws[:, PT_PREV[e], P:], bank[:, D[5] if e == 0 else D[1], P:]).then_inc(S.sw_ptp, 1)
                dve.wait_ge(S.sw_o_hi, u + 1)
                sub(act_lo[:, u, :], psum(D[2]), hi(u)).then_inc(S.sw_o_lo, 1)

            mem_attention(1)
            residual("out1", lambda k: col_k("ffn1", k), 2, False)
            ffn(1)
            for t in range(NT):
                dve.wait_ge(S.fin_tr, t + 1)
                cp(ws[:, 2 * t:2 * t + 2, :], bank[:, D[0]:D[0] + 2, :]).then_inc(S.fin_done, 1)


def kernel(x, mem, a_norm, a_w_in, a_conv, a_A_log, a_dt_bias, a_out_norm, a_w_out, kv_norm, w_kv, k_norm, b_norm,
           b_w_in, b_q_norm, b_sinks, b_w_out, mem_norm, w_mem_kv, mem_q_norm, mem_k_norm, ffn_norm, w_gate_up, w_down):
    import concourse.bacc as bacc
    from concourse.bass_utils import run_bass_kernel_spmd

    f = np.asarray

    def tiles(m):
        m = f(m)
        k, n = m.shape
        return m.reshape(k // P, P, n // P, P).transpose(2, 1, 0, 3).reshape(n // P, P, k)

    w_in, b_in = f(a_w_in)[0], f(b_w_in)[0]
    heads = w_in[:, :4 * DN_W]
    qkvz = tiles(heads).reshape(4, DN_HEADS, P, D_MODEL).transpose(1, 0, 2, 3).reshape(4 * DN_HEADS, P, D_MODEL)
    ba = w_in[:, 4 * DN_W:4 * DN_W + 2 * DN_HEADS].reshape(KT, P, 16).transpose(1, 0, 2).reshape(P, KT * 16)
    mem_kv = [tiles(f(w_mem_kv)[i]).reshape(2, MEM_HEADS, P, D_MODEL).transpose(1, 0, 2, 3).reshape(-1, P, D_MODEL)
              for i in range(2)]
    ups = [tiles(f(w_gate_up)[i]).reshape(2, 2, HALF, P, D_MODEL).transpose(1, 2, 0, 3, 4).reshape(-1, P, D_MODEL)
           for i in range(2)]
    stream = np.concatenate([mem_kv[0], mem_kv[1], qkvz, tiles(w_in[:, 4 * DN_W + 2 * DN_HEADS:]), ups[0],
                             tiles(w_kv), tiles(b_in), ups[1]])
    outs = np.stack([tiles(f(a_w_out)[0]), tiles(f(b_w_out)[0])])
    downs = np.concatenate([np.stack([tiles(m) for m in f(w_down)[i].reshape(2, HALF * P, D_MODEL)])
                            for i in range(2)])

    def per_tile(v):
        return f(v).reshape(-1, P).T

    def everywhere(v):
        return np.broadcast_to(f(v).reshape(1, -1), (P, f(v).size))

    conv = f(a_conv)[0].reshape(4, 3, DN_HEADS, P).transpose(3, 2, 1, 0).reshape(P, -1)
    slopes = -np.exp2(-8.0 * np.arange(1, SW_HEADS + 1) / SW_HEADS).astype(np.float32)
    cols = np.concatenate(
        [per_tile(f(a_norm)[0]), per_tile(f(ffn_norm)[0]), per_tile(kv_norm), per_tile(f(b_norm)[0]),
         per_tile(f(ffn_norm)[1]), per_tile(f(mem_norm)[0]), per_tile(f(mem_norm)[1]), per_tile(f(a_out_norm)[0]),
         per_tile(f(mem_q_norm)[0]), per_tile(f(mem_q_norm)[1]), per_tile(f(mem_k_norm)[0]),
         per_tile(f(mem_k_norm)[1]), per_tile(np.concatenate([f(k_norm)] * 2)),
         per_tile(np.concatenate([f(b_q_norm)[0]] * 2)), conv, everywhere(a_A_log), everywhere(a_dt_bias),
         everywhere(b_sinks), everywhere(slopes),
         everywhere(np.array([EPS, -0.5 * math.log(P), -0.5 * math.log(SW_DIM)], np.float32))], axis=1)
    arrays = {
        "x_in": f(x)[0], "mem_in": f(mem)[0], "w_stream": stream, "w_out": outs, "w_down": downs, "w_ba": ba,
        "cols_in": cols, "squares_in": squares(), "dist_in": distances(),
    }
    arrays = {n: np.ascontiguousarray(a_) for n, a_ in arrays.items()}
    nc = bacc.Bacc("TRN2", target_bir_lowering=False, num_devices=1)
    args = [nc.dram_tensor(n, a_.shape, F32, kind="ExternalInput").ap() for n, a_ in arrays.items()]
    out = nc.dram_tensor("out", (SEQ, D_MODEL), F32, kind="ExternalOutput").ap()
    yoco_kernel(nc, *args, out)
    r = run_bass_kernel_spmd(nc, [arrays], core_ids=[0])
    return r.results[0]["out"].reshape(1, SEQ, D_MODEL)
```

```python
import math
from contextlib import ExitStack

import numpy as np

import concourse.bass as bass
from concourse import mybir

F32 = mybir.dt.float32
F32R = mybir.dt.float32r
ALU = mybir.AluOpType
ACT = mybir.ActivationFunctionType
AX = mybir.AxisListType

P = 128
D_MODEL = 1024
SEQ = 512
MEM_LEN = 256
DN_HEADS = 8
DN_W = DN_HEADS * P
MEM_HEADS = 4
MEM_W = MEM_HEADS * P
SW_HEADS = 16
SW_DIM = 64
SW_KV = 2
D_FF = -(-8 * D_MODEL // (3 * 256)) * 256
EPS = 1e-6

KT = D_MODEL // P
NT = SEQ // P
MT_ = MEM_LEN // P
CAT = (DN_W + MEM_W) // P
HALF = D_FF // P // 2
WIN = 3 * SW_DIM
LEVELS = 7
QPB = P // SW_DIM

_order = [("mem0", 2 * MEM_HEADS), ("mem1", 2 * MEM_HEADS), ("dn", 4 * DN_HEADS), ("mq0", MEM_HEADS),
          ("out0", 2 * KT), ("up00", 2 * HALF), ("down00", 2 * KT), ("up01", 2 * HALF), ("down01", 2 * KT),
          ("kv", 2), ("swq", SW_HEADS // QPB), ("mq1", MEM_HEADS), ("out1", 2 * KT),
          ("up10", 2 * HALF), ("down10", 2 * KT), ("up11", 2 * HALF), ("down11", 2 * KT)]
BLOCK0, TILE0 = {}, {}
_b = _n = 0
for _name, _count in _order:
    BLOCK0[_name], TILE0[_name] = _b, _n
    _b += _count
    _n += _count // 2 if _name.startswith(("out", "down")) else _count
N_BLOCKS, N_TILES = _b, _n
OUT_SUB = (CAT // 2, CAT // 2)
DOWN_SUB = ((HALF + 1) // 2, HALF // 2)
RING = 4


def subtiles(block):
    for name, count in _order:
        if BLOCK0[name] <= block < BLOCK0[name] + count:
            half = (block - BLOCK0[name]) % 2
            return OUT_SUB[half] if name.startswith("out") else DOWN_SUB[half] if name.startswith("down") else KT
    raise ValueError(block)


COLS = {}
_c = 0
for _name, _count in [("a_norm", KT), ("ffn0", KT), ("kv_norm", KT), ("b_norm", KT), ("ffn1", KT), ("mem0", KT),
                      ("mem1", KT), ("out_norm", 1), ("mq0", 1), ("mq1", 1), ("mk0", 1), ("mk1", 1), ("k_norm", 1),
                      ("q_norm", 1), ("conv", DN_HEADS * 3 * 4), ("a_log", DN_HEADS), ("dt", DN_HEADS),
                      ("sinks", SW_HEADS), ("nslope", SW_HEADS), ("eps", 1), ("ln_q", 1), ("ln_s", 1)]:
    COLS[_name] = _c
    _c += _count
N_COLS = _c

(IDENT, ONES, ONES64, TRIU, NEG_LOWER, LEVEL0) = range(6)
N_SQ = 6 + LEVELS - 1


def squares():
    r, c = np.arange(P)[:, None], np.arange(P)[None, :]
    out = np.zeros((P, N_SQ, P), np.float32)
    out[:, IDENT] = r == c
    out[:, ONES] = 1.0
    out[:, ONES64] = r // SW_DIM == c // SW_DIM
    out[:, TRIU] = r <= c
    out[:, NEG_LOWER] = np.where(r <= c, 0.0, -1e30)
    out[:, LEVEL0] = (c == r + 1) & (r % 2 == 0)
    for k in range(1, LEVELS):
        b = 2 ** k
        out[:, LEVEL0 + k] = (r // b % 2 == 1) & (c // b == r // b - 1)
    return out


def distances():
    i, j = np.arange(P)[:, None], np.arange(WIN)[None, :]
    d = np.abs(i + SW_DIM - j).astype(np.float32)
    d = np.where((j // SW_DIM >= i // SW_DIM) & (j // SW_DIM <= i // SW_DIM + 1), d, 1e30)
    out = np.repeat(d[:, None, :], NT, axis=1)
    out[:, 0, :SW_DIM] = 1e30
    return out.astype(np.float32)


KR, KS, KRS = 14, 18, 15
(CQ, CK, CV, SZ, QN, KN, TT, ZZ, AT, MM, PM, DD, EG, VB, KBG, KDEC, E0, E1, EC) = range(19)
WS = 19


def yoco_kernel(nc, x, mem, w_stream, w_out, w_down, w_ba, cols_in, squares_in, dist_in, out):
    with ExitStack() as ctx:
        def sb(name, shape, dt=F32):
            return ctx.enter_context(nc.sbuf_tensor(name, shape, dt))

        def sem(name):
            return ctx.enter_context(nc.semaphore(name))

        xT = sb("xT", [P, KT, SEQ])
        act_hi = sb("act_hi", [P, KT + CAT, SEQ], F32R)
        act_lo = sb("act_lo", [P, KT + CAT, SEQ], F32R)
        w_raw = sb("w_raw", [P, RING, KT * P])
        w_hi = sb("w_hi", [P, RING, KT * P], F32R)
        w_lo = sb("w_lo", [P, RING, KT * P], F32R)
        ws = sb("ws", [P, WS, SEQ])
        kmem = sb("kmem", [P, 2 * MEM_HEADS, MEM_LEN])
        vmem = sb("vmem", [P, 2 * MEM_HEADS, MT_ * P])
        sq_c = sb("sq_c", [P, N_SQ, P])
        cols = sb("cols", [P, N_COLS])
        dn_s = sb("dn_s", [P, 8, DN_HEADS * NT])
        state = sb("state", [P, P])
        st = sb("st", [P, 64])

        bank = ctx.enter_context(nc.psum_tensor("bank", [P, 8, 512], F32))

        class S:
            consts_loaded = sem("consts_loaded")
            cols_loaded = sem("cols_loaded")
            dist_loaded = sem("dist_loaded")
            x_loaded = sem("x_loaded")
            mem_loaded = sem("mem_loaded")
            ba_loaded = sem("ba_loaded")
            hi_done = sem("hi_done")
            lo_done = sem("lo_done")
            block_used = sem("block_used")
            acc_free = sem("acc_free")
            m_sq = sem("m_sq")
            m_ln = sem("m_ln")
            m_rstd = sem("m_rstd")
            m_scaled = sem("m_scaled")
            m_tr = sem("m_tr")
            m_evac_hi = sem("m_evac_hi")
            m_evac_lo = sem("m_evac_lo")
            x_sq = sem("x_sq")
            x_ln = sem("x_ln")
            x_rstd = sem("x_rstd")
            x_scaled = sem("x_scaled")
            x_raw_tr = sem("x_raw_tr")
            x_raw_copied = sem("x_raw_copied")
            x_tr = sem("x_tr")
            x_evac_hi = sem("x_evac_hi")
            x_evac_lo = sem("x_evac_lo")
            mk_sq = sem("mk_sq")
            mk_ss = sem("mk_ss")
            mk_ln = sem("mk_ln")
            mk_rstd = sem("mk_rstd")
            mk_done = sem("mk_done")
            ba_hi = sem("ba_hi")
            ba_split = sem("ba_split")
            ba_mm = sem("ba_mm")
            ba_dve = sem("ba_dve")
            ba_act = sem("ba_act")
            ba_g = sem("ba_g")
            ba_cum = sem("ba_cum")
            cv_tap = sem("cv_tap")
            cv_conv = sem("cv_conv")
            c_ready = sem("c_ready")
            sz_done = sem("sz_done")
            sq_done = sem("sq_done")
            ss_done = sem("ss_done")
            rr_ln = sem("rr_ln")
            rr_done = sem("rr_done")
            qn_done = sem("qn_done")
            kn_done = sem("kn_done")
            ug_done = sem("ug_done")
            gb_done = sem("gb_done")
            eg_done = sem("eg_done")
            dm_pre = sem("dm_pre")
            dm_done = sem("dm_done")
            kb_done = sem("kb_done")
            vtr_done = sem("vtr_done")
            ktr_done = sem("ktr_done")
            vb_done = sem("vb_done")
            kbg_done = sem("kbg_done")
            kdec_done = sem("kdec_done")
            qd_done = sem("qd_done")
            gg_done = sem("gg_done")
            at_done = sem("at_done")
            mt_done = sem("mt_done")
            z_pre = sem("z_pre")
            z_done = sem("z_done")
            t_tr = sem("t_tr")
            t_done = sem("t_done")
            p_mm = sem("p_mm")
            p_done = sem("p_done")
            tz_mm = sem("tz_mm")
            tz_done = sem("tz_done")
            nw_mm = sem("nw_mm")
            nw_done = sem("nw_done")
            v_mm = sem("v_mm")
            v_done = sem("v_done")
            s_mm = sem("s_mm")
            s_done = sem("s_done")
            o_done = sem("o_done")
            osq = sem("osq")
            oss = sem("oss")
            o_ln = sem("o_ln")
            o_rstd = sem("o_rstd")
            o_t1 = sem("o_t1")
            o_t2 = sem("o_t2")
            o_hi = sem("o_hi")
            o_lo = sem("o_lo")
            mq_sq = sem("mq_sq")
            mq_ss = sem("mq_ss")
            mq_ln = sem("mq_ln")
            mq_rstd = sem("mq_rstd")
            mq_n = sem("mq_n")
            mq_sc = sem("mq_sc")
            mq_max = sem("mq_max")
            mq_exp = sem("mq_exp")
            mq_rcp = sem("mq_rcp")
            mq_p = sem("mq_p")
            mq_tr = sem("mq_tr")
            mq_pt = sem("mq_pt")
            mq_o = sem("mq_o")
            mq_hi = sem("mq_hi")
            mq_lo = sem("mq_lo")
            r_hi = sem("r_hi")
            r_lo = sem("r_lo")
            r_sq = sem("r_sq")
            r_acc = sem("r_acc")
            r_ss = sem("r_ss")
            r_ln = sem("r_ln")
            r_done = sem("r_done")
            f_silu = sem("f_silu")
            f_hid = sem("f_hid")
            f_hi = sem("f_hi")
            f_lo = sem("f_lo")
            kv_sq = sem("kv_sq")
            kv_ss = sem("kv_ss")
            kv_ln = sem("kv_ln")
            kv_rstd = sem("kv_rstd")
            kv_n = sem("kv_n")
            kv_dup = sem("kv_dup")
            kv_done = sem("kv_done")
            kv_r = sem("kv_r")
            b_hi = sem("b_hi")
            b_lo = sem("b_lo")
            sw_sq = sem("sw_sq")
            sw_ss = sem("sw_ss")
            sw_ln = sem("sw_ln")
            sw_rstd = sem("sw_rstd")
            sw_q = sem("sw_q")
            sw_sc = sem("sw_sc")
            sw_s = sem("sw_s")
            sw_mx = sem("sw_mx")
            sw_nm = sem("sw_nm")
            sw_exp = sem("sw_exp")
            sw_den = sem("sw_den")
            sw_p = sem("sw_p")
            sw_tr = sem("sw_tr")
            sw_pt = sem("sw_pt")
            sw_ptp = sem("sw_ptp")
            sw_o = sem("sw_o")
            sw_o_hi = sem("sw_o_hi")
            sw_o_lo = sem("sw_o_lo")
            fin_tr = sem("fin_tr")
            fin_done = sem("fin_done")

        raw_loaded = [sem(f"raw_loaded{i}") for i in range(RING)]
        stored = sem("stored")

        block = ctx.enter_context(nc.Block())

        def due(n):
            return not isinstance(n, int) or n > 0

        def at_once(eng):
            eng.wait_ge(S.consts_loaded, 16)

        def turns(eng, n, body):
            body(0)
            if n > 3:
                with eng.Fori(1, n - 1) as i:
                    body(i)
            elif n == 3:
                body(1)
            if n > 1:
                body(n - 1)

        def w(i):
            return ws[:, i, :]

        def w4(i):
            return ws[:, i, :].rearrange("p (t c) -> p t c", t=NT)

        def sq(i):
            return sq_c[:, i, :]

        def over_tiles(i):
            return sq_c[:, i:i + 1, :].to_broadcast([P, NT, P])

        def col(name, i=0):
            return cols[:, COLS[name] + i:COLS[name] + i + 1]

        def psum(b, n=512):
            return bank[:, b, 0:n]

        def psum4(b):
            return bank[:, b, :].rearrange("p (t c) -> p t c", t=NT)

        def tt(i, t):
            return ws[:, i, t * P:(t + 1) * P]

        D = [2, 3, 4, 5, 6, 7]

        BETA, GG, GCUM, GL, EDEC, NBEG, TMP1, TMP2 = range(8)

        def dn(i):
            return dn_s[:, i, :].rearrange("p (h t) -> p h t", h=DN_HEADS)

        def dn_bcast(i, h):
            return dn(i)[:, h, :].unsqueeze(2).to_broadcast([P, NT, P])

        kwin = ws[:, 8:11, :].rearrange("p t c -> p (t c)")[:, 0:SW_KV * (SW_DIM + SEQ)].rearrange(
            "p (g c) -> p g c", g=SW_KV)
        V_T, PT_OWN, PT_PREV, R_T, SQ_T, KN_T = 11, (12, 13), (14, 15), 16, 15, 5

        def swp(e):
            return ws[:, 4 + 2 * e:6 + 2 * e, :].rearrange("p a (t c) -> p (a t) c", c=2 * P)

        distance = ws[:, 17:19, :].rearrange("p t c -> p (t c)")[:, 0:NT * WIN].rearrange("p (t c) -> p t c", t=NT)
        ba_w = sb("ba_w", [P, 2, KT * 16], F32R)

        H_AT = (0, KT)

        H_NEXT = {"out0": 0, "down01": 0, "out1": KT}

        def col_k(name, k):
            return cols[:, bass.ds(k + COLS[name], 1)]

        def conv_w(h, j, tap):
            return cols[:, bass.ds(12 * h + (COLS["conv"] + 4 * j + tap), 1)]

        def hid_tile(layer, it, j):
            if layer == 0:
                return 2 * it + j + KT
            return 2 * it + j if j < 8 else KT + j

        def mq_p_of(t):
            return ws[:, 4 + t // 2, (t % 2) * MEM_LEN:(t % 2 + 1) * MEM_LEN]

        def cat_tile(layer, k):
            return KT + k if layer == 0 else (k if k < KT else KT + k)

        @block.sync
        def _(sp):
            sp.dma_start(ws[:, 8:12, :].rearrange("p t c -> p (t c)"),
                         mem.rearrange("(t p) d -> p t d", p=P)).then_inc(S.mem_loaded, 16)
            sp.dma_start(sq_c[:], squares_in).then_inc(S.consts_loaded, 16)
            sp.dma_start(cols[:], cols_in).then_inc(S.cols_loaded, 16)

            sp.dma_start(ws[:, E0, 0:KT * 16], w_ba).then_inc(S.ba_loaded, 16)

            def load(it, c, source, width):
                b = 4 * it + c
                if due(b - RING + 1):
                    sp.wait_ge(S.hi_done, b - RING + 1)
                if due(b - RING + 1):
                    sp.wait_ge(S.lo_done, b - RING + 1)
                sp.dma_start(w_raw[:, c % RING, 0:width * P], source).then_inc(raw_loaded[c % RING], 16)

            def load_plain(name, base_row, count):
                b0 = BLOCK0[name]

                def body(i):
                    for j in range(4):
                        load(i, b0 + j, w_stream[base_row + 4 * i + j], KT)
                if count >= 4:
                    turns(sp, count // 4, body)
                for j in range(count // 4 * 4, count):
                    load(0, b0 + j, w_stream[base_row + j], KT)

            def load_pairs(name, array, sub):
                b0 = BLOCK0[name]

                def body(i):
                    for j in range(4):
                        lo = (j % 2) * sub[0] * P
                        load(i, b0 + j, array[2 * i + j // 2, :, lo:lo + sub[j % 2] * P], sub[j % 2])
                turns(sp, KT // 2, body)

            row = 0
            for name, count in _order:
                if name.startswith("out"):
                    load_pairs(name, w_out[int(name[3])], OUT_SUB)
                elif name.startswith("down"):
                    load_pairs(name, w_down[2 * int(name[4]) + int(name[5])], DOWN_SUB)
                else:
                    load_plain(name, row, count)
                    row += count
                if name == "mem0":
                    sp.dma_start(ws[:, 0:8, :].rearrange("p t c -> p (t c)"),
                                 x.rearrange("(t p) d -> p t d", p=P)).then_inc(S.x_loaded, 16)
                if name == "kv":
                    sp.dma_start(ws[:, 17:19, :].rearrange("p t c -> p (t c)")[:, 0:NT * WIN],
                                 dist_in.rearrange("p t c -> p (t c)")).then_inc(S.dist_loaded, 16)
            sp.wait_ge(S.fin_done, NT)
            sp.dma_start(out.rearrange("(t p) d -> p t d", p=P),
                         ws[:, 0:8, :].rearrange("p (t a) c -> p t (a c)", t=NT)).then_inc(stored, 16)
            sp.wait_ge(stored, 16)

        @block.gpsimd
        def _(pool):
            def lower(it, c, width):
                pool.wait_ge(S.hi_done, 4 * it + c + 1)
                s = c % RING
                nc.gpsimd.tensor_tensor(w_lo[:, s, 0:width * P], w_raw[:, s, 0:width * P],
                                        w_hi[:, s, 0:width * P].bitcast(F32), ALU.subtract).then_inc(S.lo_done, 1)

            def lower_all(name, count):
                b0 = BLOCK0[name]
                if count >= 4:
                    turns(pool, count // 4, lambda i: [lower(i, b0 + j, subtiles(b0 + j)) for j in range(4)])
                for j in range(count // 4 * 4, count):
                    lower(0, b0 + j, subtiles(b0 + j))

            def rows_of(h):
                at_once(pool)
                if due(h):
                    pool.wait_ge(S.nw_mm, h)
                pool.wait_ge(S.ba_g, 1)
                nc.gpsimd.tensor_tensor(w4(KBG), over_tiles(TRIU), dn_bcast(GG, h), ALU.mult).then_inc(S.ug_done, 1)
                at_once(pool)
                if due(h):
                    pool.wait_ge(S.o_done, h)
                pool.wait_ge(S.ba_dve, 4)
                nc.gpsimd.tensor_tensor(w4(KDEC), over_tiles(IDENT), dn_bcast(BETA, h), ALU.mult).then_inc(S.ug_done, 1)

            def o_lower(h):
                at_once(pool)
                pool.wait_ge(S.o_hi, h + 1)
                nc.gpsimd.tensor_tensor(act_lo[:, h + KT, :], w(MM), act_hi[:, h + KT, :].bitcast(F32),
                                        ALU.subtract).then_inc(S.o_lo, 1)

            def delta(h, following):
                if due(h):
                    o_lower(h - 1)
                pool.wait_ge(S.eg_done, h + 1)
                pool.wait_ge(S.qn_done, h + 1)
                nc.gpsimd.tensor_tensor(w(EG), w(EG), w(QN), ALU.mult).then_inc(S.qd_done, 1)
                if following:
                    for j in range(4):
                        lower(h + 1, BLOCK0["dn"] + j + 2, KT)
                    rows_of(h + 1)

            lower_all("mem0", 8)
            lower_all("mem1", 8)
            dn0 = BLOCK0["dn"]
            for j in range(6):
                lower(0, dn0 + j, KT)
            rows_of(0)
            turns(pool, DN_HEADS - 1, lambda h: delta(h, True))
            delta(DN_HEADS - 1, False)
            o_lower(DN_HEADS - 1)
            for j in range(2, MEM_HEADS):
                lower(0, BLOCK0["mq0"] + j, KT)
            for name, count in _order[4:]:
                lower_all(name, count)

        @block.tensor
        def _(pe):
            def product(it, c, nsub, k0, act0, acc, start, stop, n=SEQ, off=0, ks=None):
                ks = range(nsub) if ks is None else ks
                if ks[0] == 0:
                    pe.wait_ge(S.lo_done, 4 * it + c + 1)
                for k in ks:
                    wsl = slice(k * P, (k + 1) * P)
                    for m, (wt, at) in enumerate(((w_hi, act_hi), (w_hi, act_lo), (w_lo, act_hi))):
                        mm = nc.tensor.matmul(acc, wt[:, c % RING, wsl], at[:, act0(k0 + k), off:off + n],
                                              start=(start and k == 0 and m == 0),
                                              stop=(stop and k == nsub - 1 and m == 2))
                if ks[-1] == nsub - 1:
                    mm.then_inc(S.block_used, 1)

            def acc_ready(n):
                if due(n - 1):
                    pe.wait_ge(S.acc_free, n - 1)

            def transposes4(dst, source):
                for t in range(NT):
                    mm = nc.tensor.transpose(bank[:, dst, t * P:(t + 1) * P], tt(source, t), sq(IDENT))
                return mm

            pe.wait_ge(S.consts_loaded, 16)
            pe.wait_ge(S.m_scaled, MT_)
            for k in range(KT):
                if k >= 4:
                    if due(2 * (k - 3)):
                        pe.wait_ge(S.m_evac_hi, 2 * (k - 3))
                    if due(2 * (k - 3)):
                        pe.wait_ge(S.m_evac_lo, 2 * (k - 3))
                for t in range(MT_):
                    mm = nc.tensor.transpose(bank[:, D[k % 4], t * P:(t + 1) * P],
                                             ws[:, 8 + 2 * t:10 + 2 * t, :].rearrange("p a c -> p (a c)")[
                                                 :, k * P:(k + 1) * P], sq(IDENT))
                mm.then_inc(S.m_tr, 1)

            def mem_proj(layer):
                b0, n0 = BLOCK0[f"mem{layer}"], TILE0[f"mem{layer}"]
                pe.wait_ge(S.m_evac_lo, 2 * KT)

                def body(i):
                    for j in range(2):
                        n = n0 + 4 * i + 2 * j
                        head = 2 * i + j + MEM_HEADS * layer
                        acc_ready(n)
                        product(i, b0 + 2 * j, KT, 0, lambda k: KT + k, psum(0, MEM_LEN), True, True,
                                n=MEM_LEN, off=MEM_LEN * layer)
                        acc_ready(n + 1)
                        pe.wait_ge(S.lo_done, 4 * i + b0 + 2 * j + 2)
                        s = (b0 + 2 * j + 1) % RING
                        for t in range(MT_):
                            off = MEM_LEN * layer + t * P
                            for k in range(KT):
                                for m, (at, wt) in enumerate(((act_hi, w_hi), (act_lo, w_hi), (act_hi, w_lo))):
                                    mm = nc.tensor.matmul(bank[:, 1, t * P:(t + 1) * P],
                                                          at[:, KT + k, off:off + P],
                                                          wt[:, s, k * P:(k + 1) * P],
                                                          start=(k == 0 and m == 0), stop=(k == KT - 1 and m == 2))
                        mm.then_inc(S.block_used, 1)
                        pe.wait_ge(S.mk_sq, head + 1)
                        if due(head):
                            pe.wait_ge(S.mk_ln, head)
                        nc.tensor.matmul(psum(D[4], MEM_LEN), sq(ONES), w(KS)[:, 0:MEM_LEN],
                                         start=True, stop=True).then_inc(S.mk_ss, 1)
                turns(pe, MEM_HEADS // 2, body)

            mem_proj(0)

            def x_transposes(k):
                for t in range(NT):
                    mm = nc.tensor.transpose(bank[:, D[k % 4], t * P:(t + 1) * P],
                                             ws[:, 2 * t:2 * t + 2, :].rearrange("p a c -> p (a c)")[
                                                 :, k * P:(k + 1) * P], sq(IDENT))
                return mm
            pe.wait_ge(S.x_loaded, 16)
            for k in range(KT):
                if due(k - 3):
                    pe.wait_ge(S.x_raw_copied, k - 3)
                x_transposes(k).then_inc(S.x_raw_tr, 1)
            mem_proj(1)
            pe.wait_ge(S.x_scaled, NT)
            pe.wait_ge(S.x_raw_copied, KT)
            for k in range(KT):
                if due(k - 3):
                    pe.wait_ge(S.x_evac_lo, k - 3)
                x_transposes(k).then_inc(S.x_tr, 1)

            pe.wait_ge(S.x_evac_lo, KT)
            pe.wait_ge(S.ba_split, 1)
            for t in range(NT):
                for k in range(KT):
                    for m, (at, wi) in enumerate(((act_hi, 0), (act_lo, 0), (act_hi, 1))):
                        mm = nc.tensor.matmul(bank[:, D[0], t * 16:(t + 1) * 16], at[:, k, t * P:(t + 1) * P],
                                              ba_w[:, wi, k * 16:(k + 1) * 16],
                                              start=(k == 0 and m == 0), stop=(k == KT - 1 and m == 2))
            mm.then_inc(S.ba_mm, 1)
            pe.wait_ge(S.ba_g, 1)
            nc.tensor.matmul(bank[:, D[1], 0:32], sq(TRIU), dn_s[:, GG, :], start=True, stop=True)
            nc.tensor.matmul(bank[:, D[2], 0:32], sq(ONES), dn_s[:, GG, :], start=True, stop=True
                             ).then_inc(S.ba_cum, 1)

            def proj_dn(h, j, ks=range(KT)):
                if ks[0] == 0:
                    acc_ready(TILE0["dn"] + 4 * h + j)
                product(h, BLOCK0["dn"] + j, KT, 0, lambda k: k, psum(j % 2), True, True, ks=ks)

            def half_tiles(g):
                return range(NT // 2 * g, NT // 2 * (g + 1))

            def delta(h, fill):
                pe.wait_ge(S.sq_done, 2 * h + 1)
                if due(h):
                    pe.wait_ge(S.at_done, h)
                nc.tensor.matmul(psum(D[0]), sq(ONES), w(E0), start=True, stop=True).then_inc(S.ss_done, 1)
                pe.wait_ge(S.sq_done, 2 * h + 2)
                nc.tensor.matmul(psum(D[1]), sq(ONES), w(PM), start=True, stop=True).then_inc(S.ss_done, 1)
                pe.wait_ge(S.ug_done, 2 * h + 1)
                if due(h):
                    pe.wait_ge(S.o_ln, h)
                nc.tensor.matmul(psum(D[2]), sq(ONES), w(KBG), start=True, stop=True).then_inc(S.gb_done, 1)
                pe.wait_ge(S.ug_done, 2 * h + 2)
                if due(NT * h):
                    pe.wait_ge(S.v_done, NT * h)
                nc.tensor.matmul(psum(D[3]), sq(ONES), w(KDEC), start=True, stop=True).then_inc(S.gb_done, 1)
                pe.wait_ge(S.c_ready, h + 1)
                if due(3 * h):
                    pe.wait_ge(S.s_done, 3 * h)
                transposes4(D[4], CV).then_inc(S.vtr_done, 1)
                fill(0, range(0, 5))
                pe.wait_ge(S.kn_done, h + 1)
                if due(h):
                    pe.wait_ge(S.o_t1, h)
                transposes4(D[5], KN).then_inc(S.ktr_done, 1)
                fill(0, range(5, 8))
                pe.wait_ge(S.kb_done, h + 1)
                for t in range(NT):
                    mm = nc.tensor.matmul(bank[:, D[1], t * P:(t + 1) * P], tt(KN, t), tt(PM, t), start=True, stop=True)
                mm.then_inc(S.gg_done, 1)
                pe.wait_ge(S.qn_done, h + 1)
                for t in range(NT):
                    mm = nc.tensor.matmul(bank[:, D[0], t * P:(t + 1) * P], tt(KN, t), tt(QN, t), start=True, stop=True)
                mm.then_inc(S.gg_done, 1)
                fill(1, range(0, 6))
                pe.wait_ge(S.z_done, h + 1)
                pe.wait_ge(S.dm_pre, 2 * h + 1)
                transposes4(D[2], ZZ).then_inc(S.t_tr, 1)
                fill(1, range(6, 8))
                for k in range(1, LEVELS):
                    n = 12 * h + 2 * (k - 1)
                    for g in range(2):
                        if k == 1:
                            pe.wait_ge(S.t_done, h + 1)
                        else:
                            pe.wait_ge(S.tz_done, n + g - 1)
                        for i, t in enumerate(half_tiles(g)):
                            mm = nc.tensor.matmul(bank[:, D[3 - g], i * P:(i + 1) * P], tt(MM, t), tt(TT, t),
                                                  start=True, stop=True)
                        mm.then_inc(S.p_mm, 1)
                    if k <= 4:
                        fill(2, range(2 * k - 2, 2 * k - 1))
                    for g in range(2):
                        pe.wait_ge(S.p_done, n + g + 1)
                        if k == 1:
                            pe.wait_ge(S.vb_done, h + 1)
                            pe.wait_ge(S.kdec_done, h + 1)
                        for i, t in enumerate(half_tiles(g)):
                            if k < LEVELS - 1:
                                nc.tensor.matmul(bank[:, D[4 + g], i * P:(i + 1) * P], tt(ZZ, t), tt(PM, t),
                                                 start=True, stop=True)
                            mm = nc.tensor.matmul(bank[:, D[4 + g], (2 + i) * P:(3 + i) * P], tt(PM, t), tt(ZZ, t),
                                                  start=True, stop=True)
                        mm.then_inc(S.tz_mm, 1)
                    if k <= 4:
                        fill(2, range(2 * k - 1, 2 * k))
                fill(3, range(0, 1))
                pe.wait_ge(S.tz_done, 12 * h + 12)
                pe.wait_ge(S.kbg_done, h + 1)
                for t in range(NT):
                    mm = nc.tensor.matmul(bank[:, D[2], t * P:(t + 1) * P], tt(KBG, t), tt(ZZ, t), start=True, stop=True)
                mm.then_inc(S.nw_mm, 1)
                pe.wait_ge(S.at_done, h + 1)
                for t in range(NT):
                    n = NT * h + t
                    if due(n):
                        pe.wait_ge(S.v_done, n)
                    v_acc = bank[:, D[3], 0:P]
                    mm = nc.tensor.matmul(v_acc, tt(ZZ, t), tt(VB, t), start=True, stop=(t == 0))
                    if t:
                        pe.wait_ge(S.nw_done, h + 1)
                        pe.wait_ge(S.s_done, 3 * h + t)
                        mm = nc.tensor.matmul(v_acc, tt(MM, t), state[:], start=False, stop=True)
                    mm.then_inc(S.v_mm, 1)
                    o_acc = bank[:, D[5], t * P:(t + 1) * P]
                    pe.wait_ge(S.qd_done, h + 1)
                    if t:
                        nc.tensor.matmul(o_acc, state[:], tt(EG, t), start=True, stop=False)
                    fill(3, range(t + 1, t + 2))
                    pe.wait_ge(S.v_done, n + 1)
                    if t < NT - 1:
                        nc.tensor.matmul(bank[:, D[4], 0:P], tt(KDEC, t), ws[:, E0, t * P:(t + 1) * P],
                                         start=True, stop=True).then_inc(S.s_mm, 1)
                    mm = nc.tensor.matmul(o_acc, ws[:, E0, t * P:(t + 1) * P], tt(AT, t), start=(t == 0), stop=True)
                mm.then_inc(S.o_done, 1)
                fill(3, range(5, 8))
                pe.wait_ge(S.osq, h + 1)
                nc.tensor.matmul(psum(D[2]), sq(ONES), w(E1), start=True, stop=True).then_inc(S.oss, 1)

            pe.wait_ge(S.x_evac_lo, KT)
            for j in range(4):
                proj_dn(0, j)
            turns(pe, DN_HEADS - 1, lambda h: delta(h, lambda j, ks: proj_dn(h + 1, j, ks)))

            def mem_project(layer, j, ks):
                name = f"mq{layer}"
                if ks[0] == 0:
                    acc_ready(TILE0[name] + j)
                product(0, BLOCK0[name] + j, KT, 0, lambda k: H_AT[layer] + k, psum(j % 2), True, True, ks=ks)

            def out_ahead(layer, j):
                name = f"out{layer}"
                act_of = (lambda k: cat_tile(layer, k))
                if j == 0:
                    acc_ready(TILE0[name])
                    product(0, BLOCK0[name], OUT_SUB[0], 0, act_of, psum(0), True, False)
                else:
                    product(0, BLOCK0[name] + 1, OUT_SUB[1], OUT_SUB[0], act_of, psum(0), False, True,
                            ks=range(0, KT - OUT_SUB[0]))

            def mem_attention(layer):
                def sums(j):
                    u = layer * MEM_HEADS + j
                    pe.wait_ge(S.mq_sq, u + 1)
                    if due(u):
                        pe.wait_ge(S.mq_ln, u)
                    nc.tensor.matmul(psum(D[0]), sq(ONES), w(2), start=True, stop=True).then_inc(S.mq_ss, 1)

                def scores(j):
                    u = layer * MEM_HEADS + j
                    pe.wait_ge(S.mq_n, u + 1)
                    if due(u):
                        pe.wait_ge(S.mq_p, u)
                    for t in range(NT):
                        mm = nc.tensor.matmul(bank[:, D[2] + t // 2, (t % 2) * MEM_LEN:(t % 2 + 1) * MEM_LEN],
                                              tt(3, t), kmem[:, u, :], start=True, stop=True)
                    mm.then_inc(S.mq_sc, 1)

                sums(0)
                mem_project(layer, 1, range(KT // 2 if layer else 0, KT))
                scores(0)
                for j in range(MEM_HEADS):
                    u = layer * MEM_HEADS + j
                    if j + 1 < MEM_HEADS:
                        sums(j + 1)
                    if j + 2 < MEM_HEADS:
                        mem_project(layer, j + 2, range(0, 5))
                    else:
                        if j + 2 == MEM_HEADS:
                            if layer == 0:
                                pe.wait_ge(S.o_lo, DN_HEADS)
                            else:
                                pe.wait_ge(S.sw_o_lo, SW_HEADS // QPB)
                        out_ahead(layer, j + 2 - MEM_HEADS)
                    pe.wait_ge(S.mq_p, u + 1)
                    if due(u):
                        pe.wait_ge(S.mq_pt, 2 * u)
                    for m in range(MT_):
                        for t in range(NT):
                            p_t = ws[:, 4:6, :].rearrange("p a c -> p (a c)")[
                                :, t * MEM_LEN + m * P:t * MEM_LEN + (m + 1) * P]
                            mm = nc.tensor.transpose(bank[:, D[4] + m, t * P:(t + 1) * P], p_t, sq(IDENT))
                    mm.then_inc(S.mq_tr, 1)
                    if j + 2 < MEM_HEADS:
                        mem_project(layer, j + 2, range(5, KT))
                    pe.wait_ge(S.mq_pt, 2 * u + 2)
                    if due(u):
                        pe.wait_ge(S.mq_lo, u)
                    for m in range(MT_):
                        mm = nc.tensor.matmul(psum(D[1]), vmem[:, u, m * P:(m + 1) * P], w(6 + m),
                                              start=(m == 0), stop=(m == MT_ - 1))
                    mm.then_inc(S.mq_o, 1)
                    if j + 1 < MEM_HEADS:
                        scores(j + 1)

            delta(DN_HEADS - 1, lambda j, ks: mem_project(0, 0, ks) if j == 0 else None)
            mem_attention(0)

            def out_tiles(name, layer, sub, act_of, ahead=False):
                def body(i):
                    for j in range(2):
                        c = BLOCK0[name] + 2 * j
                        if ahead and isinstance(i, int) and (i, j) == (0, 0):
                            product(i, c + 1, sub[1], sub[0], act_of, psum(j), False, True,
                                    ks=range(KT - sub[0], sub[1]))
                            continue
                        acc_ready(TILE0[name] + 2 * i + j)
                        product(i, c, sub[0], 0, act_of, psum(j), True, False)
                        product(i, c + 1, sub[1], sub[0], act_of, psum(j), False, True)
                turns(pe, KT // 2, body)

            def row_sums(r):
                if due(KT * (r + 1)):
                    pe.wait_ge(S.r_acc, KT * (r + 1))
                nc.tensor.matmul(psum(D[0]), sq(ONES), w(SQ_T), start=True, stop=True).then_inc(S.r_ss, 1)

            def ffn(layer):
                h_of = (lambda k: H_AT[layer] + k)
                for half in range(2):
                    b0, n0 = BLOCK0[f"up{layer}{half}"], TILE0[f"up{layer}{half}"]

                    def pair(it, j):
                        for g in range(2):
                            acc_ready(4 * it + n0 + 2 * j + g)
                            product(it, b0 + 2 * j + g, KT, 0, h_of, psum(g), True, True)
                            if half == 0 and isinstance(it, int) and (it, j, g) == (0, 0, 0):
                                row_sums(2 * layer)

                    def body(it):
                        pair(it, 0)
                        pair(it, 1)
                    if half == 0:
                        if due(KT * (2 * layer + 1)):
                            pe.wait_ge(S.r_lo, KT * (2 * layer + 1))
                    turns(pe, 4, body)
                    for j in range(8, HALF):
                        pair(0, j)
                    pe.wait_ge(S.f_lo, HALF * (2 * layer + half + 1))
                    out_tiles(f"down{layer}{half}", layer, DOWN_SUB, lambda k: cat_tile(layer, k))

            pe.wait_ge(S.mq_lo, MEM_HEADS)
            out_tiles("out0", 0, OUT_SUB, lambda k: cat_tile(0, k), ahead=True)
            ffn(0)

            pe.wait_ge(S.r_lo, 2 * KT)
            acc_ready(TILE0["kv"])
            product(0, BLOCK0["kv"], KT, 0, lambda k: k, psum(0), True, True)
            row_sums(1)
            acc_ready(TILE0["kv"] + 1)
            pe.wait_ge(S.lo_done, BLOCK0["kv"] + 2)
            s = (BLOCK0["kv"] + 1) % RING
            for t in range(NT):
                for k in range(KT):
                    for m, (at, wt) in enumerate(((act_hi, w_hi), (act_lo, w_hi), (act_hi, w_lo))):
                        mm = nc.tensor.matmul(bank[:, 1, t * P:(t + 1) * P], at[:, k, t * P:(t + 1) * P],
                                              wt[:, s, k * P:(k + 1) * P],
                                              start=(k == 0 and m == 0), stop=(k == KT - 1 and m == 2))
            mm.then_inc(S.block_used, 1)
            pe.wait_ge(S.r_done, 2)
            for t in range(NT):
                mm = nc.tensor.matmul(bank[:, D[1], t:t + 1], ws[:, R_T, t * P:(t + 1) * P], sq_c[:, IDENT, 0:1],
                                      start=True, stop=True)
            mm.then_inc(S.kv_ss, 1)
            pe.wait_ge(S.kv_sq, 1)
            pe.wait_ge(S.r_ln, 2)
            nc.tensor.matmul(psum(D[0]), sq(ONES64), w(3), start=True, stop=True).then_inc(S.kv_ss, 1)

            def sw_project(u, ks):
                past = u - SW_HEADS // QPB
                if past >= 0:
                    if past == 0 or ks[0] < KT // 2:
                        mem_project(1, past, ks)
                    return
                if ks[0] == 0:
                    acc_ready(TILE0["swq"] + u)
                product(0, BLOCK0["swq"] + u, KT, 0, lambda k: KT + k, psum(u % 2), True, True, ks=ks)

            def sw_sums(u):
                pe.wait_ge(S.sw_sq, u + 1)
                if due(u):
                    pe.wait_ge(S.sw_ln, u)
                nc.tensor.matmul(psum(D[4]), sq(ONES64), w(1), start=True, stop=True).then_inc(S.sw_ss, 1)

            def sw_scores(u, e):
                n = 2 * u + e
                pe.wait_ge(S.sw_q, u + 1)
                if due(n - 1):
                    pe.wait_ge(S.sw_pt, n - 1)
                if due(n - 1):
                    pe.wait_ge(S.sw_ptp, n - 1)
                rows = slice(SW_DIM * e, SW_DIM * (e + 1))
                for t in range(NT):
                    mm = nc.tensor.matmul(bank[:, D[0] + 2 * e + t // 2, (t % 2) * 256:(t % 2) * 256 + WIN],
                                          ws[rows, 3, t * P:(t + 1) * P],
                                          kwin[rows, u // 4, t * P:t * P + WIN],
                                          start=True, stop=True)
                mm.then_inc(S.sw_sc, 1)

            def sw_transposes(u, e):
                pe.wait_ge(S.sw_p, 2 * u + e + 1)
                for t in range(NT):
                    mm = nc.tensor.transpose(bank[:, D[0] + 2 * e, t * P:(t + 1) * P], swp(e)[:, t, P:2 * P], sq(IDENT))
                    if t:
                        mm = nc.tensor.transpose(bank[:, D[1] + 2 * e, t * P:(t + 1) * P], swp(e)[:, t, 0:P], sq(IDENT))
                mm.then_inc(S.sw_tr, 1)

            def sw_output(u, e):
                pe.wait_ge(S.sw_pt, 2 * u + e + 1)
                pe.wait_ge(S.sw_ptp, 2 * u + e + 1)
                if due(u):
                    pe.wait_ge(S.sw_o_lo, u)
                rows = slice(SW_DIM * e, SW_DIM * (e + 1))
                v_of = slice(u // 4 * SW_DIM, (u // 4 + 1) * SW_DIM)
                for t in range(NT):
                    o_acc = bank[rows, D[5], t * P:(t + 1) * P]
                    mm = nc.tensor.matmul(o_acc, tt(V_T, t)[:, v_of], tt(PT_OWN[e], t), start=True, stop=(t == 0))
                    if t:
                        mm = nc.tensor.matmul(o_acc, tt(V_T, t - 1)[:, v_of], tt(PT_PREV[e], t),
                                              start=False, stop=True)
                mm.then_inc(S.sw_o, 1)

            pe.wait_ge(S.b_lo, KT)
            sw_project(0, range(KT))
            sw_sums(0)
            sw_project(1, range(KT))
            pe.wait_ge(S.kv_done, 7)
            pe.wait_ge(S.kv_dup, 32)
            sw_scores(0, 0)
            sw_scores(0, 1)
            for u in range(SW_HEADS // QPB):
                following = u + 1 < SW_HEADS // QPB
                if following:
                    sw_sums(u + 1)
                sw_project(u + 2, range(0, 4))
                sw_transposes(u, 0)
                sw_project(u + 2, range(4, 6))
                sw_transposes(u, 1)
                sw_project(u + 2, range(6, KT))
                sw_output(u, 0)
                if following:
                    sw_scores(u + 1, 0)
                sw_output(u, 1)
                if following:
                    sw_scores(u + 1, 1)
            mem_attention(1)

            pe.wait_ge(S.mq_lo, 2 * MEM_HEADS)
            out_tiles("out1", 1, OUT_SUB, lambda k: cat_tile(1, k), ahead=True)
            ffn(1)

            pe.wait_ge(S.acc_free, N_TILES)
            for t in range(NT):
                if t:
                    if due(t):
                        pe.wait_ge(S.fin_done, t)
                for k in range(KT):
                    mm = nc.tensor.transpose(bank[:, D[0] + k // 4, (k % 4) * P:(k % 4 + 1) * P],
                                             xT[:, k, t * P:(t + 1) * P], sq(IDENT))
                mm.then_inc(S.fin_tr, 1)

        @block.scalar
        def _(act):
            def a(out_, in_, func, **kw):
                return nc.scalar.activation(out_, in_, func, **kw)

            def upper(it, c):
                b = 4 * it + c
                if isinstance(b, int) and b >= N_BLOCKS:
                    return
                width = subtiles(b if isinstance(b, int) else c + 4) * P
                s = c % RING
                act.wait_ge(raw_loaded[s], 16 * it + 16 * (c // RING) + 16)
                if due(b - RING + 1):
                    act.wait_ge(S.block_used, b - RING + 1)
                a(w_hi[:, s, 0:width], w_raw[:, s, 0:width], ACT.Copy).then_inc(S.hi_done, 1)

            act.preload_act_table_set("natural_log_exp_and_others")
            act.wait_ge(S.mem_loaded, 16)
            act.wait_ge(S.cols_loaded, 16)

            def rows(first, t):
                return ws[:, first + 2 * t:first + 2 * t + 2, :].rearrange("p a c -> p (a c)")
            for t in range(MT_):
                a(rows(12, t), rows(8, t), ACT.Square, accum_out=st[:, t:t + 1]).then_inc(S.m_sq, 1)
            act.wait_ge(S.m_sq, MT_)
            a(st[:, 6:8], st[:, 0:2], ACT.Ln, scale=1.0 / D_MODEL, bias=col("eps")).then_inc(S.m_ln, 1)
            act.wait_ge(S.m_ln, 1)
            a(st[:, 6:8], st[:, 6:8], ACT.Exp, scale=-0.5).then_inc(S.m_rstd, 1)
            act.wait_ge(S.m_rstd, 1)
            for t in range(MT_):
                a(rows(8, t), rows(8, t), ACT.Copy, scale=st[:, 6 + t:7 + t]).then_inc(S.m_scaled, 1)
            upper(0, 0)
            upper(0, 1)
            for k in range(KT):
                act.wait_ge(S.m_tr, k + 1)
                for layer in range(2):
                    a(act_hi[:, KT + k, MEM_LEN * layer:MEM_LEN * (layer + 1)], psum(D[k % 4], MEM_LEN), ACT.Copy, scale=col(f"mem{layer}", k)).then_inc(S.m_evac_hi, 1)

            def mem_keys(layer):
                def body(i):
                    for j in range(2):
                        c = BLOCK0[f"mem{layer}"] + 2 * j
                        head = 2 * i + j + MEM_HEADS * layer
                        upper(i, c + 2)
                        act.wait_ge(S.acc_free, 4 * i + TILE0[f"mem{layer}"] + 2 * j + 1)
                        if due(head):
                            act.wait_ge(S.mk_ss, head)
                        a(w(KS)[:, 0:MEM_LEN], w(KR)[:, 0:MEM_LEN], ACT.Square).then_inc(S.mk_sq, 1)
                        upper(i, c + 3)
                        act.wait_ge(S.mk_ss, head + 1)
                        if due(head):
                            act.wait_ge(S.mk_done, head)
                        a(w(KRS)[:, 0:MEM_LEN], psum(D[4], MEM_LEN), ACT.Ln, scale=1.0 / P, bias=col("eps")).then_inc(S.mk_ln, 1)
                        act.wait_ge(S.mk_ln, head + 1)
                        a(w(KRS)[:, 0:MEM_LEN], w(KRS)[:, 0:MEM_LEN], ACT.Exp, scale=-0.5).then_inc(S.mk_rstd, 1)
                turns(act, MEM_HEADS // 2, body)

            mem_keys(0)
            act.wait_ge(S.x_loaded, 16)
            act.wait_ge(S.m_tr, KT)
            for t in range(NT):
                if due(t - 1):
                    act.wait_ge(S.x_sq, t - 1)
                a(rows(8, t % 2), rows(0, t), ACT.Square, accum_out=st[:, 2 + t:3 + t]).then_inc(S.x_sq, 1)
            act.wait_ge(S.x_sq, NT)
            a(st[:, 8:12], st[:, 2:6], ACT.Ln, scale=1.0 / D_MODEL, bias=col("eps")).then_inc(S.x_ln, 1)
            act.wait_ge(S.x_ln, 1)
            a(st[:, 8:12], st[:, 8:12], ACT.Exp, scale=-0.5).then_inc(S.x_rstd, 1)
            act.wait_ge(S.x_rstd, 1)
            act.wait_ge(S.x_raw_tr, KT)
            for t in range(NT):
                a(rows(0, t), rows(0, t), ACT.Copy, scale=st[:, 8 + t:9 + t]).then_inc(S.x_scaled, 1)
            act.wait_ge(S.ba_loaded, 16)
            a(ba_w[:, 0, :], w(E0)[:, 0:KT * 16], ACT.Copy).then_inc(S.ba_hi, 1)
            mem_keys(1)
            for k in range(KT):
                act.wait_ge(S.x_tr, k + 1)
                a(act_hi[:, k, :], psum(D[k % 4]), ACT.Copy, scale=col("a_norm", k)).then_inc(S.x_evac_hi, 1)

            act.wait_ge(S.ba_mm, 1)
            ba_ps = bank[:, D[0], 0:NT * 16].rearrange("p (t c) -> p c t", t=NT)
            a(dn(TMP1), ba_ps[:, 0:DN_HEADS, :], ACT.Exp, scale=-1.0).then_inc(S.ba_act, 1)
            a(st[:, 16:24], cols[:, COLS["a_log"]:COLS["a_log"] + DN_HEADS], ACT.Exp).then_inc(S.ba_act, 1)
            act.wait_ge(S.ba_dve, 2)
            a(dn(GL), dn(GL), ACT.Exp, scale=-1.0).then_inc(S.ba_act, 1)
            act.wait_ge(S.ba_act, 3)
            a(dn(GL), dn(GL), ACT.Ln, bias=sq_c[:, ONES, 0:1]).then_inc(S.ba_act, 1)
            act.wait_ge(S.ba_dve, 7)
            a(dn_s[:, GL, :], bank[:, D[2], 0:32], ACT.Exp).then_inc(S.ba_act, 1)
            a(dn(EDEC), dn(TMP1), ACT.Exp).then_inc(S.ba_act, 1)
            a(dn(TMP2), dn(GCUM), ACT.Exp).then_inc(S.ba_act, 1)

            def conv_tile(h, j):
                c = BLOCK0["dn"] + j
                upper(h, c + 2)
                if j < 3:
                    at_once(act)
                    act.wait_ge(S.block_used, 4 * h + c + 1)
                    nc.scalar.activation(w(CQ + j), psum(j % 2), ACT.Copy,
                                         scale=conv_w(h, j, 3)).then_inc(S.cv_tap, 1)

            def silu_qkv(h):
                act.wait_ge(S.acc_free, TILE0["dn"] + 4 * h + 3)
                a(ws[:, CQ:CV + 1, :], ws[:, CQ:CV + 1, :], ACT.Silu).then_inc(S.c_ready, 1)

            def squares_qk(h):
                if due(h):
                    act.wait_ge(S.o_done, h)
                act.wait_ge(S.c_ready, h + 1)
                a(w(E0), w(CQ), ACT.Square).then_inc(S.sq_done, 1)
                a(w(PM), w(CK), ACT.Square).then_inc(S.sq_done, 1)

            def o_upper(h):
                at_once(act)
                act.wait_ge(S.o_t2, h + 1)
                a(act_hi[:, h + KT, :], w(MM), ACT.Copy).then_inc(S.o_hi, 1)

            def delta(h, fill, following):
                for m, (e, ln_scale) in enumerate(((E0, "ln_q"), (PM, None))):
                    act.wait_ge(S.ss_done, 2 * h + m + 1)
                    a(w(e), psum(D[m]), ACT.Ln, bias=col("eps")).then_inc(S.rr_ln, 1)
                    act.wait_ge(S.rr_ln, 2 * h + m + 1)
                    kw = dict(bias=col(ln_scale)) if ln_scale else {}
                    a(w(e), w(e), ACT.Exp, scale=-0.5, **kw).then_inc(S.rr_done, 1)
                act.wait_ge(S.gb_done, 2 * h + 1)
                a(w(EG), psum(D[2]), ACT.Exp).then_inc(S.eg_done, 1)
                if due(h):
                    o_upper(h - 1)
                act.wait_ge(S.dm_pre, 2 * h + 2)
                a(w(DD), w(DD), ACT.Exp).then_inc(S.dm_done, 1)
                fill(0)
                act.wait_ge(S.t_tr, h + 1)
                a(w(TT), psum(D[2]), ACT.Copy).then_inc(S.t_done, 1)
                fill(1)
                fill(2)
                if following:
                    silu_qkv(h + 1)
                act.wait_ge(S.acc_free, TILE0["dn"] + 4 * h + 4)
                a(w(SZ), w(EC), ACT.Silu).then_inc(S.sz_done, 1)
                act.preload_act_table_set("natural_log_exp_and_others")
                fill(3)
                act.wait_ge(S.nw_mm, h + 1)
                a(w(MM), psum(D[2]), ACT.Copy).then_inc(S.nw_done, 1)
                for t in range(NT):
                    act.wait_ge(S.v_mm, NT * h + t + 1)
                    a(tt(E0, t), bank[:, D[3], 0:P], ACT.Copy).then_inc(S.v_done, 1)
                act.wait_ge(S.o_done, h + 1)
                a(w(E1), psum(D[5]), ACT.Square).then_inc(S.osq, 1)
                if following:
                    squares_qk(h + 1)
                act.wait_ge(S.oss, h + 1)
                a(w(E1), psum(D[2]), ACT.Ln, scale=1.0 / P, bias=col("eps")).then_inc(S.o_ln, 1)
                act.wait_ge(S.o_ln, h + 1)
                a(w(E1), w(E1), ACT.Exp, scale=-0.5).then_inc(S.o_rstd, 1)

            for j in range(4):
                conv_tile(0, j)
            silu_qkv(0)
            act.preload_act_table_set("natural_log_exp_and_others")
            squares_qk(0)
            turns(act, DN_HEADS - 1, lambda h: delta(h, lambda j: conv_tile(h + 1, j), True))
            delta(DN_HEADS - 1, lambda j: upper(0, BLOCK0["mq0"] + 2) if j == 0 else
                  upper(0, BLOCK0["mq0"] + 3) if j == 3 else None, False)
            o_upper(DN_HEADS - 1)

            def mem_attention(layer):
                c = BLOCK0[f"mq{layer}"]

                def square(j):
                    act.wait_ge(S.acc_free, TILE0[f"mq{layer}"] + j + 1)
                    if due(layer * MEM_HEADS + j):
                        act.wait_ge(S.mq_n, layer * MEM_HEADS + j)
                    a(w(2), w(j % 2), ACT.Square).then_inc(S.mq_sq, 1)

                def rstd_q(j):
                    u = layer * MEM_HEADS + j
                    act.wait_ge(S.mq_ss, u + 1)
                    a(w(2), psum(D[0]), ACT.Ln, scale=1.0 / P, bias=col("eps")).then_inc(S.mq_ln, 1)
                    act.wait_ge(S.mq_ln, u + 1)
                    a(w(2), w(2), ACT.Exp, scale=-0.5, bias=col("ln_q")).then_inc(S.mq_rstd, 1)

                square(0)
                rstd_q(0)
                square(1)
                for j in range(MEM_HEADS):
                    u = layer * MEM_HEADS + j
                    if j + 1 < MEM_HEADS:
                        rstd_q(j + 1)
                    act.wait_ge(S.mq_max, 2 * u + 2)
                    if due(u):
                        act.wait_ge(S.mq_tr, u)
                    if due(u):
                        act.wait_ge(S.mq_p, u)
                    for t in range(NT):
                        a(mq_p_of(t), bank[:, D[2] + t // 2, (t % 2) * MEM_LEN:(t % 2 + 1) * MEM_LEN], ACT.Exp, bias=st[:, 28 + t:29 + t], accum_out=st[:, 32 + t:33 + t]).then_inc(S.mq_exp, 1)
                    if j + 2 < MEM_HEADS:
                        upper(0, c + j + 4)
                    act.wait_ge(S.mq_tr, u + 1)
                    if due(u):
                        act.wait_ge(S.mq_o, u)
                    a(w(6), psum(D[4]), ACT.Copy).then_inc(S.mq_pt, 1)
                    if j + 2 < MEM_HEADS:
                        square(j + 2)
                    act.wait_ge(S.mq_o, u + 1)
                    a(act_hi[:, cat_tile(layer, KT + j), :], psum(D[1]), ACT.Copy).then_inc(S.mq_hi, 1)

            mem_attention(0)

            def residual(name, gain, r, last):
                def body(i):
                    for j in range(2):
                        k = 2 * i + j
                        upper(i, BLOCK0[name] + 2 * j + 2)
                        upper(i, BLOCK0[name] + 2 * j + 3)
                        if last:
                            continue
                        act.wait_ge(S.acc_free, TILE0[name] + k + 1)
                        q = KT * r + k
                        if due(q - 1):
                            act.wait_ge(S.r_acc, q - 1)
                        a(w(13 + j), xT[:, k, :], ACT.Square).then_inc(S.r_sq, 1)
                        at_once(act)
                        nc.scalar.activation(act_hi[:, H_NEXT[name] + k, :], xT[:, k, :], ACT.Copy,
                                             scale=gain(k)).then_inc(S.r_hi, 1)
                turns(act, KT // 2, body)

            def rstd(r):
                act.wait_ge(S.r_ss, r + 1)
                a(w(R_T), psum(D[0]), ACT.Ln, scale=1.0 / D_MODEL, bias=col("eps")).then_inc(S.r_ln, 1)
                act.wait_ge(S.r_ln, r + 1)
                a(w(R_T), w(R_T), ACT.Exp, scale=-0.5).then_inc(S.r_done, 1)

            def ffn(layer):
                for half in range(2):
                    c = BLOCK0[f"up{layer}{half}"]

                    def pair(it, j):
                        upper(it, c + 2 * j + 2)
                        upper(it, c + 2 * j + 3)
                        f = HALF * (2 * layer + half) + 2 * it + j
                        act.wait_ge(S.acc_free, 4 * it + TILE0[f"up{layer}{half}"] + 2 * j + 1)
                        if due(f - 1):
                            act.wait_ge(S.f_hid, f - 1)
                        a(w(2 + j % 2), w(j % 2), ACT.Silu).then_inc(S.f_silu, 1)
                        act.wait_ge(S.f_hid, f + 1)
                        if due(f - 1):
                            act.wait_ge(S.f_lo, f - 1)
                        at_once(act)
                        a(act_hi[:, hid_tile(layer, it, j), :], w(6 + j % 2), ACT.Copy).then_inc(S.f_hi, 1)

                    def body(it):
                        pair(it, 0)
                        pair(it, 1)
                    if half == 0:
                        rstd(2 * layer)
                    turns(act, 4, body)
                    for j in range(8, HALF):
                        pair(0, j)
                    act.preload_act_table_set("natural_log_exp_and_others")
                    nxt = None if half == 0 or layer == 1 else (lambda k: col_k("kv_norm", k))
                    residual(f"down{layer}{half}", nxt, 1, nxt is None)

            residual("out0", lambda k: col_k("ffn0", k), 0, False)
            ffn(0)

            upper(0, BLOCK0["kv"] + 2)
            upper(0, BLOCK0["kv"] + 3)
            act.wait_ge(S.block_used, BLOCK0["kv"])
            for k in range(KT):
                a(act_hi[:, KT + k, :], xT[:, k, :], ACT.Copy, scale=col("b_norm", k)).then_inc(S.b_hi, 1)
            rstd(1)
            act.wait_ge(S.acc_free, TILE0["kv"] + 1)
            a(w(3), w(2), ACT.Square).then_inc(S.kv_sq, 1)
            act.wait_ge(S.kv_ss, 2)
            a(w(4), psum(D[0]), ACT.Ln, scale=1.0 / SW_DIM, bias=col("eps")).then_inc(S.kv_ln, 1)
            act.wait_ge(S.kv_ln, 1)
            a(w(4), w(4), ACT.Exp, scale=-0.5).then_inc(S.kv_rstd, 1)

            def sw_square(u):
                act.wait_ge(S.acc_free, TILE0["swq"] + u + 1)
                if due(u):
                    act.wait_ge(S.sw_ss, u)
                a(w(1), w(0), ACT.Square).then_inc(S.sw_sq, 1)

            def sw_rstd_q(u):
                act.wait_ge(S.sw_ss, u + 1)
                if due(u):
                    act.wait_ge(S.sw_q, u)
                a(w(2), psum(D[4]), ACT.Ln, scale=1.0 / SW_DIM, bias=col("eps")).then_inc(S.sw_ln, 1)
                act.wait_ge(S.sw_ln, u + 1)
                a(w(2), w(2), ACT.Exp, scale=-0.5, bias=col("ln_s")).then_inc(S.sw_rstd, 1)

            act.wait_ge(S.kv_n, 1)
            for g in range(SW_KV):
                other = slice(SW_DIM * (1 - g), SW_DIM * (2 - g))
                act.dma_start(kwin[other, g, SW_DIM:], ws[SW_DIM * g:SW_DIM * (g + 1), KN_T, :]
                              ).then_inc(S.kv_dup, 16)
            upper(0, BLOCK0["swq"] + 2)
            sw_square(0)
            sw_rstd_q(0)
            upper(0, BLOCK0["swq"] + 3)
            sw_square(1)
            for u in range(SW_HEADS // QPB):
                following = u + 1 < SW_HEADS // QPB
                if following:
                    sw_rstd_q(u + 1)
                for e in range(QPB):
                    n = 2 * u + e
                    act.wait_ge(S.sw_nm, n + 1)
                    for t in range(NT):
                        a(swp(e)[:, t, SW_DIM:], swp(e)[:, t, SW_DIM:], ACT.Exp,
                          bias=st[:, 36 + 4 * e + t:37 + 4 * e + t], accum_out=st[:, 44 + 4 * e + t:45 + 4 * e + t]).then_inc(S.sw_exp, 1)
                    a(st[:, 52 + 4 * e:56 + 4 * e], st[:, 36 + 4 * e:40 + 4 * e], ACT.Exp,
                      bias=col("sinks", n)).then_inc(S.sw_exp, 1)
                upper(0, BLOCK0["swq"] + u + 4)
                for e in range(QPB):
                    n = 2 * u + e
                    act.wait_ge(S.sw_tr, n + 1)
                    if due(n - 1):
                        act.wait_ge(S.sw_o, n - 1)
                    a(w(PT_OWN[e]), psum(D[0] + 2 * e), ACT.Copy).then_inc(S.sw_pt, 1)
                if u + 2 < SW_HEADS // QPB:
                    sw_square(u + 2)
                act.wait_ge(S.sw_o, 2 * u + 2)
                a(act_hi[:, u, :], psum(D[5]), ACT.Copy).then_inc(S.sw_o_hi, 1)

            mem_attention(1)
            residual("out1", lambda k: col_k("ffn1", k), 2, False)
            ffn(1)

        @block.vector
        def _(dve):
            V = nc.vector

            def mul(out_, x_, y_):
                return V.tensor_tensor(out_, x_, y_, ALU.mult)

            def sub(out_, x_, y_):
                return V.tensor_tensor(out_, x_, y_, ALU.subtract)

            def stt(out_, x_, scalar, y_, op0, op1):
                return V.scalar_tensor_tensor(out=out_, in0=x_, scalar=scalar, in1=y_, op0=op0, op1=op1)

            def cp(out_, x_):
                return V.tensor_copy(out_, x_)

            def hi(tile_):
                return act_hi[:, tile_, :].bitcast(F32)

            dve.wait_ge(S.consts_loaded, 16)
            dve.wait_ge(S.cols_loaded, 16)
            for k in range(KT):
                dve.wait_ge(S.m_evac_hi, 2 * k + 2)
                for layer in range(2):
                    own = slice(MEM_LEN * layer, MEM_LEN * (layer + 1))
                    stt(act_lo[:, KT + k, own], psum(D[k % 4], MEM_LEN), col(f"mem{layer}", k), hi(KT + k)[:, own],
                        ALU.mult, ALU.subtract).then_inc(S.m_evac_lo, 1)

            def mem_kv(layer):
                def body(i):
                    for j in range(2):
                        c, n = BLOCK0[f"mem{layer}"] + 2 * j, 4 * i + TILE0[f"mem{layer}"] + 2 * j
                        head = 2 * i + j + MEM_HEADS * layer
                        dve.wait_ge(S.block_used, 4 * i + c + 1)
                        if due(head):
                            dve.wait_ge(S.mk_sq, head)
                        if due(head):
                            dve.wait_ge(S.mk_done, head)
                        cp(w(KR)[:, 0:MEM_LEN], psum(0, MEM_LEN)).then_inc(S.acc_free, 1)
                        dve.wait_ge(S.block_used, 4 * i + c + 2)
                        cp(vmem[:, head, :], psum(1, MT_ * P)).then_inc(S.acc_free, 1)
                        dve.wait_ge(S.mk_rstd, head + 1)
                        dve.wait_ge(S.acc_free, n + 1)
                        stt(kmem[:, head, :], w(KR)[:, 0:MEM_LEN], col(f"mk{layer}"), w(KRS)[:, 0:MEM_LEN],
                            ALU.mult, ALU.mult).then_inc(S.mk_done, 1)
                turns(dve, MEM_HEADS // 2, body)

            mem_kv(0)
            for k in range(KT):
                dve.wait_ge(S.x_raw_tr, k + 1)
                cp(xT[:, k, :], psum(D[k % 4])).then_inc(S.x_raw_copied, 1)
            dve.wait_ge(S.ba_hi, 1)
            sub(ba_w[:, 1, :], w(E0)[:, 0:KT * 16], ba_w[:, 0, :].bitcast(F32)).then_inc(S.ba_split, 1)
            mem_kv(1)
            for k in range(KT):
                dve.wait_ge(S.x_evac_hi, k + 1)
                stt(act_lo[:, k, :], psum(D[k % 4]), col("a_norm", k), hi(k), ALU.mult, ALU.subtract).then_inc(S.x_evac_lo, 1)

            def over_t(name):
                return cols[:, COLS[name]:COLS[name] + DN_HEADS].unsqueeze(2).to_broadcast([P, DN_HEADS, NT])
            ba_ps = bank[:, D[0], 0:NT * 16].rearrange("p (t c) -> p c t", t=NT)
            dve.wait_ge(S.ba_act, 1)
            V.tensor_tensor(dn(TMP2), ba_ps[:, DN_HEADS:, :], over_t("dt"), ALU.add).then_inc(S.ba_dve, 1)
            dve.wait_ge(S.ba_dve, 1)
            stt(dn(GL), dn(TMP2), -1.0, dn(TMP2), ALU.mult, ALU.max).then_inc(S.ba_dve, 1)
            V.tensor_scalar(dn(TMP1), dn(TMP1), 1.0, None, ALU.add).then_inc(S.ba_dve, 1)
            dve.wait_ge(S.ba_dve, 3)
            V.reciprocal(dn(BETA), dn(TMP1)).then_inc(S.ba_dve, 1)
            dve.wait_ge(S.ba_act, 4)
            stt(dn(TMP2), dn(TMP2), 0.0, dn(GL), ALU.max, ALU.add).then_inc(S.ba_dve, 1)
            dve.wait_ge(S.ba_dve, 5)
            stt(dn(GG), dn(TMP2), -1.0, st[:, 16:24].unsqueeze(2).to_broadcast([P, DN_HEADS, NT]),
                ALU.mult, ALU.mult).then_inc(S.ba_g, 1)
            dve.wait_ge(S.ba_cum, 1)
            cp(dn_s[:, GCUM, :], bank[:, D[1], 0:32]).then_inc(S.ba_dve, 1)
            dve.wait_ge(S.ba_dve, 6)
            sub(dn_s[:, TMP1, :], bank[:, D[2], 0:32], dn_s[:, GCUM, :]).then_inc(S.ba_dve, 1)
            dve.wait_ge(S.ba_act, 7)
            stt(dn(NBEG), dn(BETA), -1.0, dn(TMP2), ALU.mult, ALU.mult).then_inc(S.ba_dve, 1)
            dve.wait_ge(S.ba_dve, 8)

            def conv_tile(h, j):
                if j < 3:
                    dve.wait_ge(S.cv_tap, 3 * h + j + 1)
                    for d in range(1, 4):
                        taps = 6 * h + 2 * j + d - 1
                        if d > 1:
                            dve.wait_ge(S.cv_conv, taps)
                        stt(w(CQ + j)[:, d:], psum(j % 2)[:, 0:SEQ - d], conv_w(h, j, 3 - d), w(CQ + j)[:, d:],
                            ALU.mult, ALU.add).then_inc(S.cv_conv if d < 3 else S.acc_free, 1)
                else:
                    dve.wait_ge(S.block_used, 4 * h + BLOCK0["dn"] + 4)
                    if due(h):
                        dve.wait_ge(S.sz_done, h)
                    cp(w(EC), psum(1)).then_inc(S.acc_free, 1)

            def delta(h, fill):
                dve.wait_ge(S.rr_done, 2 * h + 1)
                mul(w(QN), w(CQ), w(E0)).then_inc(S.qn_done, 1)
                dve.wait_ge(S.rr_done, 2 * h + 2)
                mul(w(KN), w(CK), w(PM)).then_inc(S.kn_done, 1)
                dve.wait_ge(S.gb_done, 2 * h + 2)
                dve.wait_ge(S.kn_done, h + 1)
                mul(w(PM), w(KN), psum(D[3])).then_inc(S.kb_done, 1)
                dve.wait_ge(S.eg_done, h + 1)
                V.tensor_tensor(w4(DD), psum4(D[2]), over_tiles(NEG_LOWER), ALU.add).then_inc(S.dm_pre, 1)
                dve.wait_ge(S.dm_pre, 2 * h + 1)
                sub(w4(DD), w4(DD), dn_bcast(GCUM, h)).then_inc(S.dm_pre, 1)
                dve.wait_ge(S.vtr_done, h + 1)
                mul(w4(VB), psum4(D[4]), dn_bcast(BETA, h)).then_inc(S.vb_done, 1)
                dve.wait_ge(S.dm_done, h + 1)
                dve.wait_ge(S.gg_done, 2 * h + 1)
                if due(h):
                    dve.wait_ge(S.o_lo, h)
                mul(w(MM), psum(D[1]), w(DD)).then_inc(S.mt_done, 1)
                dve.wait_ge(S.mt_done, h + 1)
                mul(w4(ZZ), w4(MM), over_tiles(LEVEL0)).then_inc(S.z_pre, 1)
                dve.wait_ge(S.z_pre, h + 1)
                sub(w4(ZZ), over_tiles(IDENT), w4(ZZ)).then_inc(S.z_done, 1)
                dve.wait_ge(S.gg_done, 2 * h + 2)
                mul(w(AT), psum(D[0]), w(DD)).then_inc(S.at_done, 1)
                dve.wait_ge(S.ktr_done, h + 1)
                mul(w4(KBG), psum4(D[5]), dn_bcast(NBEG, h)).then_inc(S.kbg_done, 1)
                mul(w4(KDEC), psum4(D[5]), dn_bcast(EDEC, h)).then_inc(S.kdec_done, 1)
                fill(0)
                for k in range(1, LEVELS):
                    n = 12 * h + 2 * (k - 1)
                    for g in range(2):
                        dve.wait_ge(S.p_mm, n + g + 1)
                        own = slice(SEQ // 2 * g, SEQ // 2 * (g + 1))
                        mul(w(PM)[:, own].rearrange("p (t c) -> p t c", c=P),
                            bank[:, D[3 - g], 0:SEQ // 2].rearrange("p (t c) -> p t c", c=P),
                            sq_c[:, LEVEL0 + k:LEVEL0 + k + 1, :].to_broadcast([P, NT // 2, P])).then_inc(S.p_done, 1)
                    for g in range(2):
                        dve.wait_ge(S.tz_mm, n + g + 1)
                        own = slice(SEQ // 2 * g, SEQ // 2 * (g + 1))
                        if k < LEVELS - 1:
                            both = ws[:, TT:ZZ + 1, own]
                            sub(both, both, bank[:, D[4 + g], :].rearrange("p (a c) -> p a c", a=2)
                                ).then_inc(S.tz_done, 1)
                        else:
                            sub(w(ZZ)[:, own], w(ZZ)[:, own], bank[:, D[4 + g], SEQ // 2:]).then_inc(S.tz_done, 1)
                    if k == 1:
                        fill(1)
                    if k == 4:
                        fill(2)
                for t in range(NT - 1):
                    dve.wait_ge(S.s_mm, 3 * h + t + 1)
                    if t == 0:
                        cp(state[:], bank[:, D[4], 0:P]).then_inc(S.s_done, 1)
                    else:
                        dve.wait_ge(S.s_done, 3 * h + t)
                        stt(state[:], state[:], dn(GL)[:, h, t:t + 1], bank[:, D[4], 0:P], ALU.mult, ALU.add
                            ).then_inc(S.s_done, 1)
                fill(3)
                dve.wait_ge(S.o_rstd, h + 1)
                mul(w(E1), psum(D[5]), w(E1)).then_inc(S.o_t1, 1)
                dve.wait_ge(S.o_t1, h + 1)
                dve.wait_ge(S.sz_done, h + 1)
                stt(w(MM), w(E1), col("out_norm"), w(SZ), ALU.mult, ALU.mult).then_inc(S.o_t2, 1)

            for j in range(4):
                conv_tile(0, j)
            turns(dve, DN_HEADS - 1, lambda h: delta(h, lambda j: conv_tile(h + 1, j)))

            def mem_raw(layer, j):
                dve.wait_ge(S.block_used, BLOCK0[f"mq{layer}"] + j + 1)
                if due(layer * MEM_HEADS + j - 1):
                    dve.wait_ge(S.mq_n, layer * MEM_HEADS + j - 1)
                if layer == 0:
                    cp(w(j % 2), psum(j % 2)).then_inc(S.acc_free, 1)
                else:
                    mul(w(j % 2), psum(j % 2), w(R_T)).then_inc(S.acc_free, 1)

            def mem_attention(layer):
                def normed(j):
                    u = layer * MEM_HEADS + j
                    dve.wait_ge(S.mq_rstd, u + 1)
                    if due(u):
                        dve.wait_ge(S.mq_sc, u)
                    dve.wait_ge(S.acc_free, TILE0[f"mq{layer}"] + j + 1)
                    stt(w(3), w(j % 2), col(f"mq{layer}"), w(2), ALU.mult, ALU.mult).then_inc(S.mq_n, 1)

                normed(0)
                mem_raw(layer, 1)
                for j in range(MEM_HEADS):
                    u = layer * MEM_HEADS + j
                    dve.wait_ge(S.mq_sc, u + 1)
                    if due(2 * u):
                        dve.wait_ge(S.mq_max, 2 * u)
                    V.tensor_reduce(st[:, 24:28], bank[:, D[2]:D[2] + 2, :].rearrange("p a (b c) -> p (a b) c", b=2),
                                    AX.X, ALU.max).then_inc(S.mq_max, 1)
                    dve.wait_ge(S.mq_max, 2 * u + 1)
                    V.tensor_scalar(st[:, 28:32], st[:, 24:28], -1.0, None, ALU.mult).then_inc(S.mq_max, 1)
                    if j + 1 < MEM_HEADS:
                        normed(j + 1)
                    dve.wait_ge(S.mq_exp, NT * (u + 1))
                    V.reciprocal(st[:, 32:36], st[:, 32:36]).then_inc(S.mq_rcp, 1)
                    dve.wait_ge(S.mq_rcp, u + 1)
                    p4 = ws[:, 4:6, :].rearrange("p a (b c) -> p (a b) c", b=2)
                    mul(p4, p4, st[:, 32:36].unsqueeze(2).to_broadcast([P, NT, MEM_LEN])).then_inc(S.mq_p, 1)
                    dve.wait_ge(S.mq_tr, u + 1)
                    if due(u):
                        dve.wait_ge(S.mq_o, u)
                    cp(w(7), psum(D[5])).then_inc(S.mq_pt, 1)
                    if j + 2 < MEM_HEADS:
                        mem_raw(layer, j + 2)
                    dve.wait_ge(S.mq_hi, u + 1)
                    tile_ = cat_tile(layer, KT + j)
                    sub(act_lo[:, tile_, :], psum(D[1]), hi(tile_)).then_inc(S.mq_lo, 1)

            delta(DN_HEADS - 1, lambda j: mem_raw(0, 0) if j == 0 else None)
            mem_attention(0)

            def residual(name, gain, r, last):
                def body(i):
                    for j in range(2):
                        k = 2 * i + j
                        dve.wait_ge(S.block_used, 4 * i + BLOCK0[name] + 2 * j + 2)
                        V.tensor_tensor(xT[:, k, :], xT[:, k, :], psum(j), ALU.add
                                        ).then_inc(S.acc_free, 1)
                        if last:
                            continue
                        q = KT * r + k
                        dve.wait_ge(S.r_sq, q + 1)
                        if due(q):
                            dve.wait_ge(S.r_acc, q)
                        if isinstance(k, int) and k == 0:
                            if due(r):
                                dve.wait_ge(S.r_ss, r)
                            cp(w(SQ_T), w(13 + j)).then_inc(S.r_acc, 1)
                        else:
                            V.tensor_tensor(w(SQ_T), w(SQ_T), w(13 + j), ALU.add).then_inc(S.r_acc, 1)
                        dve.wait_ge(S.r_hi, q + 1)
                        stt(act_lo[:, H_NEXT[name] + k, :], xT[:, k, :], gain(k), hi(H_NEXT[name] + k),
                            ALU.mult, ALU.subtract).then_inc(S.r_lo, 1)
                turns(dve, KT // 2, body)

            def ffn(layer):
                for half in range(2):
                    c = BLOCK0[f"up{layer}{half}"]

                    def pair(it, j):
                        f = HALF * (2 * layer + half) + 2 * it + j
                        dve.wait_ge(S.block_used, 4 * it + c + 2 * j + 1)
                        dve.wait_ge(S.r_done, 2 * layer + 1)
                        if due(f - 1):
                            dve.wait_ge(S.f_silu, f - 1)
                        mul(w(j % 2), psum(0), w(R_T)).then_inc(S.acc_free, 1)
                        dve.wait_ge(S.block_used, 4 * it + c + 2 * j + 2)
                        mul(w(4 + j % 2), psum(1), w(R_T)).then_inc(S.acc_free, 1)
                        dve.wait_ge(S.f_silu, f + 1)
                        dve.wait_ge(S.acc_free, 4 * it + TILE0[f"up{layer}{half}"] + 2 * j + 2)
                        if due(f - 1):
                            dve.wait_ge(S.f_lo, f - 1)
                        mul(w(6 + j % 2), w(4 + j % 2), w(2 + j % 2)).then_inc(S.f_hid, 1)
                        dve.wait_ge(S.f_hi, f + 1)
                        tile_ = hid_tile(layer, it, j)
                        sub(act_lo[:, tile_, :], w(6 + j % 2), hi(tile_)).then_inc(S.f_lo, 1)

                    def body(it):
                        pair(it, 0)
                        pair(it, 1)
                    turns(dve, 4, body)
                    for j in range(8, HALF):
                        pair(0, j)
                    nxt = None if half == 0 or layer == 1 else (lambda k: col_k("kv_norm", k))
                    residual(f"down{layer}{half}", nxt, 1, nxt is None)

            residual("out0", lambda k: col_k("ffn0", k), 0, False)
            ffn(0)

            V.memset(kwin[:, :, 0:SW_DIM], 0.0).then_inc(S.kv_done, 1)
            for k in range(KT):
                dve.wait_ge(S.b_hi, k + 1)
                stt(act_lo[:, KT + k, :], xT[:, k, :], col("b_norm", k), hi(KT + k), ALU.mult, ALU.subtract
                    ).then_inc(S.b_lo, 1)
            dve.wait_ge(S.r_done, 2)
            dve.wait_ge(S.block_used, BLOCK0["kv"] + 1)
            mul(w(2), psum(0), w(R_T)).then_inc(S.acc_free, 1)
            dve.wait_ge(S.kv_ss, 1)
            cp(st[:, 12:16], bank[:, D[1], 0:NT]).then_inc(S.kv_r, 1)
            dve.wait_ge(S.block_used, BLOCK0["kv"] + 2)
            dve.wait_ge(S.kv_r, 1)
            mul(w4(V_T), psum4(1), st[:, 12:16].unsqueeze(2).to_broadcast([P, NT, P])).then_inc(S.acc_free, 1)
            dve.wait_ge(S.kv_rstd, 1)
            dve.wait_ge(S.acc_free, TILE0["kv"] + 1)
            stt(w(KN_T), w(2), col("k_norm"), w(4), ALU.mult, ALU.mult).then_inc(S.kv_n, 1)
            dve.wait_ge(S.kv_n, 1)
            for g in range(SW_KV):
                rows_ = slice(SW_DIM * g, SW_DIM * (g + 1))
                cp(kwin[rows_, g, SW_DIM:], ws[rows_, KN_T, :]).then_inc(S.kv_done, 1)

            def sw_raw(u):
                if u >= SW_HEADS // QPB:
                    if u == SW_HEADS // QPB:
                        mem_raw(1, 0)
                    return
                dve.wait_ge(S.block_used, BLOCK0["swq"] + u + 1)
                if due(u):
                    dve.wait_ge(S.sw_q, u)
                mul(w(0), psum(u % 2), w(R_T)).then_inc(S.acc_free, 1)

            def sw_normed(u):
                dve.wait_ge(S.sw_rstd, u + 1)
                dve.wait_ge(S.acc_free, TILE0["swq"] + u + 1)
                if due(2 * u):
                    dve.wait_ge(S.sw_sc, 2 * u)
                stt(w(3), w(0), col("q_norm"), w(2), ALU.mult, ALU.mult).then_inc(S.sw_q, 1)

            sw_raw(0)
            sw_normed(0)
            dve.wait_ge(S.dist_loaded, 16)
            dve.wait_ge(S.kv_dup, 32)
            for e in range(QPB):
                V.memset(swp(e)[:, :, 0:SW_DIM], 0.0).then_inc(S.kv_done, 1)
                V.memset(ws[:, PT_PREV[e], 0:P], 0.0).then_inc(S.kv_done, 1)
            sw_raw(1)
            for u in range(SW_HEADS // QPB):
                for e in range(QPB):
                    n = 2 * u + e
                    dve.wait_ge(S.sw_sc, n + 1)
                    if due(n - 1):
                        dve.wait_ge(S.sw_tr, n - 1)
                    scores = bank[:, D[0] + 2 * e:D[0] + 2 * e + 2, :].rearrange("p a (b c) -> p (a b) c", b=2)
                    stt(swp(e)[:, :, SW_DIM:], distance, col("nslope", n), scores[:, :, 0:WIN],
                        ALU.mult, ALU.add).then_inc(S.sw_s, 1)
                    dve.wait_ge(S.sw_s, n + 1)
                    V.tensor_reduce(st[:, 24 + 4 * e:28 + 4 * e], swp(e)[:, :, SW_DIM:], AX.X, ALU.max
                                    ).then_inc(S.sw_mx, 1)
                    dve.wait_ge(S.sw_mx, n + 1)
                    if due(2 * n - 2):
                        dve.wait_ge(S.sw_den, 2 * n - 2)
                    V.tensor_scalar(st[:, 36 + 4 * e:40 + 4 * e], st[:, 24 + 4 * e:28 + 4 * e], col("sinks", n), -1.0,
                                    ALU.max, ALU.mult).then_inc(S.sw_nm, 1)
                if u + 1 < SW_HEADS // QPB:
                    sw_normed(u + 1)
                for e in range(QPB):
                    n = 2 * u + e
                    den = st[:, 44 + 4 * e:48 + 4 * e]
                    dve.wait_ge(S.sw_exp, (NT + 1) * (n + 1))
                    V.tensor_tensor(den, den, st[:, 52 + 4 * e:56 + 4 * e], ALU.add).then_inc(S.sw_den, 1)
                    dve.wait_ge(S.sw_den, 2 * n + 1)
                    V.reciprocal(den, den).then_inc(S.sw_den, 1)
                    dve.wait_ge(S.sw_den, 2 * n + 2)
                    mul(swp(e)[:, :, SW_DIM:], swp(e)[:, :, SW_DIM:], den.unsqueeze(2).to_broadcast([P, NT, WIN])).then_inc(S.sw_p, 1)
                for e in range(QPB):
                    n = 2 * u + e
                    dve.wait_ge(S.sw_tr, n + 1)
                    if due(n - 1):
                        dve.wait_ge(S.sw_o, n - 1)
                    cp(ws[:, PT_PREV[e], P:], bank[:, D[1] + 2 * e, P:]).then_inc(S.sw_ptp, 1)
                sw_raw(u + 2)
                dve.wait_ge(S.sw_o_hi, u + 1)
                sub(act_lo[:, u, :], psum(D[5]), hi(u)).then_inc(S.sw_o_lo, 1)

            mem_attention(1)
            residual("out1", lambda k: col_k("ffn1", k), 2, False)
            ffn(1)
            for t in range(NT):
                dve.wait_ge(S.fin_tr, t + 1)
                cp(ws[:, 2 * t:2 * t + 2, :], bank[:, D[0]:D[0] + 2, :]).then_inc(S.fin_done, 1)


def kernel(x, mem, a_norm, a_w_in, a_conv, a_A_log, a_dt_bias, a_out_norm, a_w_out, kv_norm, w_kv, k_norm, b_norm,
           b_w_in, b_q_norm, b_sinks, b_w_out, mem_norm, w_mem_kv, mem_q_norm, mem_k_norm, ffn_norm, w_gate_up, w_down):
    import concourse.bacc as bacc
    from concourse.bass_utils import run_bass_kernel_spmd

    f = np.asarray

    def tiles(m):
        m = f(m)
        k, n = m.shape
        return m.reshape(k // P, P, n // P, P).transpose(2, 1, 0, 3).reshape(n // P, P, k)

    w_in, b_in = f(a_w_in)[0], f(b_w_in)[0]
    heads = w_in[:, :4 * DN_W]
    qkvz = tiles(heads).reshape(4, DN_HEADS, P, D_MODEL).transpose(1, 0, 2, 3).reshape(4 * DN_HEADS, P, D_MODEL)
    ba = w_in[:, 4 * DN_W:4 * DN_W + 2 * DN_HEADS].reshape(KT, P, 16).transpose(1, 0, 2).reshape(P, KT * 16)
    mem_kv = [tiles(f(w_mem_kv)[i]).reshape(2, MEM_HEADS, P, D_MODEL).transpose(1, 0, 2, 3).reshape(-1, P, D_MODEL)
              for i in range(2)]
    ups = [tiles(f(w_gate_up)[i]).reshape(2, 2, HALF, P, D_MODEL).transpose(1, 2, 0, 3, 4).reshape(-1, P, D_MODEL)
           for i in range(2)]
    stream = np.concatenate([mem_kv[0], mem_kv[1], qkvz, tiles(w_in[:, 4 * DN_W + 2 * DN_HEADS:]), ups[0],
                             tiles(w_kv), tiles(b_in), ups[1]])
    outs = np.stack([tiles(f(a_w_out)[0]), tiles(f(b_w_out)[0])])
    downs = np.concatenate([np.stack([tiles(m) for m in f(w_down)[i].reshape(2, HALF * P, D_MODEL)])
                            for i in range(2)])

    def per_tile(v):
        return f(v).reshape(-1, P).T

    def everywhere(v):
        return np.broadcast_to(f(v).reshape(1, -1), (P, f(v).size))

    conv = f(a_conv)[0].reshape(4, 3, DN_HEADS, P).transpose(3, 2, 1, 0).reshape(P, -1)
    slopes = -np.exp2(-8.0 * np.arange(1, SW_HEADS + 1) / SW_HEADS).astype(np.float32)
    cols = np.concatenate(
        [per_tile(f(a_norm)[0]), per_tile(f(ffn_norm)[0]), per_tile(kv_norm), per_tile(f(b_norm)[0]),
         per_tile(f(ffn_norm)[1]), per_tile(f(mem_norm)[0]), per_tile(f(mem_norm)[1]), per_tile(f(a_out_norm)[0]),
         per_tile(f(mem_q_norm)[0]), per_tile(f(mem_q_norm)[1]), per_tile(f(mem_k_norm)[0]),
         per_tile(f(mem_k_norm)[1]), per_tile(np.concatenate([f(k_norm)] * 2)),
         per_tile(np.concatenate([f(b_q_norm)[0]] * 2)), conv, everywhere(a_A_log), everywhere(a_dt_bias),
         everywhere(b_sinks), everywhere(slopes),
         everywhere(np.array([EPS, -0.5 * math.log(P), -0.5 * math.log(SW_DIM)], np.float32))], axis=1)
    arrays = {
        "x_in": f(x)[0], "mem_in": f(mem)[0], "w_stream": stream, "w_out": outs, "w_down": downs, "w_ba": ba,
        "cols_in": cols, "squares_in": squares(), "dist_in": distances(),
    }
    arrays = {n: np.ascontiguousarray(a_) for n, a_ in arrays.items()}
    nc = bacc.Bacc("TRN2", target_bir_lowering=False, num_devices=1)
    args = [nc.dram_tensor(n, a_.shape, F32, kind="ExternalInput").ap() for n, a_ in arrays.items()]
    out = nc.dram_tensor("out", (SEQ, D_MODEL), F32, kind="ExternalOutput").ap()
    yoco_kernel(nc, *args, out)
    r = run_bass_kernel_spmd(nc, [arrays], core_ids=[0])
    return r.results[0]["out"].reshape(1, SEQ, D_MODEL)
```

```python
import math
from contextlib import ExitStack

import numpy as np

import concourse.bass as bass
from concourse import mybir

F32 = mybir.dt.float32
F32R = mybir.dt.float32r
ALU = mybir.AluOpType
ACT = mybir.ActivationFunctionType
AX = mybir.AxisListType

P = 128
D_MODEL = 1024
SEQ = 512
MEM_LEN = 256
DN_HEADS = 8
DN_W = DN_HEADS * P
MEM_HEADS = 4
MEM_W = MEM_HEADS * P
SW_HEADS = 16
SW_DIM = 64
SW_KV = 2
D_FF = -(-8 * D_MODEL // (3 * 256)) * 256
EPS = 1e-6

KT = D_MODEL // P
NT = SEQ // P
MT_ = MEM_LEN // P
CAT = (DN_W + MEM_W) // P
HALF = D_FF // P // 2
WIN = 3 * SW_DIM
LEVELS = 7
QPB = P // SW_DIM

_order = [("mem0", 2 * MEM_HEADS), ("mem1", 2 * MEM_HEADS), ("dn", 4 * DN_HEADS), ("mq0", MEM_HEADS),
          ("out0", 2 * KT), ("up00", 2 * HALF), ("down00", 2 * KT), ("up01", 2 * HALF), ("down01", 2 * KT),
          ("kv", 2), ("swq", SW_HEADS // QPB), ("mq1", MEM_HEADS), ("out1", 2 * KT),
          ("up10", 2 * HALF), ("down10", 2 * KT), ("up11", 2 * HALF), ("down11", 2 * KT)]
BLOCK0, TILE0 = {}, {}
_b = _n = 0
for _name, _count in _order:
    BLOCK0[_name], TILE0[_name] = _b, _n
    _b += _count
    _n += _count // 2 if _name.startswith(("out", "down")) else _count
N_BLOCKS, N_TILES = _b, _n
LAST = _order[-1][0]
OUT_SUB = (CAT // 2, CAT // 2)
DOWN_SUB = ((HALF + 1) // 2, HALF // 2)
RING = 4


def subtiles(block):
    for name, count in _order:
        if BLOCK0[name] <= block < BLOCK0[name] + count:
            half = (block - BLOCK0[name]) % 2
            return OUT_SUB[half] if name.startswith("out") else DOWN_SUB[half] if name.startswith("down") else KT
    raise ValueError(block)


COLS = {}
_c = 0
for _name, _count in [("a_norm", KT), ("ffn0", KT), ("kv_norm", KT), ("b_norm", KT), ("ffn1", KT), ("mem0", KT),
                      ("mem1", KT), ("out_norm", 1), ("mq0", 1), ("mq1", 1), ("mk0", 1), ("mk1", 1), ("k_norm", 1),
                      ("q_norm", 1), ("conv", DN_HEADS * 3 * 4), ("a_log", DN_HEADS), ("dt", DN_HEADS),
                      ("sinks", SW_HEADS), ("nslope", SW_HEADS), ("eps", 1), ("ln_q", 1), ("ln_s", 1)]:
    COLS[_name] = _c
    _c += _count
N_COLS = _c

(IDENT, ONES, ONES64, TRIU, NEG_LOWER, LEVEL0) = range(6)
N_SQ = 6 + LEVELS - 1


def squares():
    r, c = np.arange(P)[:, None], np.arange(P)[None, :]
    out = np.zeros((P, N_SQ, P), np.float32)
    out[:, IDENT] = r == c
    out[:, ONES] = 1.0
    out[:, ONES64] = r // SW_DIM == c // SW_DIM
    out[:, TRIU] = r <= c
    out[:, NEG_LOWER] = np.where(r <= c, 0.0, -1e30)
    out[:, LEVEL0] = (c == r + 1) & (r % 2 == 0)
    for k in range(1, LEVELS):
        b = 2 ** k
        out[:, LEVEL0 + k] = (r // b % 2 == 1) & (c // b == r // b - 1)
    return out


def distances():
    i, j = np.arange(P)[:, None], np.arange(WIN)[None, :]
    d = np.abs(i + SW_DIM - j).astype(np.float32)
    d = np.where((j // SW_DIM >= i // SW_DIM) & (j // SW_DIM <= i // SW_DIM + 1), d, 1e30)
    out = np.repeat(d[:, None, :], NT, axis=1)
    out[:, 0, :SW_DIM] = 1e30
    return out.astype(np.float32)


KR, KS, KRS = 14, 18, 15
(CQ, CK, CV, SZ, QN, KN, TT, ZZ, AT, MM, PM, DD, EG, VB, KBG, KDEC, E0, E1, EC) = range(19)
WS = 19


def yoco_kernel(nc, x, mem, w_stream, w_out, w_down, w_ba, cols_in, squares_in, dist_in, out):
    with ExitStack() as ctx:
        def sb(name, shape, dt=F32):
            return ctx.enter_context(nc.sbuf_tensor(name, shape, dt))

        def sem(name):
            return ctx.enter_context(nc.semaphore(name))

        xT = sb("xT", [P, KT, SEQ])
        act_hi = sb("act_hi", [P, KT + CAT, SEQ], F32R)
        act_lo = sb("act_lo", [P, KT + CAT, SEQ], F32R)
        w_raw = sb("w_raw", [P, RING, KT * P])
        w_hi = sb("w_hi", [P, RING, KT * P], F32R)
        w_lo = sb("w_lo", [P, RING, KT * P], F32R)
        ws = sb("ws", [P, WS, SEQ])
        kmem = sb("kmem", [P, 2 * MEM_HEADS, MEM_LEN])
        vmem = sb("vmem", [P, 2 * MEM_HEADS, MT_ * P])
        sq_c = sb("sq_c", [P, N_SQ, P])
        cols = sb("cols", [P, N_COLS])
        dn_s = sb("dn_s", [P, 8, DN_HEADS * NT])
        state = sb("state", [P, P])
        st = sb("st", [P, 64])

        bank = ctx.enter_context(nc.psum_tensor("bank", [P, 8, 512], F32))

        class S:
            consts_loaded = sem("consts_loaded")
            cols_loaded = sem("cols_loaded")
            dist_loaded = sem("dist_loaded")
            x_loaded = sem("x_loaded")
            mem_loaded = sem("mem_loaded")
            mem_rest_loaded = sem("mem_rest_loaded")
            ba_loaded = sem("ba_loaded")
            hi_done = sem("hi_done")
            lo_done = sem("lo_done")
            block_used = sem("block_used")
            acc_free = sem("acc_free")
            m_sq = sem("m_sq")
            m_ln = sem("m_ln")
            m_rstd = sem("m_rstd")
            m_scaled = sem("m_scaled")
            m_tr = sem("m_tr")
            m_evac_hi = sem("m_evac_hi")
            m_evac_lo = sem("m_evac_lo")
            x_sq = sem("x_sq")
            x_ln = sem("x_ln")
            x_rstd = sem("x_rstd")
            x_scaled = sem("x_scaled")
            x_raw_tr = sem("x_raw_tr")
            x_raw_copied = sem("x_raw_copied")
            x_tr = sem("x_tr")
            x_evac_hi = sem("x_evac_hi")
            x_evac_lo = sem("x_evac_lo")
            mk_sq = sem("mk_sq")
            mk_ss = sem("mk_ss")
            mk_ln = sem("mk_ln")
            mk_rstd = sem("mk_rstd")
            mk_done = sem("mk_done")
            mv_tr = sem("mv_tr")
            mv_done = sem("mv_done")
            ba_hi = sem("ba_hi")
            ba_split = sem("ba_split")
            ba_raw = sem("ba_raw")
            ba_copied = sem("ba_copied")
            ba_mm = sem("ba_mm")
            ba_dve = sem("ba_dve")
            ba_act = sem("ba_act")
            ba_g = sem("ba_g")
            ba_cum = sem("ba_cum")
            cv_tap = sem("cv_tap")
            cv_conv = sem("cv_conv")
            c_ready = sem("c_ready")
            sz_done = sem("sz_done")
            sq_done = sem("sq_done")
            ss_done = sem("ss_done")
            rr_ln = sem("rr_ln")
            rr_done = sem("rr_done")
            qn_done = sem("qn_done")
            kn_done = sem("kn_done")
            ug_done = sem("ug_done")
            gb_done = sem("gb_done")
            eg_done = sem("eg_done")
            dm_pre = sem("dm_pre")
            dm_done = sem("dm_done")
            kb_done = sem("kb_done")
            vtr_done = sem("vtr_done")
            ktr_done = sem("ktr_done")
            vb_done = sem("vb_done")
            kbg_done = sem("kbg_done")
            kdec_done = sem("kdec_done")
            qd_done = sem("qd_done")
            gg_done = sem("gg_done")
            at_done = sem("at_done")
            mt_done = sem("mt_done")
            z_pre = sem("z_pre")
            z_done = sem("z_done")
            t_tr = sem("t_tr")
            t_done = sem("t_done")
            p_mm = sem("p_mm")
            p_done = sem("p_done")
            tz_mm = sem("tz_mm")
            tz_done = sem("tz_done")
            nw_mm = sem("nw_mm")
            nw_done = sem("nw_done")
            v_mm = sem("v_mm")
            v_done = sem("v_done")
            s_mm = sem("s_mm")
            s_done = sem("s_done")
            o_done = sem("o_done")
            osq = sem("osq")
            oss = sem("oss")
            o_ln = sem("o_ln")
            o_rstd = sem("o_rstd")
            o_t1 = sem("o_t1")
            o_t2 = sem("o_t2")
            o_hi = sem("o_hi")
            o_lo = sem("o_lo")
            mq_sq = sem("mq_sq")
            mq_ss = sem("mq_ss")
            mq_ln = sem("mq_ln")
            mq_rstd = sem("mq_rstd")
            mq_n = sem("mq_n")
            mq_sc = sem("mq_sc")
            mq_max = sem("mq_max")
            mq_exp = sem("mq_exp")
            mq_rcp = sem("mq_rcp")
            mq_p = sem("mq_p")
            mq_tr = sem("mq_tr")
            mq_pt = sem("mq_pt")
            mq_o = sem("mq_o")
            mq_hi = sem("mq_hi")
            mq_lo = sem("mq_lo")
            r_hi = sem("r_hi")
            r_lo = sem("r_lo")
            r_sq = sem("r_sq")
            r_acc = sem("r_acc")
            r_ss = sem("r_ss")
            r_ln = sem("r_ln")
            r_done = sem("r_done")
            f_silu = sem("f_silu")
            f_hid = sem("f_hid")
            f_hi = sem("f_hi")
            f_lo = sem("f_lo")
            kv_sq = sem("kv_sq")
            kv_ss = sem("kv_ss")
            kv_ln = sem("kv_ln")
            kv_rstd = sem("kv_rstd")
            kv_n = sem("kv_n")
            kv_dup = sem("kv_dup")
            kv_done = sem("kv_done")
            kv_vt = sem("kv_vt")
            b_hi = sem("b_hi")
            b_lo = sem("b_lo")
            sw_sq = sem("sw_sq")
            sw_ss = sem("sw_ss")
            sw_ln = sem("sw_ln")
            sw_rstd = sem("sw_rstd")
            sw_q = sem("sw_q")
            sw_sc = sem("sw_sc")
            sw_s = sem("sw_s")
            sw_mx = sem("sw_mx")
            sw_nm = sem("sw_nm")
            sw_exp = sem("sw_exp")
            sw_den = sem("sw_den")
            sw_p = sem("sw_p")
            sw_tr = sem("sw_tr")
            sw_pt = sem("sw_pt")
            sw_ptp = sem("sw_ptp")
            sw_o = sem("sw_o")
            sw_o_hi = sem("sw_o_hi")
            sw_o_lo = sem("sw_o_lo")
            fin_tr = sem("fin_tr")
            fin_done = sem("fin_done")

        raw_loaded = [sem(f"raw_loaded{i}") for i in range(RING)]
        stored = sem("stored")

        block = ctx.enter_context(nc.Block())

        def due(n):
            return not isinstance(n, int) or n > 0

        def at_once(eng):
            eng.wait_ge(S.consts_loaded, 16)

        def turns(eng, n, body):
            body(0)
            if n > 3:
                with eng.Fori(1, n - 1) as i:
                    body(i)
            elif n == 3:
                body(1)
            if n > 1:
                body(n - 1)

        def w(i):
            return ws[:, i, :]

        def w4(i):
            return ws[:, i, :].rearrange("p (t c) -> p t c", t=NT)

        def sq(i):
            return sq_c[:, i, :]

        def over_tiles(i):
            return sq_c[:, i:i + 1, :].to_broadcast([P, NT, P])

        def col(name, i=0):
            return cols[:, COLS[name] + i:COLS[name] + i + 1]

        def psum(b, n=512):
            return bank[:, b, 0:n]

        def psum4(b):
            return bank[:, b, :].rearrange("p (t c) -> p t c", t=NT)

        def tt(i, t):
            return ws[:, i, t * P:(t + 1) * P]

        result = ws[:, 0:8, :].rearrange("p (t a) c -> p t (a c)", t=NT)
        STORES = ((0, KT // 2), (KT // 2, KT - 1), (KT - 1, KT))

        D = [2, 3, 4, 5, 6, 7]

        MEM_ORDER = [*range(0, KT, 2), *range(1, KT, 2)]

        def mem_ps(k):
            return bank[:, D[k // 2], (k % 2) * MEM_LEN:(k % 2 + 1) * MEM_LEN]

        raw_values = ws[:, KR, MEM_LEN:]

        BETA, GG, GCUM, GL, EDEC, NBEG, TMP1, TMP2 = range(8)

        def dn(i):
            return dn_s[:, i, :].rearrange("p (h t) -> p h t", h=DN_HEADS)

        def dn_bcast(i, h):
            return dn(i)[:, h, :].unsqueeze(2).to_broadcast([P, NT, P])

        kwin = ws[:, 8:11, :].rearrange("p t c -> p (t c)")[:, 0:SW_KV * (SW_DIM + SEQ)].rearrange(
            "p (g c) -> p g c", g=SW_KV)
        V_T, PT_OWN, PT_PREV, R_T, SQ_T, KN_T, V_F = 11, (12, 13), (14, 15), 16, 15, 5, 6

        def swp(e):
            return ws[:, 4 + 2 * e:6 + 2 * e, :].rearrange("p a (t c) -> p (a t) c", c=2 * P)

        distance = ws[:, 17:19, :].rearrange("p t c -> p (t c)")[:, 0:NT * WIN].rearrange("p (t c) -> p t c", t=NT)
        ba_w = sb("ba_w", [P, 2, KT * 16], F32R)

        H_AT = (0, KT)

        H_NEXT = {"out0": 0, "down01": 0, "out1": KT}

        def col_k(name, k):
            return cols[:, bass.ds(k + COLS[name], 1)]

        def conv_w(h, j, tap):
            return cols[:, bass.ds(12 * h + (COLS["conv"] + 4 * j + tap), 1)]

        def hid_tile(layer, it, j):
            if layer == 0:
                return 2 * it + j + KT
            return 2 * it + j if j < 8 else KT + j

        def mq_p_of(t):
            return ws[:, 4 + t // 2, (t % 2) * MEM_LEN:(t % 2 + 1) * MEM_LEN]

        def cat_tile(layer, k):
            return KT + k if layer == 0 else (k if k < KT else KT + k)

        @block.sync
        def _(sp):
            sp.dma_start(ws[:, 8:10, :].rearrange("p t c -> p (t c)"), mem[0:P, :]).then_inc(S.mem_loaded, 16)
            sp.dma_start(cols[:], cols_in).then_inc(S.cols_loaded, 16)
            sp.dma_start(ws[:, 10:12, :].rearrange("p t c -> p (t c)"), mem[P:2 * P, :]).then_inc(S.mem_rest_loaded, 16)
            sp.dma_start(sq_c[:], squares_in).then_inc(S.consts_loaded, 16)

            sp.dma_start(ws[:, E0, 0:KT * 16], w_ba).then_inc(S.ba_loaded, 16)

            def load(it, c, source, width):
                b = 4 * it + c
                if due(b - RING + 1):
                    sp.wait_ge(S.hi_done, b - RING + 1)
                if due(b - RING + 1):
                    sp.wait_ge(S.lo_done, b - RING + 1)
                sp.dma_start(w_raw[:, c % RING, 0:width * P], source).then_inc(raw_loaded[c % RING], 16)

            def load_plain(name, base_row, count):
                b0 = BLOCK0[name]

                def body(i):
                    for j in range(4):
                        load(i, b0 + j, w_stream[base_row + 4 * i + j], KT)
                if count >= 4:
                    turns(sp, count // 4, body)
                for j in range(count // 4 * 4, count):
                    load(0, b0 + j, w_stream[base_row + j], KT)

            def load_pairs(name, array, sub):
                b0 = BLOCK0[name]

                def body(i):
                    for j in range(4):
                        lo = (j % 2) * sub[0] * P
                        load(i, b0 + j, array[2 * i + j // 2, :, lo:lo + sub[j % 2] * P], sub[j % 2])
                turns(sp, KT // 2, body)

            row = 0
            for name, count in _order:
                if name.startswith("out"):
                    load_pairs(name, w_out[int(name[3])], OUT_SUB)
                elif name.startswith("down"):
                    load_pairs(name, w_down[2 * int(name[4]) + int(name[5])], DOWN_SUB)
                else:
                    load_plain(name, row, count)
                    row += count
                if name == "mem0":
                    sp.dma_start(ws[:, 0:8, :].rearrange("p t c -> p (t c)"),
                                 x.rearrange("(t p) d -> p t d", p=P)).then_inc(S.x_loaded, 16)
                if name == "kv":
                    sp.dma_start(ws[:, 17:19, :].rearrange("p t c -> p (t c)")[:, 0:NT * WIN],
                                 dist_in.rearrange("p t c -> p (t c)")).then_inc(S.dist_loaded, 16)
            for first, end in STORES:
                sp.wait_ge(S.fin_done, end)
                sp.dma_start(out.rearrange("(t p) d -> p t d", p=P)[:, :, first * P:end * P],
                             result[:, :, first * P:end * P]).then_inc(stored, 16)
            sp.wait_ge(stored, 16 * len(STORES))

        @block.gpsimd
        def _(pool):
            def lower(it, c, width):
                pool.wait_ge(S.hi_done, 4 * it + c + 1)
                s = c % RING
                nc.gpsimd.tensor_tensor(w_lo[:, s, 0:width * P], w_raw[:, s, 0:width * P],
                                        w_hi[:, s, 0:width * P].bitcast(F32), ALU.subtract).then_inc(S.lo_done, 1)

            def lower_all(name, count):
                b0 = BLOCK0[name]
                if count >= 4:
                    turns(pool, count // 4, lambda i: [lower(i, b0 + j, subtiles(b0 + j)) for j in range(4)])
                for j in range(count // 4 * 4, count):
                    lower(0, b0 + j, subtiles(b0 + j))

            def rows_of(h):
                at_once(pool)
                if due(h):
                    pool.wait_ge(S.nw_mm, h)
                pool.wait_ge(S.ba_g, 1)
                nc.gpsimd.tensor_tensor(w4(KBG), over_tiles(TRIU), dn_bcast(GG, h), ALU.mult).then_inc(S.ug_done, 1)
                at_once(pool)
                if due(h):
                    pool.wait_ge(S.o_done, h)
                pool.wait_ge(S.ba_dve, 4)
                nc.gpsimd.tensor_tensor(w4(KDEC), over_tiles(IDENT), dn_bcast(BETA, h), ALU.mult).then_inc(S.ug_done, 1)

            def o_lower(h):
                at_once(pool)
                pool.wait_ge(S.o_hi, h + 1)
                nc.gpsimd.tensor_tensor(act_lo[:, h + KT, :], w(MM), act_hi[:, h + KT, :].bitcast(F32),
                                        ALU.subtract).then_inc(S.o_lo, 1)

            def delta(h, following):
                if due(h):
                    o_lower(h - 1)
                pool.wait_ge(S.eg_done, h + 1)
                pool.wait_ge(S.qn_done, h + 1)
                nc.gpsimd.tensor_tensor(w(EG), w(EG), w(QN), ALU.mult).then_inc(S.qd_done, 1)
                if following:
                    for j in range(4):
                        lower(h + 1, BLOCK0["dn"] + j + 2, KT)
                    rows_of(h + 1)

            lower_all("mem0", 8)
            lower_all("mem1", 8)
            dn0 = BLOCK0["dn"]
            for j in range(6):
                lower(0, dn0 + j, KT)
            rows_of(0)
            turns(pool, DN_HEADS - 1, lambda h: delta(h, True))
            delta(DN_HEADS - 1, False)
            o_lower(DN_HEADS - 1)
            for j in range(2, MEM_HEADS):
                lower(0, BLOCK0["mq0"] + j, KT)
            for name, count in _order[4:]:
                lower_all(name, count)

        @block.tensor
        def _(pe):
            def product(it, c, nsub, k0, act0, acc, start, stop, n=SEQ, off=0, ks=None):
                ks = range(nsub) if ks is None else ks
                if ks[0] == 0:
                    pe.wait_ge(S.lo_done, 4 * it + c + 1)
                for k in ks:
                    wsl = slice(k * P, (k + 1) * P)
                    for m, (wt, at) in enumerate(((w_hi, act_hi), (w_hi, act_lo), (w_lo, act_hi))):
                        mm = nc.tensor.matmul(acc, wt[:, c % RING, wsl], at[:, act0(k0 + k), off:off + n],
                                              start=(start and k == 0 and m == 0),
                                              stop=(stop and k == nsub - 1 and m == 2))
                if ks[-1] == nsub - 1:
                    mm.then_inc(S.block_used, 1)

            def acc_ready(n):
                if due(n - 1):
                    pe.wait_ge(S.acc_free, n - 1)

            def transposes4(dst, source):
                for t in range(NT):
                    mm = nc.tensor.transpose(bank[:, dst, t * P:(t + 1) * P], tt(source, t), sq(IDENT))
                return mm

            pe.wait_ge(S.consts_loaded, 16)
            pe.wait_ge(S.m_scaled, MT_)
            for k in range(KT):
                for t in range(MT_):
                    mm = nc.tensor.transpose(mem_ps(k)[:, t * P:(t + 1) * P],
                                             ws[:, 8 + 2 * t:10 + 2 * t, :].rearrange("p a c -> p (a c)")[
                                                 :, k * P:(k + 1) * P], sq(IDENT))
                mm.then_inc(S.m_tr, 1)

            def key_sums(head):
                pe.wait_ge(S.mk_sq, head + 1)
                if due(head):
                    pe.wait_ge(S.mk_ln, head)
                nc.tensor.matmul(psum(D[4], MEM_LEN), sq(ONES), w(KS)[:, 0:MEM_LEN],
                                 start=True, stop=True).then_inc(S.mk_ss, 1)

            def mem_proj(layer):
                b0, n0 = BLOCK0[f"mem{layer}"], TILE0[f"mem{layer}"]
                pe.wait_ge(S.m_evac_lo, KT * (layer + 1))
                for j in range(MEM_HEADS):
                    head = j + MEM_HEADS * layer
                    for part in range(2):
                        acc_ready(n0 + 2 * j + part)
                        product(0, b0 + 2 * j + part, KT, 0, lambda k: KT + k, psum(part, MEM_LEN), True, True,
                                n=MEM_LEN, off=MEM_LEN * layer)
                        if part == 0 and j > 0:
                            key_sums(head - 1)
                    pe.wait_ge(S.acc_free, n0 + 2 * j + 1)
                    if due(head):
                        pe.wait_ge(S.mv_done, head)
                    for t in range(MT_):
                        mm = nc.tensor.transpose(bank[:, D[5], t * P:(t + 1) * P], raw_values[:, t * P:(t + 1) * P],
                                                 sq(IDENT))
                    mm.then_inc(S.mv_tr, 1)
                key_sums(MEM_HEADS * (layer + 1) - 1)

            mem_proj(0)

            def x_transposes(k):
                for t in range(NT):
                    mm = nc.tensor.transpose(bank[:, D[k % 4], t * P:(t + 1) * P],
                                             ws[:, 2 * t:2 * t + 2, :].rearrange("p a c -> p (a c)")[
                                                 :, k * P:(k + 1) * P], sq(IDENT))
                return mm
            pe.wait_ge(S.x_loaded, 16)
            pe.wait_ge(S.m_evac_lo, 2 * KT)
            for k in range(KT):
                if due(k - 3):
                    pe.wait_ge(S.x_raw_copied, k - 3)
                x_transposes(k).then_inc(S.x_raw_tr, 1)
            mem_proj(1)
            pe.wait_ge(S.x_scaled, NT)
            pe.wait_ge(S.x_raw_copied, KT)
            for k in range(KT):
                if due(k - 3):
                    pe.wait_ge(S.x_evac_lo, k - 3)
                x_transposes(k).then_inc(S.x_tr, 1)

            pe.wait_ge(S.x_evac_lo, KT)
            pe.wait_ge(S.ba_split, 1)
            for k in range(KT):
                for m, (wi, at) in enumerate(((0, act_hi), (0, act_lo), (1, act_hi))):
                    mm = nc.tensor.matmul(bank[0:16, D[3], :], ba_w[:, wi, k * 16:(k + 1) * 16], at[:, k, :],
                                          start=(k == 0 and m == 0), stop=(k == KT - 1 and m == 2))
            mm.then_inc(S.ba_raw, 1)

            def proj_dn(h, j, ks=range(KT)):
                if ks[0] == 0:
                    acc_ready(TILE0["dn"] + 4 * h + j)
                product(h, BLOCK0["dn"] + j, KT, 0, lambda k: k, psum(j % 2), True, True, ks=ks)

            LEVEL_FILL = (0, 2, 4, 6, 7, 8)

            def half_tiles(g):
                return range(NT // 2 * g, NT // 2 * (g + 1))

            def delta(h, fill):
                pe.wait_ge(S.sq_done, 2 * h + 1)
                if due(h):
                    pe.wait_ge(S.at_done, h)
                nc.tensor.matmul(psum(D[0]), sq(ONES), w(E0), start=True, stop=True).then_inc(S.ss_done, 1)
                pe.wait_ge(S.sq_done, 2 * h + 2)
                nc.tensor.matmul(psum(D[1]), sq(ONES), w(PM), start=True, stop=True).then_inc(S.ss_done, 1)
                pe.wait_ge(S.ug_done, 2 * h + 1)
                if due(h):
                    pe.wait_ge(S.o_ln, h)
                nc.tensor.matmul(psum(D[2]), sq(ONES), w(KBG), start=True, stop=True).then_inc(S.gb_done, 1)
                pe.wait_ge(S.ug_done, 2 * h + 2)
                if due(NT * h):
                    pe.wait_ge(S.v_done, NT * h)
                nc.tensor.matmul(psum(D[3]), sq(ONES), w(KDEC), start=True, stop=True).then_inc(S.gb_done, 1)
                pe.wait_ge(S.c_ready, h + 1)
                if due(3 * h):
                    pe.wait_ge(S.s_done, 3 * h)
                transposes4(D[4], CV).then_inc(S.vtr_done, 1)
                fill(0, range(0, 5))
                pe.wait_ge(S.kn_done, h + 1)
                if due(h):
                    pe.wait_ge(S.o_t1, h)
                transposes4(D[5], KN).then_inc(S.ktr_done, 1)
                fill(0, range(5, 8))
                pe.wait_ge(S.kb_done, h + 1)
                for t in range(NT):
                    mm = nc.tensor.matmul(bank[:, D[1], t * P:(t + 1) * P], tt(KN, t), tt(PM, t), start=True, stop=True)
                mm.then_inc(S.gg_done, 1)
                pe.wait_ge(S.qn_done, h + 1)
                for t in range(NT):
                    mm = nc.tensor.matmul(bank[:, D[0], t * P:(t + 1) * P], tt(KN, t), tt(QN, t), start=True, stop=True)
                mm.then_inc(S.gg_done, 1)
                fill(1, range(0, 6))
                pe.wait_ge(S.z_done, h + 1)
                pe.wait_ge(S.dm_pre, 2 * h + 1)
                transposes4(D[2], ZZ).then_inc(S.t_tr, 1)
                fill(1, range(6, 8))
                for k in range(1, LEVELS):
                    n = 12 * h + 2 * (k - 1)
                    for g in range(2):
                        if k == 1:
                            pe.wait_ge(S.t_done, h + 1)
                        else:
                            pe.wait_ge(S.tz_done, n + g - 1)
                        for i, t in enumerate(half_tiles(g)):
                            mm = nc.tensor.matmul(bank[:, D[3 - g], i * P:(i + 1) * P], tt(MM, t), tt(TT, t),
                                                  start=True, stop=True)
                        mm.then_inc(S.p_mm, 1)
                    if k <= 5:
                        fill(2, range(LEVEL_FILL[k - 1], LEVEL_FILL[k - 1] + 1))
                    for g in range(2):
                        pe.wait_ge(S.p_done, n + g + 1)
                        if k == 1:
                            pe.wait_ge(S.vb_done, h + 1)
                            pe.wait_ge(S.kdec_done, h + 1)
                        for i, t in enumerate(half_tiles(g)):
                            if k < LEVELS - 1:
                                nc.tensor.matmul(bank[:, D[4 + g], i * P:(i + 1) * P], tt(ZZ, t), tt(PM, t),
                                                 start=True, stop=True)
                            mm = nc.tensor.matmul(bank[:, D[4 + g], (2 + i) * P:(3 + i) * P], tt(PM, t), tt(ZZ, t),
                                                  start=True, stop=True)
                        mm.then_inc(S.tz_mm, 1)
                    if k <= 3:
                        fill(2, range(LEVEL_FILL[k - 1] + 1, LEVEL_FILL[k]))
                fill(3, range(0, 1))
                pe.wait_ge(S.tz_done, 12 * h + 12)
                pe.wait_ge(S.kbg_done, h + 1)
                for t in range(NT):
                    mm = nc.tensor.matmul(bank[:, D[2], t * P:(t + 1) * P], tt(KBG, t), tt(ZZ, t), start=True, stop=True)
                mm.then_inc(S.nw_mm, 1)
                pe.wait_ge(S.at_done, h + 1)
                for t in range(NT):
                    n = NT * h + t
                    if due(n):
                        pe.wait_ge(S.v_done, n)
                    v_acc = bank[:, D[3], 0:P]
                    mm = nc.tensor.matmul(v_acc, tt(ZZ, t), tt(VB, t), start=True, stop=(t == 0))
                    if t:
                        pe.wait_ge(S.nw_done, h + 1)
                        pe.wait_ge(S.s_done, 3 * h + t)
                        mm = nc.tensor.matmul(v_acc, tt(MM, t), state[:], start=False, stop=True)
                    mm.then_inc(S.v_mm, 1)
                    o_acc = bank[:, D[5], t * P:(t + 1) * P]
                    pe.wait_ge(S.qd_done, h + 1)
                    if t:
                        nc.tensor.matmul(o_acc, state[:], tt(EG, t), start=True, stop=False)
                    fill(3, range(t + 1, t + 2))
                    pe.wait_ge(S.v_done, n + 1)
                    if t < NT - 1:
                        nc.tensor.matmul(bank[:, D[4], 0:P], tt(KDEC, t), ws[:, E0, t * P:(t + 1) * P],
                                         start=True, stop=True).then_inc(S.s_mm, 1)
                    mm = nc.tensor.matmul(o_acc, ws[:, E0, t * P:(t + 1) * P], tt(AT, t), start=(t == 0), stop=True)
                mm.then_inc(S.o_done, 1)
                fill(3, range(5, 8))
                pe.wait_ge(S.osq, h + 1)
                nc.tensor.matmul(psum(D[2]), sq(ONES), w(E1), start=True, stop=True).then_inc(S.oss, 1)

            proj_dn(0, 0)
            pe.wait_ge(S.ba_copied, 1)
            for t in range(NT):
                mm = nc.tensor.transpose(bank[:, D[0], t * 16:(t + 1) * 16], ws[0:16, E1, t * P:(t + 1) * P],
                                         sq_c[0:16, IDENT, 0:16])
            mm.then_inc(S.ba_mm, 1)
            proj_dn(0, 1)
            pe.wait_ge(S.ba_g, 1)
            nc.tensor.matmul(bank[:, D[1], 0:32], sq(TRIU), dn_s[:, GG, :], start=True, stop=True)
            nc.tensor.matmul(bank[:, D[2], 0:32], sq(ONES), dn_s[:, GG, :], start=True, stop=True
                             ).then_inc(S.ba_cum, 1)
            for j in range(2, 4):
                proj_dn(0, j)
            turns(pe, DN_HEADS - 1, lambda h: delta(h, lambda j, ks: proj_dn(h + 1, j, ks)))

            def mem_project(layer, j, ks):
                name = f"mq{layer}"
                if ks[0] == 0:
                    acc_ready(TILE0[name] + j)
                product(0, BLOCK0[name] + j, KT, 0, lambda k: H_AT[layer] + k, psum(j % 2), True, True, ks=ks)

            def out_ahead(layer, j):
                name = f"out{layer}"
                act_of = (lambda k: cat_tile(layer, k))
                if j == 0:
                    acc_ready(TILE0[name])
                    product(0, BLOCK0[name], OUT_SUB[0], 0, act_of, psum(0), True, False)
                else:
                    product(0, BLOCK0[name] + 1, OUT_SUB[1], OUT_SUB[0], act_of, psum(0), False, True,
                            ks=range(0, KT - OUT_SUB[0]))
                    pe.wait_ge(S.mq_lo, MEM_HEADS * layer + MEM_HEADS - 1)
                    product(0, BLOCK0[name] + 1, OUT_SUB[1], OUT_SUB[0], act_of, psum(0), False, True,
                            ks=range(KT - OUT_SUB[0], OUT_SUB[1] - 1))

            def mem_attention(layer):
                def sums(j):
                    u = layer * MEM_HEADS + j
                    pe.wait_ge(S.mq_sq, u + 1)
                    if due(u):
                        pe.wait_ge(S.mq_ln, u)
                    nc.tensor.matmul(psum(D[0]), sq(ONES), w(2), start=True, stop=True).then_inc(S.mq_ss, 1)

                def scores(j):
                    u = layer * MEM_HEADS + j
                    pe.wait_ge(S.mq_n, u + 1)
                    if due(u):
                        pe.wait_ge(S.mq_p, u)
                    for t in range(NT):
                        mm = nc.tensor.matmul(bank[:, D[2] + t // 2, (t % 2) * MEM_LEN:(t % 2 + 1) * MEM_LEN],
                                              tt(3, t), kmem[:, u, :], start=True, stop=True)
                    mm.then_inc(S.mq_sc, 1)

                sums(0)
                mem_project(layer, 1, range(KT // 2 if layer else 0, KT))
                scores(0)
                for j in range(MEM_HEADS):
                    u = layer * MEM_HEADS + j
                    if j + 1 < MEM_HEADS:
                        sums(j + 1)
                    if j + 2 < MEM_HEADS:
                        mem_project(layer, j + 2, range(0, 7))
                    else:
                        if j + 2 == MEM_HEADS:
                            if layer == 0:
                                pe.wait_ge(S.o_lo, DN_HEADS)
                            else:
                                pe.wait_ge(S.sw_o_lo, SW_HEADS // QPB)
                        out_ahead(layer, j + 2 - MEM_HEADS)
                    pe.wait_ge(S.mq_p, u + 1)
                    if due(u):
                        pe.wait_ge(S.mq_pt, 2 * u)
                    for m in range(MT_):
                        for t in range(NT):
                            p_t = ws[:, 4:6, :].rearrange("p a c -> p (a c)")[
                                :, t * MEM_LEN + m * P:t * MEM_LEN + (m + 1) * P]
                            mm = nc.tensor.transpose(bank[:, D[4] + m, t * P:(t + 1) * P], p_t, sq(IDENT))
                    mm.then_inc(S.mq_tr, 1)
                    if j + 2 < MEM_HEADS:
                        mem_project(layer, j + 2, range(7, KT))
                    pe.wait_ge(S.mq_pt, 2 * u + 2)
                    if due(u):
                        pe.wait_ge(S.mq_lo, u)
                    for m in range(MT_):
                        mm = nc.tensor.matmul(psum(D[1]), vmem[:, u, m * P:(m + 1) * P], w(6 + m),
                                              start=(m == 0), stop=(m == MT_ - 1))
                    mm.then_inc(S.mq_o, 1)
                    if j + 1 < MEM_HEADS:
                        scores(j + 1)

            delta(DN_HEADS - 1, lambda j, ks: mem_project(0, 0, ks) if j == 0 else None)
            mem_attention(0)

            def out_tiles(name, layer, sub, act_of, ahead=False, hidden=None):
                def tile(i, j):
                    c = BLOCK0[name] + 2 * j
                    first = isinstance(i, int) and (i, j) == (0, 0)
                    if ahead and first:
                        product(i, c + 1, sub[1], sub[0], act_of, psum(j), False, True, ks=range(sub[1] - 1, sub[1]))
                        return
                    acc_ready(TILE0[name] + 2 * i + j)
                    product(i, c, sub[0], 0, act_of, psum(j), True, False)
                    if hidden and first:
                        product(i, c + 1, sub[1], sub[0], act_of, psum(j), False, True, ks=range(sub[1] - 1))
                        pe.wait_ge(S.f_lo, hidden)
                        product(i, c + 1, sub[1], sub[0], act_of, psum(j), False, True, ks=range(sub[1] - 1, sub[1]))
                        return
                    product(i, c + 1, sub[1], sub[0], act_of, psum(j), False, True)

                def body(i):
                    for j in range(2):
                        tile(i, j)
                if name != LAST:
                    turns(pe, KT // 2, body)
                    return
                for i in range(KT // 2):
                    for j in range(2):
                        tile(i, j)
                        if 2 * i + j:
                            turn_result(2 * i + j - 1)
                turn_result(KT - 1)

            def turn_result(k):
                pe.wait_ge(S.acc_free, TILE0[LAST] + k + 1)
                if due(k - 3):
                    pe.wait_ge(S.fin_done, k - 3)
                for t in range(NT):
                    mm = nc.tensor.transpose(bank[:, D[k % 4], t * P:(t + 1) * P], xT[:, k, t * P:(t + 1) * P],
                                             sq(IDENT))
                mm.then_inc(S.fin_tr, 1)

            def row_sums(r):
                if due(KT * (r + 1)):
                    pe.wait_ge(S.r_acc, KT * (r + 1))
                nc.tensor.matmul(psum(D[0]), sq(ONES), w(SQ_T), start=True, stop=True).then_inc(S.r_ss, 1)

            def ffn(layer):
                h_of = (lambda k: H_AT[layer] + k)
                for half in range(2):
                    b0, n0 = BLOCK0[f"up{layer}{half}"], TILE0[f"up{layer}{half}"]

                    def pair(it, j):
                        for g in range(2):
                            acc_ready(4 * it + n0 + 2 * j + g)
                            if half == 0 and isinstance(it, int) and (it, j, g) == (0, 0, 0):
                                product(it, b0, KT, 0, h_of, psum(g), True, True, ks=range(KT - 1))
                                pe.wait_ge(S.r_lo, KT * (2 * layer + 1))
                                product(it, b0, KT, 0, h_of, psum(g), True, True, ks=range(KT - 1, KT))
                                row_sums(2 * layer)
                                continue
                            product(it, b0 + 2 * j + g, KT, 0, h_of, psum(g), True, True)

                    def body(it):
                        pair(it, 0)
                        pair(it, 1)
                    if half == 0:
                        pe.wait_ge(S.r_lo, KT * (2 * layer + 1) - 1)
                    turns(pe, 4, body)
                    for j in range(8, HALF):
                        pair(0, j)
                    pe.wait_ge(S.f_lo, HALF * (2 * layer + half + 1) - 1)
                    out_tiles(f"down{layer}{half}", layer, DOWN_SUB, lambda k: cat_tile(layer, k),
                              hidden=HALF * (2 * layer + half + 1))

            pe.wait_ge(S.mq_lo, MEM_HEADS)
            out_tiles("out0", 0, OUT_SUB, lambda k: cat_tile(0, k), ahead=True)
            ffn(0)

            pe.wait_ge(S.r_lo, 2 * KT - 1)
            acc_ready(TILE0["kv"])
            product(0, BLOCK0["kv"], KT, 0, lambda k: k, psum(0), True, True, ks=range(KT - 1))
            pe.wait_ge(S.r_lo, 2 * KT)
            product(0, BLOCK0["kv"], KT, 0, lambda k: k, psum(0), True, True, ks=range(KT - 1, KT))
            row_sums(1)
            acc_ready(TILE0["kv"] + 1)
            product(0, BLOCK0["kv"] + 1, KT, 0, lambda k: k, psum(1), True, True)
            pe.wait_ge(S.kv_sq, 1)
            pe.wait_ge(S.r_ln, 2)
            nc.tensor.matmul(psum(D[0]), sq(ONES64), w(3), start=True, stop=True).then_inc(S.kv_ss, 1)

            def sw_project(u, ks):
                past = u - SW_HEADS // QPB
                if past >= 0:
                    if past == 0 or ks[0] < KT // 2:
                        mem_project(1, past, ks)
                    return
                if ks[0] == 0:
                    acc_ready(TILE0["swq"] + u)
                product(0, BLOCK0["swq"] + u, KT, 0, lambda k: KT + k, psum(u % 2), True, True, ks=ks)

            def sw_sums(u):
                pe.wait_ge(S.sw_sq, u + 1)
                if due(u):
                    pe.wait_ge(S.sw_ln, u)
                nc.tensor.matmul(psum(D[4]), sq(ONES64), w(1), start=True, stop=True).then_inc(S.sw_ss, 1)

            def sw_scores(u, e):
                n = 2 * u + e
                pe.wait_ge(S.sw_q, u + 1)
                if due(n - 1):
                    pe.wait_ge(S.sw_pt, n - 1)
                if due(n - 1):
                    pe.wait_ge(S.sw_ptp, n - 1)
                rows = slice(SW_DIM * e, SW_DIM * (e + 1))
                for t in range(NT):
                    mm = nc.tensor.matmul(bank[:, D[0] + 2 * e + t // 2, (t % 2) * 256:(t % 2) * 256 + WIN],
                                          ws[rows, 3, t * P:(t + 1) * P],
                                          kwin[rows, u // 4, t * P:t * P + WIN],
                                          start=True, stop=True)
                mm.then_inc(S.sw_sc, 1)

            def sw_transposes(u, e):
                pe.wait_ge(S.sw_p, 2 * u + e + 1)
                for t in range(NT):
                    mm = nc.tensor.transpose(bank[:, D[0] + 2 * e, t * P:(t + 1) * P], swp(e)[:, t, P:2 * P], sq(IDENT))
                    if t:
                        mm = nc.tensor.transpose(bank[:, D[1] + 2 * e, t * P:(t + 1) * P], swp(e)[:, t, 0:P], sq(IDENT))
                mm.then_inc(S.sw_tr, 1)

            def sw_output(u, e):
                pe.wait_ge(S.sw_pt, 2 * u + e + 1)
                pe.wait_ge(S.sw_ptp, 2 * u + e + 1)
                if due(u):
                    pe.wait_ge(S.sw_o_lo, u)
                rows = slice(SW_DIM * e, SW_DIM * (e + 1))
                v_of = slice(u // 4 * SW_DIM, (u // 4 + 1) * SW_DIM)
                for t in range(NT):
                    o_acc = bank[rows, D[5], t * P:(t + 1) * P]
                    mm = nc.tensor.matmul(o_acc, tt(V_T, t)[:, v_of], tt(PT_OWN[e], t), start=True, stop=(t == 0))
                    if t:
                        mm = nc.tensor.matmul(o_acc, tt(V_T, t - 1)[:, v_of], tt(PT_PREV[e], t),
                                              start=False, stop=True)
                mm.then_inc(S.sw_o, 1)

            pe.wait_ge(S.b_lo, KT)
            sw_project(0, range(KT))
            pe.wait_ge(S.acc_free, TILE0["kv"] + 2)
            transposes4(D[1], V_F).then_inc(S.kv_vt, 1)
            sw_sums(0)
            sw_project(1, range(KT))
            pe.wait_ge(S.kv_done, 8)
            pe.wait_ge(S.kv_dup, 32)
            sw_scores(0, 0)
            sw_scores(0, 1)
            for u in range(SW_HEADS // QPB):
                following = u + 1 < SW_HEADS // QPB
                if following:
                    sw_sums(u + 1)
                sw_project(u + 2, range(0, 4))
                sw_project(u + 2, range(4, 7))
                sw_transposes(u, 0)
                sw_project(u + 2, range(7, KT))
                sw_transposes(u, 1)
                sw_output(u, 0)
                if following:
                    sw_scores(u + 1, 0)
                sw_output(u, 1)
                if following:
                    sw_scores(u + 1, 1)
            mem_attention(1)

            pe.wait_ge(S.mq_lo, 2 * MEM_HEADS)
            out_tiles("out1", 1, OUT_SUB, lambda k: cat_tile(1, k), ahead=True)
            ffn(1)

        @block.scalar
        def _(act):
            def a(out_, in_, func, **kw):
                return nc.scalar.activation(out_, in_, func, **kw)

            def upper(it, c):
                b = 4 * it + c
                if isinstance(b, int) and b >= N_BLOCKS:
                    return
                width = subtiles(b if isinstance(b, int) else c + 4) * P
                s = c % RING
                act.wait_ge(raw_loaded[s], 16 * it + 16 * (c // RING) + 16)
                if due(b - RING + 1):
                    act.wait_ge(S.block_used, b - RING + 1)
                a(w_hi[:, s, 0:width], w_raw[:, s, 0:width], ACT.Copy).then_inc(S.hi_done, 1)

            act.preload_act_table_set("natural_log_exp_and_others")
            act.wait_ge(S.mem_loaded, 16)
            act.wait_ge(S.cols_loaded, 16)

            def rows(first, t):
                return ws[:, first + 2 * t:first + 2 * t + 2, :].rearrange("p a c -> p (a c)")
            for t in range(MT_):
                if t == 1:
                    act.wait_ge(S.mem_rest_loaded, 16)
                a(rows(12, t), rows(8, t), ACT.Square, accum_out=st[:, t:t + 1]).then_inc(S.m_sq, 1)
            act.wait_ge(S.m_sq, MT_)
            a(st[:, 6:8], st[:, 0:2], ACT.Ln, scale=1.0 / D_MODEL, bias=col("eps")).then_inc(S.m_ln, 1)
            act.wait_ge(S.m_ln, 1)
            a(st[:, 6:8], st[:, 6:8], ACT.Exp, scale=-0.5).then_inc(S.m_rstd, 1)
            act.wait_ge(S.m_rstd, 1)
            for t in range(MT_):
                a(rows(8, t), rows(8, t), ACT.Copy, scale=st[:, 6 + t:7 + t]).then_inc(S.m_scaled, 1)
            upper(0, 0)
            upper(0, 1)

            def mem_upper(layer):
                own = slice(MEM_LEN * layer, MEM_LEN * (layer + 1))
                for i, k in enumerate(MEM_ORDER):
                    act.wait_ge(S.m_tr, 2 * (k // 2) + 2)
                    if due(KT * layer + i - 3):
                        act.wait_ge(S.m_evac_lo, KT * layer + i - 3)
                    a(act_hi[:, KT + k, own], mem_ps(k), ACT.Copy, scale=col(f"mem{layer}", k)).then_inc(S.m_evac_hi, 1)
            mem_upper(0)

            def key_rstd(head):
                act.wait_ge(S.mk_ss, head + 1)
                if due(head):
                    act.wait_ge(S.mk_done, head)
                a(w(KRS)[:, 0:MEM_LEN], psum(D[4], MEM_LEN), ACT.Ln, scale=1.0 / P, bias=col("eps")).then_inc(S.mk_ln, 1)
                act.wait_ge(S.mk_ln, head + 1)
                a(w(KRS)[:, 0:MEM_LEN], w(KRS)[:, 0:MEM_LEN], ACT.Exp, scale=-0.5).then_inc(S.mk_rstd, 1)

            def mem_keys(layer):
                for j in range(MEM_HEADS):
                    c = BLOCK0[f"mem{layer}"] + 2 * j
                    head = j + MEM_HEADS * layer
                    upper(0, c + 2)
                    if j > 0:
                        key_rstd(head - 1)
                    upper(0, c + 3)
                    if head == 0:
                        mem_upper(1)
                    act.wait_ge(S.acc_free, TILE0[f"mem{layer}"] + 2 * j + 2)
                    if due(head):
                        act.wait_ge(S.mk_ss, head)
                    a(w(KS)[:, 0:MEM_LEN], w(KR)[:, 0:MEM_LEN], ACT.Square).then_inc(S.mk_sq, 1)
                key_rstd(MEM_HEADS * (layer + 1) - 1)

            mem_keys(0)
            act.wait_ge(S.x_loaded, 16)
            act.wait_ge(S.m_tr, KT)
            for t in range(NT):
                if due(t - 1):
                    act.wait_ge(S.x_sq, t - 1)
                a(rows(8, t % 2), rows(0, t), ACT.Square, accum_out=st[:, 2 + t:3 + t]).then_inc(S.x_sq, 1)
            act.wait_ge(S.x_sq, NT)
            a(st[:, 8:12], st[:, 2:6], ACT.Ln, scale=1.0 / D_MODEL, bias=col("eps")).then_inc(S.x_ln, 1)
            act.wait_ge(S.x_ln, 1)
            a(st[:, 8:12], st[:, 8:12], ACT.Exp, scale=-0.5).then_inc(S.x_rstd, 1)
            act.wait_ge(S.x_rstd, 1)
            act.wait_ge(S.x_raw_tr, KT)
            for t in range(NT):
                a(rows(0, t), rows(0, t), ACT.Copy, scale=st[:, 8 + t:9 + t]).then_inc(S.x_scaled, 1)
            act.wait_ge(S.ba_loaded, 16)
            a(ba_w[:, 0, :], w(E0)[:, 0:KT * 16], ACT.Copy).then_inc(S.ba_hi, 1)
            mem_keys(1)
            for k in range(KT):
                act.wait_ge(S.x_tr, k + 1)
                a(act_hi[:, k, :], psum(D[k % 4]), ACT.Copy, scale=col("a_norm", k)).then_inc(S.x_evac_hi, 1)

            def conv_tile(h, j):
                c = BLOCK0["dn"] + j
                upper(h, c + 2)
                if j < 3:
                    at_once(act)
                    act.wait_ge(S.block_used, 4 * h + c + 1)
                    nc.scalar.activation(w(CQ + j), psum(j % 2), ACT.Copy,
                                         scale=conv_w(h, j, 3)).then_inc(S.cv_tap, 1)

            act.wait_ge(S.ba_mm, 1)
            ba_ps = bank[:, D[0], 0:NT * 16].rearrange("p (t c) -> p c t", t=NT)
            a(dn(TMP1), ba_ps[:, 0:DN_HEADS, :], ACT.Exp, scale=-1.0).then_inc(S.ba_act, 1)
            a(st[:, 16:24], cols[:, COLS["a_log"]:COLS["a_log"] + DN_HEADS], ACT.Exp).then_inc(S.ba_act, 1)
            act.wait_ge(S.ba_dve, 2)
            a(dn(GL), dn(GL), ACT.Exp, scale=-1.0).then_inc(S.ba_act, 1)
            act.wait_ge(S.ba_act, 3)
            a(dn(GL), dn(GL), ACT.Ln, bias=sq_c[:, ONES, 0:1]).then_inc(S.ba_act, 1)
            conv_tile(0, 0)
            act.wait_ge(S.ba_dve, 7)
            a(dn_s[:, GL, :], bank[:, D[2], 0:32], ACT.Exp).then_inc(S.ba_act, 1)
            a(dn(EDEC), dn(TMP1), ACT.Exp).then_inc(S.ba_act, 1)
            a(dn(TMP2), dn(GCUM), ACT.Exp).then_inc(S.ba_act, 1)

            def silu_qkv(h):
                act.wait_ge(S.acc_free, TILE0["dn"] + 4 * h + 3)
                a(ws[:, CQ:CV + 1, :], ws[:, CQ:CV + 1, :], ACT.Silu).then_inc(S.c_ready, 1)

            def squares_qk(h):
                if due(h):
                    act.wait_ge(S.o_done, h)
                act.wait_ge(S.c_ready, h + 1)
                a(w(E0), w(CQ), ACT.Square).then_inc(S.sq_done, 1)
                a(w(PM), w(CK), ACT.Square).then_inc(S.sq_done, 1)

            def o_upper(h):
                at_once(act)
                act.wait_ge(S.o_t2, h + 1)
                a(act_hi[:, h + KT, :], w(MM), ACT.Copy).then_inc(S.o_hi, 1)

            def delta(h, fill, following):
                for m, (e, ln_scale) in enumerate(((E0, "ln_q"), (PM, None))):
                    act.wait_ge(S.ss_done, 2 * h + m + 1)
                    a(w(e), psum(D[m]), ACT.Ln, bias=col("eps")).then_inc(S.rr_ln, 1)
                    act.wait_ge(S.rr_ln, 2 * h + m + 1)
                    kw = dict(bias=col(ln_scale)) if ln_scale else {}
                    a(w(e), w(e), ACT.Exp, scale=-0.5, **kw).then_inc(S.rr_done, 1)
                act.wait_ge(S.gb_done, 2 * h + 1)
                a(w(EG), psum(D[2]), ACT.Exp).then_inc(S.eg_done, 1)
                if due(h):
                    o_upper(h - 1)
                act.wait_ge(S.dm_pre, 2 * h + 2)
                a(w(DD), w(DD), ACT.Exp).then_inc(S.dm_done, 1)
                fill(0)
                act.wait_ge(S.t_tr, h + 1)
                a(w(TT), psum(D[2]), ACT.Copy).then_inc(S.t_done, 1)
                fill(1)
                fill(2)
                if following:
                    silu_qkv(h + 1)
                act.wait_ge(S.acc_free, TILE0["dn"] + 4 * h + 4)
                a(w(SZ), w(EC), ACT.Silu).then_inc(S.sz_done, 1)
                act.preload_act_table_set("natural_log_exp_and_others")
                fill(3)
                act.wait_ge(S.o_done, h + 1)
                a(w(E1), psum(D[5]), ACT.Square).then_inc(S.osq, 1)
                if following:
                    squares_qk(h + 1)
                act.wait_ge(S.oss, h + 1)
                a(w(E1), psum(D[2]), ACT.Ln, scale=1.0 / P, bias=col("eps")).then_inc(S.o_ln, 1)
                act.wait_ge(S.o_ln, h + 1)
                a(w(E1), w(E1), ACT.Exp, scale=-0.5).then_inc(S.o_rstd, 1)

            for j in range(1, 4):
                conv_tile(0, j)
            silu_qkv(0)
            act.preload_act_table_set("natural_log_exp_and_others")
            squares_qk(0)
            turns(act, DN_HEADS - 1, lambda h: delta(h, lambda j: conv_tile(h + 1, j), True))
            def mem_square(layer, j):
                act.wait_ge(S.acc_free, TILE0[f"mq{layer}"] + j + 1)
                if due(layer * MEM_HEADS + j):
                    act.wait_ge(S.mq_n, layer * MEM_HEADS + j)
                a(w(2), w(j % 2), ACT.Square).then_inc(S.mq_sq, 1)

            def beside_last(j):
                if j == 0:
                    upper(0, BLOCK0["mq0"] + 2)
                if j == 3:
                    upper(0, BLOCK0["mq0"] + 3)
                    mem_square(0, 0)
            delta(DN_HEADS - 1, beside_last, False)

            def mem_attention(layer):
                c = BLOCK0[f"mq{layer}"]

                def square(j):
                    mem_square(layer, j)

                def rstd_q(j):
                    u = layer * MEM_HEADS + j
                    act.wait_ge(S.mq_ss, u + 1)
                    a(w(2), psum(D[0]), ACT.Ln, scale=1.0 / P, bias=col("eps")).then_inc(S.mq_ln, 1)
                    act.wait_ge(S.mq_ln, u + 1)
                    a(w(2), w(2), ACT.Exp, scale=-0.5, bias=col("ln_q")).then_inc(S.mq_rstd, 1)

                rstd_q(0)
                if layer == 0:
                    o_upper(DN_HEADS - 1)
                square(1)
                for j in range(MEM_HEADS):
                    u = layer * MEM_HEADS + j
                    if j + 1 < MEM_HEADS:
                        rstd_q(j + 1)
                    act.wait_ge(S.mq_max, 2 * u + 2)
                    if due(u):
                        act.wait_ge(S.mq_tr, u)
                    if due(u):
                        act.wait_ge(S.mq_p, u)
                    for t in range(NT):
                        a(mq_p_of(t), bank[:, D[2] + t // 2, (t % 2) * MEM_LEN:(t % 2 + 1) * MEM_LEN], ACT.Exp, bias=st[:, 28 + t:29 + t], accum_out=st[:, 32 + t:33 + t]).then_inc(S.mq_exp, 1)
                    if j + 2 < MEM_HEADS:
                        upper(0, c + j + 4)
                    act.wait_ge(S.mq_tr, u + 1)
                    if due(u):
                        act.wait_ge(S.mq_o, u)
                    a(w(6), psum(D[4]), ACT.Copy).then_inc(S.mq_pt, 1)
                    if j + 2 < MEM_HEADS:
                        square(j + 2)
                    act.wait_ge(S.mq_o, u + 1)
                    a(act_hi[:, cat_tile(layer, KT + j), :], psum(D[1]), ACT.Copy).then_inc(S.mq_hi, 1)

            mem_attention(0)

            def residual(name, gain, r, last):
                def body(i):
                    for j in range(2):
                        k = 2 * i + j
                        upper(i, BLOCK0[name] + 2 * j + 2)
                        upper(i, BLOCK0[name] + 2 * j + 3)
                        if name == LAST and k > 0:
                            result_out(k - 1)
                        if last:
                            continue
                        act.wait_ge(S.acc_free, TILE0[name] + k + 1)
                        q = KT * r + k
                        if due(q - 1):
                            act.wait_ge(S.r_acc, q - 1)
                        a(w(13 + j), xT[:, k, :], ACT.Square).then_inc(S.r_sq, 1)
                        at_once(act)
                        nc.scalar.activation(act_hi[:, H_NEXT[name] + k, :], xT[:, k, :], ACT.Copy,
                                             scale=gain(k)).then_inc(S.r_hi, 1)
                if name != LAST:
                    turns(act, KT // 2, body)
                    return
                for i in range(KT // 2):
                    body(i)
                result_out(KT - 1)

            def result_out(k):
                act.wait_ge(S.fin_tr, k + 1)
                a(result[:, :, k * P:(k + 1) * P], psum4(D[k % 4]), ACT.Copy).then_inc(S.fin_done, 1)

            def rstd(r):
                act.wait_ge(S.r_ss, r + 1)
                a(w(R_T), psum(D[0]), ACT.Ln, scale=1.0 / D_MODEL, bias=col("eps")).then_inc(S.r_ln, 1)
                act.wait_ge(S.r_ln, r + 1)
                a(w(R_T), w(R_T), ACT.Exp, scale=-0.5).then_inc(S.r_done, 1)

            def ffn(layer):
                for half in range(2):
                    c = BLOCK0[f"up{layer}{half}"]

                    def pair(it, j):
                        upper(it, c + 2 * j + 2)
                        upper(it, c + 2 * j + 3)
                        f = HALF * (2 * layer + half) + 2 * it + j
                        act.wait_ge(S.acc_free, 4 * it + TILE0[f"up{layer}{half}"] + 2 * j + 1)
                        if due(f - 1):
                            act.wait_ge(S.f_hid, f - 1)
                        a(w(2 + j % 2), w(j % 2), ACT.Silu).then_inc(S.f_silu, 1)
                        act.wait_ge(S.f_hid, f + 1)
                        if due(f - 1):
                            act.wait_ge(S.f_lo, f - 1)
                        at_once(act)
                        a(act_hi[:, hid_tile(layer, it, j), :], w(6 + j % 2), ACT.Copy).then_inc(S.f_hi, 1)

                    def body(it):
                        pair(it, 0)
                        pair(it, 1)
                    if half == 0:
                        rstd(2 * layer)
                    turns(act, 4, body)
                    for j in range(8, HALF):
                        pair(0, j)
                    act.preload_act_table_set("natural_log_exp_and_others")
                    nxt = None if half == 0 or layer == 1 else (lambda k: col_k("kv_norm", k))
                    residual(f"down{layer}{half}", nxt, 1, nxt is None)

            residual("out0", lambda k: col_k("ffn0", k), 0, False)
            ffn(0)

            upper(0, BLOCK0["kv"] + 2)
            upper(0, BLOCK0["kv"] + 3)
            act.wait_ge(S.block_used, BLOCK0["kv"])
            for k in range(KT):
                a(act_hi[:, KT + k, :], xT[:, k, :], ACT.Copy, scale=col("b_norm", k)).then_inc(S.b_hi, 1)
            rstd(1)
            act.wait_ge(S.acc_free, TILE0["kv"] + 1)
            a(w(3), w(2), ACT.Square).then_inc(S.kv_sq, 1)
            act.wait_ge(S.kv_ss, 1)
            a(w(4), psum(D[0]), ACT.Ln, scale=1.0 / SW_DIM, bias=col("eps")).then_inc(S.kv_ln, 1)
            act.wait_ge(S.kv_ln, 1)
            a(w(4), w(4), ACT.Exp, scale=-0.5).then_inc(S.kv_rstd, 1)

            def sw_square(u):
                act.wait_ge(S.acc_free, TILE0["swq"] + u + 1)
                if due(u):
                    act.wait_ge(S.sw_ss, u)
                a(w(1), w(0), ACT.Square).then_inc(S.sw_sq, 1)

            def sw_rstd_q(u):
                act.wait_ge(S.sw_ss, u + 1)
                if due(u):
                    act.wait_ge(S.sw_q, u)
                a(w(2), psum(D[4]), ACT.Ln, scale=1.0 / SW_DIM, bias=col("eps")).then_inc(S.sw_ln, 1)
                act.wait_ge(S.sw_ln, u + 1)
                a(w(2), w(2), ACT.Exp, scale=-0.5, bias=col("ln_s")).then_inc(S.sw_rstd, 1)

            act.wait_ge(S.kv_n, 1)
            for g in range(SW_KV):
                other = slice(SW_DIM * (1 - g), SW_DIM * (2 - g))
                act.dma_start(kwin[other, g, SW_DIM:], ws[SW_DIM * g:SW_DIM * (g + 1), KN_T, :]
                              ).then_inc(S.kv_dup, 16)
            upper(0, BLOCK0["swq"] + 2)
            sw_square(0)
            sw_rstd_q(0)
            upper(0, BLOCK0["swq"] + 3)
            sw_square(1)
            for u in range(SW_HEADS // QPB):
                following = u + 1 < SW_HEADS // QPB
                if following:
                    sw_rstd_q(u + 1)
                for e in range(QPB):
                    n = 2 * u + e
                    act.wait_ge(S.sw_nm, n + 1)
                    for t in range(NT):
                        a(swp(e)[:, t, SW_DIM:], swp(e)[:, t, SW_DIM:], ACT.Exp,
                          bias=st[:, 36 + 4 * e + t:37 + 4 * e + t], accum_out=st[:, 44 + 4 * e + t:45 + 4 * e + t]).then_inc(S.sw_exp, 1)
                    a(st[:, 52 + 4 * e:56 + 4 * e], st[:, 36 + 4 * e:40 + 4 * e], ACT.Exp,
                      bias=col("sinks", n)).then_inc(S.sw_exp, 1)
                upper(0, BLOCK0["swq"] + u + 4)
                for e in range(QPB):
                    n = 2 * u + e
                    act.wait_ge(S.sw_tr, n + 1)
                    if due(n - 1):
                        act.wait_ge(S.sw_o, n - 1)
                    a(w(PT_OWN[e]), psum(D[0] + 2 * e), ACT.Copy).then_inc(S.sw_pt, 1)
                if u + 2 < SW_HEADS // QPB:
                    sw_square(u + 2)
                elif u + 1 == SW_HEADS // QPB:
                    mem_square(1, 0)
                act.wait_ge(S.sw_o, 2 * u + 2)
                a(act_hi[:, u, :], psum(D[5]), ACT.Copy).then_inc(S.sw_o_hi, 1)

            mem_attention(1)
            residual("out1", lambda k: col_k("ffn1", k), 2, False)
            ffn(1)

        @block.vector
        def _(dve):
            V = nc.vector

            def mul(out_, x_, y_):
                return V.tensor_tensor(out_, x_, y_, ALU.mult)

            def sub(out_, x_, y_):
                return V.tensor_tensor(out_, x_, y_, ALU.subtract)

            def stt(out_, x_, scalar, y_, op0, op1):
                return V.scalar_tensor_tensor(out=out_, in0=x_, scalar=scalar, in1=y_, op0=op0, op1=op1)

            def cp(out_, x_):
                return V.tensor_copy(out_, x_)

            def hi(tile_):
                return act_hi[:, tile_, :].bitcast(F32)

            dve.wait_ge(S.consts_loaded, 16)
            dve.wait_ge(S.cols_loaded, 16)

            def mem_lower(layer):
                own = slice(MEM_LEN * layer, MEM_LEN * (layer + 1))
                for i, k in enumerate(MEM_ORDER):
                    dve.wait_ge(S.m_evac_hi, KT * layer + i + 1)
                    stt(act_lo[:, KT + k, own], mem_ps(k), col(f"mem{layer}", k), hi(KT + k)[:, own],
                        ALU.mult, ALU.subtract).then_inc(S.m_evac_lo, 1)
            mem_lower(0)

            def key_normed(layer, head):
                dve.wait_ge(S.mk_rstd, head + 1)
                stt(kmem[:, head, :], w(KR)[:, 0:MEM_LEN], col(f"mk{layer}"), w(KRS)[:, 0:MEM_LEN],
                    ALU.mult, ALU.mult).then_inc(S.mk_done, 1)

            def mem_kv(layer):
                for j in range(MEM_HEADS):
                    c, n = BLOCK0[f"mem{layer}"] + 2 * j, TILE0[f"mem{layer}"] + 2 * j
                    head = j + MEM_HEADS * layer
                    dve.wait_ge(S.block_used, c + 1)
                    if due(head):
                        dve.wait_ge(S.mv_tr, head)
                    cp(raw_values, psum(0, MEM_LEN)).then_inc(S.acc_free, 1)
                    if j > 0:
                        key_normed(layer, head - 1)
                    dve.wait_ge(S.block_used, c + 2)
                    if due(head):
                        dve.wait_ge(S.mk_done, head)
                    cp(w(KR)[:, 0:MEM_LEN], psum(1, MEM_LEN)).then_inc(S.acc_free, 1)
                    dve.wait_ge(S.mv_tr, head + 1)
                    cp(vmem[:, head, :], psum(D[5], MEM_LEN)).then_inc(S.mv_done, 1)
                    if head == 0:
                        mem_lower(1)
                key_normed(layer, MEM_HEADS * (layer + 1) - 1)

            mem_kv(0)
            for k in range(KT):
                dve.wait_ge(S.x_raw_tr, k + 1)
                cp(xT[:, k, :], psum(D[k % 4])).then_inc(S.x_raw_copied, 1)
            dve.wait_ge(S.ba_hi, 1)
            sub(ba_w[:, 1, :], w(E0)[:, 0:KT * 16], ba_w[:, 0, :].bitcast(F32)).then_inc(S.ba_split, 1)
            mem_kv(1)
            for k in range(KT):
                dve.wait_ge(S.x_evac_hi, k + 1)
                stt(act_lo[:, k, :], psum(D[k % 4]), col("a_norm", k), hi(k), ALU.mult, ALU.subtract).then_inc(S.x_evac_lo, 1)

            def conv_tile(h, j):
                if j < 3:
                    for d in range(1, 4):
                        conv_tap(h, j, d)
                else:
                    dve.wait_ge(S.block_used, 4 * h + BLOCK0["dn"] + 4)
                    if due(h):
                        dve.wait_ge(S.sz_done, h)
                    cp(w(EC), psum(1)).then_inc(S.acc_free, 1)

            def conv_tap(h, j, d):
                if d == 1:
                    dve.wait_ge(S.cv_tap, 3 * h + j + 1)
                else:
                    dve.wait_ge(S.cv_conv, 6 * h + 2 * j + d - 1)
                stt(w(CQ + j)[:, d:], psum(j % 2)[:, 0:SEQ - d], conv_w(h, j, 3 - d), w(CQ + j)[:, d:],
                    ALU.mult, ALU.add).then_inc(S.cv_conv if d < 3 else S.acc_free, 1)

            def over_t(name):
                return cols[:, COLS[name]:COLS[name] + DN_HEADS].unsqueeze(2).to_broadcast([P, DN_HEADS, NT])
            ba_ps = bank[:, D[0], 0:NT * 16].rearrange("p (t c) -> p c t", t=NT)
            dve.wait_ge(S.ba_raw, 1)
            cp(ws[0:16, E1, :], bank[0:16, D[3], :]).then_inc(S.ba_copied, 1)
            dve.wait_ge(S.ba_act, 1)
            V.tensor_tensor(dn(TMP2), ba_ps[:, DN_HEADS:, :], over_t("dt"), ALU.add).then_inc(S.ba_dve, 1)
            dve.wait_ge(S.ba_dve, 1)
            stt(dn(GL), dn(TMP2), -1.0, dn(TMP2), ALU.mult, ALU.max).then_inc(S.ba_dve, 1)
            V.tensor_scalar(dn(TMP1), dn(TMP1), 1.0, None, ALU.add).then_inc(S.ba_dve, 1)
            dve.wait_ge(S.ba_dve, 3)
            V.reciprocal(dn(BETA), dn(TMP1)).then_inc(S.ba_dve, 1)
            dve.wait_ge(S.ba_act, 4)
            stt(dn(TMP2), dn(TMP2), 0.0, dn(GL), ALU.max, ALU.add).then_inc(S.ba_dve, 1)
            dve.wait_ge(S.ba_dve, 5)
            stt(dn(GG), dn(TMP2), -1.0, st[:, 16:24].unsqueeze(2).to_broadcast([P, DN_HEADS, NT]),
                ALU.mult, ALU.mult).then_inc(S.ba_g, 1)
            conv_tile(0, 0)
            dve.wait_ge(S.ba_cum, 1)
            cp(dn_s[:, GCUM, :], bank[:, D[1], 0:32]).then_inc(S.ba_dve, 1)
            dve.wait_ge(S.ba_dve, 6)
            sub(dn_s[:, TMP1, :], bank[:, D[2], 0:32], dn_s[:, GCUM, :]).then_inc(S.ba_dve, 1)
            dve.wait_ge(S.ba_act, 7)
            stt(dn(NBEG), dn(BETA), -1.0, dn(TMP2), ALU.mult, ALU.mult).then_inc(S.ba_dve, 1)
            dve.wait_ge(S.ba_dve, 8)

            def delta(h, fill):
                dve.wait_ge(S.rr_done, 2 * h + 1)
                mul(w(QN), w(CQ), w(E0)).then_inc(S.qn_done, 1)
                dve.wait_ge(S.rr_done, 2 * h + 2)
                mul(w(KN), w(CK), w(PM)).then_inc(S.kn_done, 1)
                dve.wait_ge(S.gb_done, 2 * h + 2)
                dve.wait_ge(S.kn_done, h + 1)
                mul(w(PM), w(KN), psum(D[3])).then_inc(S.kb_done, 1)
                dve.wait_ge(S.eg_done, h + 1)
                V.tensor_tensor(w4(DD), psum4(D[2]), over_tiles(NEG_LOWER), ALU.add).then_inc(S.dm_pre, 1)
                dve.wait_ge(S.dm_pre, 2 * h + 1)
                sub(w4(DD), w4(DD), dn_bcast(GCUM, h)).then_inc(S.dm_pre, 1)
                dve.wait_ge(S.vtr_done, h + 1)
                mul(w4(VB), psum4(D[4]), dn_bcast(BETA, h)).then_inc(S.vb_done, 1)
                dve.wait_ge(S.dm_done, h + 1)
                dve.wait_ge(S.gg_done, 2 * h + 1)
                if due(h):
                    dve.wait_ge(S.o_lo, h)
                mul(w(MM), psum(D[1]), w(DD)).then_inc(S.mt_done, 1)
                dve.wait_ge(S.mt_done, h + 1)
                mul(w4(ZZ), w4(MM), over_tiles(LEVEL0)).then_inc(S.z_pre, 1)
                dve.wait_ge(S.z_pre, h + 1)
                sub(w4(ZZ), over_tiles(IDENT), w4(ZZ)).then_inc(S.z_done, 1)
                dve.wait_ge(S.gg_done, 2 * h + 2)
                mul(w(AT), psum(D[0]), w(DD)).then_inc(S.at_done, 1)
                dve.wait_ge(S.ktr_done, h + 1)
                mul(w4(KBG), psum4(D[5]), dn_bcast(NBEG, h)).then_inc(S.kbg_done, 1)
                mul(w4(KDEC), psum4(D[5]), dn_bcast(EDEC, h)).then_inc(S.kdec_done, 1)
                fill(0)
                for k in range(1, LEVELS):
                    n = 12 * h + 2 * (k - 1)
                    for g in range(2):
                        dve.wait_ge(S.p_mm, n + g + 1)
                        own = slice(SEQ // 2 * g, SEQ // 2 * (g + 1))
                        mul(w(PM)[:, own].rearrange("p (t c) -> p t c", c=P),
                            bank[:, D[3 - g], 0:SEQ // 2].rearrange("p (t c) -> p t c", c=P),
                            sq_c[:, LEVEL0 + k:LEVEL0 + k + 1, :].to_broadcast([P, NT // 2, P])).then_inc(S.p_done, 1)
                    for g in range(2):
                        dve.wait_ge(S.tz_mm, n + g + 1)
                        own = slice(SEQ // 2 * g, SEQ // 2 * (g + 1))
                        if k < LEVELS - 1:
                            both = ws[:, TT:ZZ + 1, own]
                            sub(both, both, bank[:, D[4 + g], :].rearrange("p (a c) -> p a c", a=2)
                                ).then_inc(S.tz_done, 1)
                        else:
                            sub(w(ZZ)[:, own], w(ZZ)[:, own], bank[:, D[4 + g], SEQ // 2:]).then_inc(S.tz_done, 1)
                    if k <= 3:
                        fill(1, k)
                    if k >= 5:
                        fill(2, k - 4)
                fill(2, 3)
                dve.wait_ge(S.nw_mm, h + 1)
                cp(w(MM), psum(D[2])).then_inc(S.nw_done, 1)
                for t in range(NT):
                    dve.wait_ge(S.v_mm, NT * h + t + 1)
                    cp(tt(E0, t), bank[:, D[3], 0:P]).then_inc(S.v_done, 1)
                    if t == NT - 1:
                        break
                    dve.wait_ge(S.s_mm, 3 * h + t + 1)
                    if t == 0:
                        cp(state[:], bank[:, D[4], 0:P]).then_inc(S.s_done, 1)
                    else:
                        dve.wait_ge(S.s_done, 3 * h + t)
                        stt(state[:], state[:], dn(GL)[:, h, t:t + 1], bank[:, D[4], 0:P], ALU.mult, ALU.add
                            ).then_inc(S.s_done, 1)
                fill(3)
                dve.wait_ge(S.o_rstd, h + 1)
                mul(w(E1), psum(D[5]), w(E1)).then_inc(S.o_t1, 1)
                dve.wait_ge(S.o_t1, h + 1)
                dve.wait_ge(S.sz_done, h + 1)
                stt(w(MM), w(E1), col("out_norm"), w(SZ), ALU.mult, ALU.mult).then_inc(S.o_t2, 1)

            for j in range(1, 4):
                conv_tile(0, j)
            turns(dve, DN_HEADS - 1, lambda h: delta(h, lambda j, d=None: conv_tap(h + 1, j, d) if d else
                                                     conv_tile(h + 1, j)))

            def mem_raw(layer, j):
                dve.wait_ge(S.block_used, BLOCK0[f"mq{layer}"] + j + 1)
                if due(layer * MEM_HEADS + j - 1):
                    dve.wait_ge(S.mq_n, layer * MEM_HEADS + j - 1)
                if layer == 0:
                    cp(w(j % 2), psum(j % 2)).then_inc(S.acc_free, 1)
                else:
                    mul(w(j % 2), psum(j % 2), w(R_T)).then_inc(S.acc_free, 1)

            def mem_attention(layer):
                def normed(j):
                    u = layer * MEM_HEADS + j
                    dve.wait_ge(S.mq_rstd, u + 1)
                    if u == 0:
                        dve.wait_ge(S.o_t2, DN_HEADS)
                    if due(u):
                        dve.wait_ge(S.mq_sc, u)
                    dve.wait_ge(S.acc_free, TILE0[f"mq{layer}"] + j + 1)
                    stt(w(3), w(j % 2), col(f"mq{layer}"), w(2), ALU.mult, ALU.mult).then_inc(S.mq_n, 1)

                normed(0)
                mem_raw(layer, 1)
                for j in range(MEM_HEADS):
                    u = layer * MEM_HEADS + j
                    dve.wait_ge(S.mq_sc, u + 1)
                    if due(2 * u):
                        dve.wait_ge(S.mq_max, 2 * u)
                    V.tensor_reduce(st[:, 24:28], bank[:, D[2]:D[2] + 2, :].rearrange("p a (b c) -> p (a b) c", b=2),
                                    AX.X, ALU.max).then_inc(S.mq_max, 1)
                    dve.wait_ge(S.mq_max, 2 * u + 1)
                    V.tensor_scalar(st[:, 28:32], st[:, 24:28], -1.0, None, ALU.mult).then_inc(S.mq_max, 1)
                    if j + 1 < MEM_HEADS:
                        normed(j + 1)
                    dve.wait_ge(S.mq_exp, NT * (u + 1))
                    V.reciprocal(st[:, 32:36], st[:, 32:36]).then_inc(S.mq_rcp, 1)
                    dve.wait_ge(S.mq_rcp, u + 1)
                    p4 = ws[:, 4:6, :].rearrange("p a (b c) -> p (a b) c", b=2)
                    mul(p4, p4, st[:, 32:36].unsqueeze(2).to_broadcast([P, NT, MEM_LEN])).then_inc(S.mq_p, 1)
                    dve.wait_ge(S.mq_tr, u + 1)
                    if due(u):
                        dve.wait_ge(S.mq_o, u)
                    cp(w(7), psum(D[5])).then_inc(S.mq_pt, 1)
                    if j + 2 < MEM_HEADS:
                        mem_raw(layer, j + 2)
                    dve.wait_ge(S.mq_hi, u + 1)
                    tile_ = cat_tile(layer, KT + j)
                    sub(act_lo[:, tile_, :], psum(D[1]), hi(tile_)).then_inc(S.mq_lo, 1)

            delta(DN_HEADS - 1, lambda j, d=None: mem_raw(0, 0) if j == 0 else None)
            mem_attention(0)

            def residual(name, gain, r, last):
                def body(i):
                    for j in range(2):
                        k = 2 * i + j
                        dve.wait_ge(S.block_used, 4 * i + BLOCK0[name] + 2 * j + 2)
                        V.tensor_tensor(xT[:, k, :], xT[:, k, :], psum(j), ALU.add
                                        ).then_inc(S.acc_free, 1)
                        if last:
                            continue
                        q = KT * r + k
                        dve.wait_ge(S.r_sq, q + 1)
                        if due(q):
                            dve.wait_ge(S.r_acc, q)
                        if isinstance(k, int) and k == 0:
                            if due(r):
                                dve.wait_ge(S.r_ss, r)
                            cp(w(SQ_T), w(13 + j)).then_inc(S.r_acc, 1)
                        else:
                            V.tensor_tensor(w(SQ_T), w(SQ_T), w(13 + j), ALU.add).then_inc(S.r_acc, 1)
                        dve.wait_ge(S.r_hi, q + 1)
                        stt(act_lo[:, H_NEXT[name] + k, :], xT[:, k, :], gain(k), hi(H_NEXT[name] + k),
                            ALU.mult, ALU.subtract).then_inc(S.r_lo, 1)
                turns(dve, KT // 2, body)

            def ffn(layer):
                for half in range(2):
                    c = BLOCK0[f"up{layer}{half}"]

                    def pair(it, j):
                        f = HALF * (2 * layer + half) + 2 * it + j
                        dve.wait_ge(S.block_used, 4 * it + c + 2 * j + 1)
                        dve.wait_ge(S.r_done, 2 * layer + 1)
                        if due(f - 1):
                            dve.wait_ge(S.f_silu, f - 1)
                        mul(w(j % 2), psum(0), w(R_T)).then_inc(S.acc_free, 1)
                        dve.wait_ge(S.block_used, 4 * it + c + 2 * j + 2)
                        mul(w(4 + j % 2), psum(1), w(R_T)).then_inc(S.acc_free, 1)
                        dve.wait_ge(S.f_silu, f + 1)
                        dve.wait_ge(S.acc_free, 4 * it + TILE0[f"up{layer}{half}"] + 2 * j + 2)
                        if due(f - 1):
                            dve.wait_ge(S.f_lo, f - 1)
                        mul(w(6 + j % 2), w(4 + j % 2), w(2 + j % 2)).then_inc(S.f_hid, 1)
                        dve.wait_ge(S.f_hi, f + 1)
                        tile_ = hid_tile(layer, it, j)
                        sub(act_lo[:, tile_, :], w(6 + j % 2), hi(tile_)).then_inc(S.f_lo, 1)

                    def body(it):
                        pair(it, 0)
                        pair(it, 1)
                    turns(dve, 4, body)
                    for j in range(8, HALF):
                        pair(0, j)
                    nxt = None if half == 0 or layer == 1 else (lambda k: col_k("kv_norm", k))
                    residual(f"down{layer}{half}", nxt, 1, nxt is None)

            residual("out0", lambda k: col_k("ffn0", k), 0, False)
            ffn(0)

            V.memset(kwin[:, :, 0:SW_DIM], 0.0).then_inc(S.kv_done, 1)
            for k in range(KT):
                dve.wait_ge(S.b_hi, k + 1)
                stt(act_lo[:, KT + k, :], xT[:, k, :], col("b_norm", k), hi(KT + k), ALU.mult, ALU.subtract
                    ).then_inc(S.b_lo, 1)
            dve.wait_ge(S.r_done, 2)
            dve.wait_ge(S.block_used, BLOCK0["kv"] + 1)
            mul(w(2), psum(0), w(R_T)).then_inc(S.acc_free, 1)
            dve.wait_ge(S.block_used, BLOCK0["kv"] + 2)
            mul(w(V_F), psum(1), w(R_T)).then_inc(S.acc_free, 1)
            dve.wait_ge(S.kv_rstd, 1)
            dve.wait_ge(S.acc_free, TILE0["kv"] + 1)
            stt(w(KN_T), w(2), col("k_norm"), w(4), ALU.mult, ALU.mult).then_inc(S.kv_n, 1)
            dve.wait_ge(S.kv_n, 1)
            for g in range(SW_KV):
                rows_ = slice(SW_DIM * g, SW_DIM * (g + 1))
                cp(kwin[rows_, g, SW_DIM:], ws[rows_, KN_T, :]).then_inc(S.kv_done, 1)

            def sw_raw(u):
                if u >= SW_HEADS // QPB:
                    if u == SW_HEADS // QPB:
                        dve.wait_ge(S.sw_q, u)
                        mem_raw(1, 0)
                    return
                dve.wait_ge(S.block_used, BLOCK0["swq"] + u + 1)
                if due(u):
                    dve.wait_ge(S.sw_q, u)
                mul(w(0), psum(u % 2), w(R_T)).then_inc(S.acc_free, 1)

            def sw_normed(u):
                dve.wait_ge(S.sw_rstd, u + 1)
                dve.wait_ge(S.acc_free, TILE0["swq"] + u + 1)
                if due(2 * u):
                    dve.wait_ge(S.sw_sc, 2 * u)
                stt(w(3), w(0), col("q_norm"), w(2), ALU.mult, ALU.mult).then_inc(S.sw_q, 1)

            sw_raw(0)
            dve.wait_ge(S.kv_vt, 1)
            cp(w(V_T), psum(D[1])).then_inc(S.kv_done, 1)
            sw_normed(0)
            dve.wait_ge(S.dist_loaded, 16)
            dve.wait_ge(S.kv_dup, 32)
            for e in range(QPB):
                V.memset(swp(e)[:, :, 0:SW_DIM], 0.0).then_inc(S.kv_done, 1)
                V.memset(ws[:, PT_PREV[e], 0:P], 0.0).then_inc(S.kv_done, 1)
            sw_raw(1)
            for u in range(SW_HEADS // QPB):
                for e in range(QPB):
                    n = 2 * u + e
                    dve.wait_ge(S.sw_sc, n + 1)
                    if due(n - 1):
                        dve.wait_ge(S.sw_tr, n - 1)
                    scores = bank[:, D[0] + 2 * e:D[0] + 2 * e + 2, :].rearrange("p a (b c) -> p (a b) c", b=2)
                    stt(swp(e)[:, :, SW_DIM:], distance, col("nslope", n), scores[:, :, 0:WIN],
                        ALU.mult, ALU.add).then_inc(S.sw_s, 1)
                    dve.wait_ge(S.sw_s, n + 1)
                    V.tensor_reduce(st[:, 24 + 4 * e:28 + 4 * e], swp(e)[:, :, SW_DIM:], AX.X, ALU.max
                                    ).then_inc(S.sw_mx, 1)
                    dve.wait_ge(S.sw_mx, n + 1)
                    if due(2 * n - 2):
                        dve.wait_ge(S.sw_den, 2 * n - 2)
                    V.tensor_scalar(st[:, 36 + 4 * e:40 + 4 * e], st[:, 24 + 4 * e:28 + 4 * e], col("sinks", n), -1.0,
                                    ALU.max, ALU.mult).then_inc(S.sw_nm, 1)
                for e in range(QPB):
                    n = 2 * u + e
                    den = st[:, 44 + 4 * e:48 + 4 * e]
                    dve.wait_ge(S.sw_exp, (NT + 1) * (n + 1))
                    V.tensor_tensor(den, den, st[:, 52 + 4 * e:56 + 4 * e], ALU.add).then_inc(S.sw_den, 1)
                    dve.wait_ge(S.sw_den, 2 * n + 1)
                    V.reciprocal(den, den).then_inc(S.sw_den, 1)
                    dve.wait_ge(S.sw_den, 2 * n + 2)
                    mul(swp(e)[:, :, SW_DIM:], swp(e)[:, :, SW_DIM:], den.unsqueeze(2).to_broadcast([P, NT, WIN])).then_inc(S.sw_p, 1)
                for e in range(QPB):
                    n = 2 * u + e
                    dve.wait_ge(S.sw_tr, n + 1)
                    if due(n - 1):
                        dve.wait_ge(S.sw_o, n - 1)
                    cp(ws[:, PT_PREV[e], P:], bank[:, D[1] + 2 * e, P:]).then_inc(S.sw_ptp, 1)
                    if e == 0 and u + 1 < SW_HEADS // QPB:
                        sw_normed(u + 1)
                sw_raw(u + 2)
                dve.wait_ge(S.sw_o_hi, u + 1)
                sub(act_lo[:, u, :], psum(D[5]), hi(u)).then_inc(S.sw_o_lo, 1)

            mem_attention(1)
            residual("out1", lambda k: col_k("ffn1", k), 2, False)
            ffn(1)

def kernel(x, mem, a_norm, a_w_in, a_conv, a_A_log, a_dt_bias, a_out_norm, a_w_out, kv_norm, w_kv, k_norm, b_norm,
           b_w_in, b_q_norm, b_sinks, b_w_out, mem_norm, w_mem_kv, mem_q_norm, mem_k_norm, ffn_norm, w_gate_up, w_down):
    import concourse.bacc as bacc
    from concourse.bass_utils import run_bass_kernel_spmd

    f = np.asarray

    def tiles(m):
        m = f(m)
        k, n = m.shape
        return m.reshape(k // P, P, n // P, P).transpose(2, 1, 0, 3).reshape(n // P, P, k)

    w_in, b_in = f(a_w_in)[0], f(b_w_in)[0]
    heads = w_in[:, :4 * DN_W]
    qkvz = tiles(heads).reshape(4, DN_HEADS, P, D_MODEL).transpose(1, 0, 2, 3).reshape(4 * DN_HEADS, P, D_MODEL)
    ba = w_in[:, 4 * DN_W:4 * DN_W + 2 * DN_HEADS].reshape(KT, P, 16).transpose(1, 0, 2).reshape(P, KT * 16)
    mem_kv = [tiles(f(w_mem_kv)[i]).reshape(2, MEM_HEADS, P, D_MODEL)[::-1].transpose(1, 0, 2, 3).reshape(-1, P, D_MODEL)
              for i in range(2)]
    ups = [tiles(f(w_gate_up)[i]).reshape(2, 2, HALF, P, D_MODEL).transpose(1, 2, 0, 3, 4).reshape(-1, P, D_MODEL)
           for i in range(2)]
    stream = np.concatenate([mem_kv[0], mem_kv[1], qkvz, tiles(w_in[:, 4 * DN_W + 2 * DN_HEADS:]), ups[0],
                             tiles(w_kv), tiles(b_in), ups[1]])
    outs = np.stack([tiles(f(a_w_out)[0]), tiles(f(b_w_out)[0])])
    downs = np.concatenate([np.stack([tiles(m) for m in f(w_down)[i].reshape(2, HALF * P, D_MODEL)])
                            for i in range(2)])

    def per_tile(v):
        return f(v).reshape(-1, P).T

    def everywhere(v):
        return np.broadcast_to(f(v).reshape(1, -1), (P, f(v).size))

    conv = f(a_conv)[0].reshape(4, 3, DN_HEADS, P).transpose(3, 2, 1, 0).reshape(P, -1)
    slopes = -np.exp2(-8.0 * np.arange(1, SW_HEADS + 1) / SW_HEADS).astype(np.float32)
    cols = np.concatenate(
        [per_tile(f(a_norm)[0]), per_tile(f(ffn_norm)[0]), per_tile(kv_norm), per_tile(f(b_norm)[0]),
         per_tile(f(ffn_norm)[1]), per_tile(f(mem_norm)[0]), per_tile(f(mem_norm)[1]), per_tile(f(a_out_norm)[0]),
         per_tile(f(mem_q_norm)[0]), per_tile(f(mem_q_norm)[1]), per_tile(f(mem_k_norm)[0]),
         per_tile(f(mem_k_norm)[1]), per_tile(np.concatenate([f(k_norm)] * 2)),
         per_tile(np.concatenate([f(b_q_norm)[0]] * 2)), conv, everywhere(a_A_log), everywhere(a_dt_bias),
         everywhere(b_sinks), everywhere(slopes),
         everywhere(np.array([EPS, -0.5 * math.log(P), -0.5 * math.log(SW_DIM)], np.float32))], axis=1)
    arrays = {
        "x_in": f(x)[0], "mem_in": f(mem)[0], "w_stream": stream, "w_out": outs, "w_down": downs, "w_ba": ba,
        "cols_in": cols, "squares_in": squares(), "dist_in": distances(),
    }
    arrays = {n: np.ascontiguousarray(a_) for n, a_ in arrays.items()}
    nc = bacc.Bacc("TRN2", target_bir_lowering=False, num_devices=1)
    args = [nc.dram_tensor(n, a_.shape, F32, kind="ExternalInput").ap() for n, a_ in arrays.items()]
    out = nc.dram_tensor("out", (SEQ, D_MODEL), F32, kind="ExternalOutput").ap()
    yoco_kernel(nc, *args, out)
    r = run_bass_kernel_spmd(nc, [arrays], core_ids=[0])
    return r.results[0]["out"].reshape(1, SEQ, D_MODEL)
```
